# Optimizing a Trainium2 kernel written in Bass

```python
import math
import jax
import jax.numpy as jnp
from jax import lax
import numpy as np

D_MODEL = 1024
BATCH = 1
SEQ = 256
DEPTH = 1

ATTN_HEADS = 8
HEAD_DIM = 64
ATTN_WIDTH = ATTN_HEADS * HEAD_DIM
IDX_HEADS = 8
IDX_DIM = 32
MAX_TOPK_KEYS = 256
Q_BLOCK = 64
SSD_HEADS = 8
SSD_HEAD_DIM = 64
SSD_WIDTH = SSD_HEADS * SSD_HEAD_DIM
SSD_GROUPS = 2
D_STATE = 128
CONV_WIDTH = 4
CHUNK = 128
MIX_WIDTH = ATTN_WIDTH + SSD_WIDTH
PEER_HEADS = 8
N_KEYS = 128
N_EXPERTS = N_KEYS * N_KEYS
PEER_QUERY_DIM = 256
PEER_HALF = PEER_QUERY_DIM // 2
PEER_SUB_TOPK = 16
PEER_TOPK = 16
TOK_BLOCK = 128
ROPE_THETA = 10000.0
LN_EPS = 1e-5
DEEPNORM_ALPHA = (2 * DEPTH) ** 0.25
DEEPNORM_BETA = (8 * DEPTH) ** -0.25

IN_SIZES = (ATTN_WIDTH, ATTN_WIDTH, ATTN_WIDTH, IDX_HEADS * IDX_DIM, IDX_DIM, IDX_HEADS,
            SSD_WIDTH, SSD_WIDTH + 2 * SSD_GROUPS * D_STATE, SSD_HEADS)
IN_WIDTH = sum(IN_SIZES)
SPLIT_POINTS = tuple(sum(IN_SIZES[:i + 1]) for i in range(len(IN_SIZES) - 1))
XBC_WIDTH = SSD_WIDTH + 2 * SSD_GROUPS * D_STATE

kernel_name = "hymba_dsa_ssd_peer_deepnorm"

def layer_norm(x, g, b):
    xf = x.astype(jnp.float32)
    mu = jnp.mean(xf, -1, keepdims=True)
    var = jnp.mean(jnp.square(xf - mu), -1, keepdims=True)
    y = (xf - mu) * lax.rsqrt(var + LN_EPS)
    return (y * g.astype(jnp.float32) + b.astype(jnp.float32)).astype(x.dtype)

def rope(x, positions):
    d = x.shape[-1]
    inv = ROPE_THETA ** (-jnp.arange(0, d, 2, dtype=jnp.float32) / d)
    ang = positions.astype(jnp.float32)[..., None] * inv
    ang = ang.reshape(ang.shape[:2] + (1,) * (x.ndim - 3) + ang.shape[-1:])
    cos = jnp.cos(ang).astype(x.dtype)
    sin = jnp.sin(ang).astype(x.dtype)
    x1, x2 = x[..., : d // 2], x[..., d // 2:]
    return jnp.concatenate([x1 * cos - x2 * sin, x2 * cos + x1 * sin], axis=-1)

def dsa_attention(q, k, v, iq, ik, iw, positions):
    bsz, seq, _ = q.shape
    q = rope(q.reshape(bsz, seq, ATTN_HEADS, HEAD_DIM), positions)
    k = rope(k.reshape(bsz, seq, ATTN_HEADS, HEAD_DIM), positions)
    v = v.reshape(bsz, seq, ATTN_HEADS, HEAD_DIM)
    iq = rope(iq.reshape(bsz, seq, IDX_HEADS, IDX_DIM), positions)
    ik = rope(ik, positions)
    iw = iw * (IDX_HEADS ** -0.5)
    topk = min(MAX_TOPK_KEYS, seq // 4)
    nb = seq // Q_BLOCK
    key_pos = jnp.arange(seq)

    def blockify(a):
        return a.reshape((bsz, nb, Q_BLOCK) + a.shape[2:]).swapaxes(0, 1)

    def one_block(args):
        qb, iqb, iwb, start = args
        t = start + jnp.arange(Q_BLOCK)
        rel = jax.nn.relu(jnp.einsum('bqhd,bsd->bqhs', iqb, ik) * (IDX_DIM ** -0.5))
        score = jnp.einsum('bqh,bqhs->bqs', iwb, rel).astype(jnp.float32)
        causal = key_pos[None, :] <= t[:, None]
        score = jnp.where(causal[None], score, -jnp.inf)
        _, idx = lax.top_k(score, topk)
        kg = jax.vmap(lambda kb, ib: kb[ib])(k, idx)
        vg = jax.vmap(lambda vb, ib: vb[ib])(v, idx)
        logits = jnp.einsum('bqhd,bqkhd->bqhk', qb, kg).astype(jnp.float32) * (HEAD_DIM ** -0.5)
        valid = idx <= t[None, :, None]
        logits = jnp.where(valid[:, :, None, :], logits, -jnp.inf)
        p = jax.nn.softmax(logits, axis=-1).astype(vg.dtype)
        return jnp.einsum('bqhk,bqkhd->bqhd', p, vg)

    starts = jnp.arange(nb, dtype=jnp.int32) * Q_BLOCK
    out = lax.map(one_block, (blockify(q), blockify(iq), blockify(iw), starts))
    return out.swapaxes(0, 1).reshape(bsz, seq, ATTN_WIDTH)

def segsum(a):
    t = a.shape[-1]
    ac = jnp.cumsum(a, axis=-1)
    seg = ac[..., :, None] - ac[..., None, :]
    mask = jnp.tril(jnp.ones((t, t), dtype=bool))
    return jnp.where(mask, seg, -jnp.inf)

def ssd_scan(xs, dt, a, bm, cm):
    bsz, seq, nh, hp = xs.shape
    nc = seq // CHUNK
    rep = nh // bm.shape[2]
    bm = jnp.repeat(bm, rep, axis=2)
    cm = jnp.repeat(cm, rep, axis=2)
    n = bm.shape[-1]
    xc = (xs * dt[..., None]).reshape(bsz, nc, CHUNK, nh, hp)
    bc = bm.reshape(bsz, nc, CHUNK, nh, n)
    cc = cm.reshape(bsz, nc, CHUNK, nh, n)
    ac = (dt * a).reshape(bsz, nc, CHUNK, nh).transpose(0, 3, 1, 2)
    a_cum = jnp.cumsum(ac, axis=-1)
    decay_in = jnp.exp(segsum(ac))
    cb = jnp.einsum('bclhn,bcshn->bhcls', cc, bc)
    y_diag = jnp.einsum('bhcls,bcshp->bclhp', cb * decay_in, xc)
    decay_to_end = jnp.exp(a_cum[..., -1:] - a_cum).transpose(0, 2, 3, 1)
    states = jnp.einsum('bclhn,bclhp->bchpn', bc, xc * decay_to_end[..., None])
    states = jnp.concatenate([jnp.zeros_like(states[:, :1]), states], axis=1)
    chunk_decay = jnp.exp(segsum(jnp.pad(a_cum[..., -1], ((0, 0), (0, 0), (1, 0)))))
    carried = jnp.einsum('bhzc,bchpn->bzhpn', chunk_decay, states)[:, :-1]
    y_off = jnp.einsum('bclhn,bchpn->bclhp', cc, carried) * jnp.exp(a_cum).transpose(0, 2, 3, 1)[..., None]
    return (y_diag + y_off).reshape(bsz, seq, nh, hp)

def ssd_mixer(z, xbc, dt, conv_w, conv_b, dt_bias, a_log, d_skip, norm_w):
    bsz, seq, _ = z.shape
    xbc = lax.conv_general_dilated(
        xbc, conv_w[:, None, :].astype(xbc.dtype), window_strides=(1,),
        padding=[(CONV_WIDTH - 1, 0)], dimension_numbers=('NWC', 'WIO', 'NWC'),
        feature_group_count=XBC_WIDTH) + conv_b.astype(xbc.dtype)
    xbc = jax.nn.silu(xbc).astype(jnp.float32)
    xs = xbc[..., :SSD_WIDTH].reshape(bsz, seq, SSD_HEADS, SSD_HEAD_DIM)
    bm = xbc[..., SSD_WIDTH:SSD_WIDTH + SSD_GROUPS * D_STATE].reshape(bsz, seq, SSD_GROUPS, D_STATE)
    cm = xbc[..., SSD_WIDTH + SSD_GROUPS * D_STATE:].reshape(bsz, seq, SSD_GROUPS, D_STATE)
    dt = jax.nn.softplus(dt.astype(jnp.float32) + dt_bias.astype(jnp.float32))
    a = -jnp.exp(a_log.astype(jnp.float32))
    y = ssd_scan(xs, dt, a, bm, cm) + xs * d_skip.astype(jnp.float32)[:, None]
    y = y.reshape(bsz, seq, SSD_WIDTH) * jax.nn.silu(z.astype(jnp.float32))
    yg = y.reshape(bsz, seq, SSD_GROUPS, SSD_WIDTH // SSD_GROUPS)
    yg = yg * lax.rsqrt(jnp.mean(jnp.square(yg), -1, keepdims=True) + LN_EPS)
    y = yg.reshape(bsz, seq, SSD_WIDTH) * norm_w.astype(jnp.float32)
    return y.astype(z.dtype)

def token_mix(x, positions, w_in, conv_w, conv_b, dt_bias, a_log, d_skip, norm_w, w_out):
    proj = x @ w_in
    q, k, v, iq, ik, iw, z, xbc, dt = jnp.split(proj, SPLIT_POINTS, axis=-1)
    attn = dsa_attention(q, k, v, iq, ik, iw, positions)
    ssd = ssd_mixer(z, xbc, dt, conv_w, conv_b, dt_bias, a_log, d_skip, norm_w)
    return jnp.concatenate([attn, ssd], axis=-1) @ w_out

def peer(h, wq, k1, k2, u, v):
    bsz, seq, dm = h.shape
    xt = h.reshape(-1, dm)
    ntok = xt.shape[0]
    q = (xt @ wq).reshape(ntok, PEER_HEADS, 2, PEER_HALF)
    s1 = jnp.einsum('nhd,kd->nhk', q[:, :, 0], k1).astype(jnp.float32)
    s2 = jnp.einsum('nhd,kd->nhk', q[:, :, 1], k2).astype(jnp.float32)
    v1, i1 = lax.top_k(s1, PEER_SUB_TOPK)
    v2, i2 = lax.top_k(s2, PEER_SUB_TOPK)
    cand = (v1[..., :, None] + v2[..., None, :]).reshape(ntok, PEER_HEADS, -1)
    cidx = (i1[..., :, None] * N_KEYS + i2[..., None, :]).reshape(ntok, PEER_HEADS, -1)
    best, pos = lax.top_k(cand, PEER_TOPK)
    eidx = jnp.take_along_axis(cidx, pos, axis=-1).reshape(ntok, PEER_HEADS * PEER_TOPK)
    gate = jax.nn.softmax(best, axis=-1).reshape(ntok, PEER_HEADS * PEER_TOPK).astype(h.dtype)
    nb = ntok // TOK_BLOCK

    def one_block(args):
        xb, ib, gb = args
        act = jax.nn.gelu(jnp.einsum('td,tkd->tk', xb, u[ib]), approximate=False) * gb
        return jnp.einsum('tk,tkd->td', act, v[ib])

    out = lax.map(one_block, (xt.reshape(nb, TOK_BLOCK, dm),
                              eidx.reshape(nb, TOK_BLOCK, -1),
                              gate.reshape(nb, TOK_BLOCK, -1)))
    return out.reshape(bsz, seq, dm)

def setup_inputs(seed: int = 0) -> dict:
    key = jax.random.key(seed)
    ks = jax.random.split(key, 20)
    f32 = jnp.float32
    x = jax.random.normal(ks[0], (BATCH, SEQ, D_MODEL), f32)
    positions = jnp.broadcast_to(jnp.arange(SEQ, dtype=jnp.int32), (BATCH, SEQ))
    col_scale = jnp.ones((IN_WIDTH,), f32).at[2 * ATTN_WIDTH:3 * ATTN_WIDTH].set(DEEPNORM_BETA)
    w_in = jax.random.normal(ks[1], (DEPTH, D_MODEL, IN_WIDTH), f32) * (D_MODEL ** -0.5) * col_scale
    conv_w = jax.random.normal(ks[2], (DEPTH, CONV_WIDTH, XBC_WIDTH), f32) * (CONV_WIDTH ** -0.5)
    conv_b = 0.02 * jax.random.normal(ks[3], (DEPTH, XBC_WIDTH), f32)
    dt0 = jnp.exp(jax.random.uniform(ks[4], (DEPTH, SSD_HEADS), f32, math.log(1e-3), math.log(1e-1)))
    dt_bias = dt0 + jnp.log(-jnp.expm1(-dt0))
    a_log = jnp.log(jax.random.uniform(ks[5], (DEPTH, SSD_HEADS), f32, 1.0, 16.0))
    d_skip = 1.0 + 0.1 * jax.random.normal(ks[6], (DEPTH, SSD_HEADS), f32)
    ssm_norm_w = 1.0 + 0.02 * jax.random.normal(ks[7], (DEPTH, SSD_WIDTH), f32)
    w_out = jax.random.normal(ks[8], (DEPTH, MIX_WIDTH, D_MODEL), f32) * (MIX_WIDTH ** -0.5) * DEEPNORM_BETA
    ln1_g = 1.0 + 0.02 * jax.random.normal(ks[9], (DEPTH, D_MODEL), f32)
    ln1_b = 0.02 * jax.random.normal(ks[10], (DEPTH, D_MODEL), f32)
    peer_wq = jax.random.normal(ks[11], (DEPTH, D_MODEL, PEER_HEADS * PEER_QUERY_DIM), f32) * (D_MODEL ** -0.5)
    peer_k1 = jax.random.normal(ks[12], (DEPTH, N_KEYS, PEER_HALF), f32) * (PEER_HALF ** -0.5)
    peer_k2 = jax.random.normal(ks[13], (DEPTH, N_KEYS, PEER_HALF), f32) * (PEER_HALF ** -0.5)
    peer_u = jax.random.normal(ks[14], (DEPTH, N_EXPERTS, D_MODEL), f32) * (D_MODEL ** -0.5)
    peer_v = jax.random.normal(ks[15], (DEPTH, N_EXPERTS, D_MODEL), f32) * DEEPNORM_BETA
    ln2_g = 1.0 + 0.02 * jax.random.normal(ks[16], (DEPTH, D_MODEL), f32)
    ln2_b = 0.02 * jax.random.normal(ks[17], (DEPTH, D_MODEL), f32)
    return {"x": x, "positions": positions, "w_in": w_in, "conv_w": conv_w, "conv_b": conv_b,
            "dt_bias": dt_bias, "a_log": a_log, "d_skip": d_skip, "ssm_norm_w": ssm_norm_w,
            "w_out": w_out, "ln1_g": ln1_g, "ln1_b": ln1_b, "peer_wq": peer_wq,
            "peer_k1": peer_k1, "peer_k2": peer_k2, "peer_u": peer_u, "peer_v": peer_v,
            "ln2_g": ln2_g, "ln2_b": ln2_b}

def reference(x, positions, w_in, conv_w, conv_b, dt_bias, a_log, d_skip, ssm_norm_w,
              w_out, ln1_g, ln1_b, peer_wq, peer_k1, peer_k2, peer_u, peer_v, ln2_g, ln2_b):
    for i in range(DEPTH):
        mix = token_mix(x, positions, w_in[i], conv_w[i], conv_b[i], dt_bias[i], a_log[i],
                        d_skip[i], ssm_norm_w[i], w_out[i])
        x = layer_norm(DEEPNORM_ALPHA * x + mix, ln1_g[i], ln1_b[i])
        ffn = peer(x, peer_wq[i], peer_k1[i], peer_k2[i], peer_u[i], peer_v[i])
        x = layer_norm(DEEPNORM_ALPHA * x + ffn, ln2_g[i], ln2_b[i])
    return x


_drawn_inputs = setup_inputs


def setup_inputs(seed=0):
    import zlib

    import numpy as np

    out = dict(_drawn_inputs(seed))
    spreads = {}
    factors = {}
    for name, (base, spread) in spreads.items():
        noise = np.random.default_rng([zlib.crc32(name.encode()), seed]).standard_normal(out[name].shape)
        drawn = base * np.exp(spread * noise) if base else spread * noise
        out[name] = jnp.asarray(drawn.astype(out[name].dtype))
    for name, factor in factors.items():
        out[name] = (out[name] * factor).astype(out[name].dtype)
    return out
```

```python
from contextlib import ExitStack

import concourse.bass as bass
import numpy as np
from concourse import mybir

P = 128
D_MODEL, SEQ = 1024, 256
TILES = SEQ // P
KT = D_MODEL // P
HEADS, HEAD_DIM = 8, 64
ATTN_WIDTH = HEADS * HEAD_DIM
IDX_HEADS, IDX_DIM = 8, 32
TOPK_KEYS = min(256, SEQ // 4)
SSD_HEADS, SSD_WIDTH, GROUPS, CONV_WIDTH = 8, 512, 2, 4
GROUP_HEADS = SSD_HEADS // GROUPS
IDX_COLS = IDX_HEADS * IDX_DIM + IDX_DIM + IDX_HEADS
XBC_WIDTH = SSD_WIDTH + 2 * GROUPS * P
CT = XBC_WIDTH // P
Q0, K0, V0, I0 = 0, ATTN_WIDTH, 2 * ATTN_WIDTH, 3 * ATTN_WIDTH
Z0 = I0 + IDX_COLS
X0 = Z0 + SSD_WIDTH
DT0 = X0 + XBC_WIDTH
PEER_HEADS, N_KEYS, PEER_TOPK = 8, 128, 16
SIDES = 2 * PEER_HEADS
UNITS = TILES * PEER_HEADS
SLOTS = PEER_TOPK
ROPE_THETA, LN_EPS = 10000.0, 1e-5
ALPHA = 2.0 ** 0.25
TWO_PI = 2.0 * np.pi
TWO_PI_HI = 6.28125
TWO_PI_MID = float(np.float32(np.round((TWO_PI - TWO_PI_HI) * 2.0 ** 20) / 2.0 ** 20))
TWO_PI_LO = float(np.float32(TWO_PI - TWO_PI_HI - TWO_PI_MID))
ROUND_MAGIC = 1.5 * 2.0 ** 23
SIN_LIMIT = 3.1415925
NON_CAUSAL, TAKEN, TAKEN_BELOW, NOT_SELECTED = -3.0e38, -3.4e38, -3.2e38, -1.0e30
HALF_FREQS = HEAD_DIM // 2 + IDX_DIM // 2

PSUM_BANKS = 8


def psum_jobs():
    jobs = [("xT", t, half) for t in range(TILES) for half in range(2)]
    jobs += [("consts",)]
    jobs += [("proj_idx", t) for t in range(TILES)] + [("proj_q", t) for t in range(TILES)]
    jobs += [("T_idx", t) for t in range(TILES)]
    jobs += [("proj_k", 0), ("T_qk", 0, 0), ("proj_k", 1), ("T_qk", 1, 0)]
    jobs += [("idx_dot", t, g) for t in range(TILES) for g in range(4)]
    jobs += [("proj_z", t) for t in range(TILES)] + [("T_qk", s, 1) for s in range(2)]
    jobs += [("proj_xbc", n) for n in range(CT // 2)]
    jobs += [("proj_v", t) for t in range(TILES)]
    sums = [[("cum_col", t), ("cum_row", t, 0), ("cum_row", t, 1)] for t in range(TILES)]
    jobs += sums[0]
    jobs += [("logits", 0, n) for n in range(4)]
    jobs += [("cb", 0), ("T_xs", 0), ("T_b",)]
    jobs += [("T_p", 0, n) for n in range(2)] + [("pv", 0), ("y_diag", 0), ("state",)] + sums[1]
    jobs += [("logits", 1, n) for n in range(4)]
    jobs += [("cb", 1), ("T_xs", 1), ("T_attn", 0), ("T_y", 0), ("out", 0, 0), ("out", 0, 1)]
    jobs += [("T_p", 1, n) for n in range(4)] + [("pv", 1), ("y_off",), ("y_diag", 1)]
    jobs += [("T_attn", 1), ("T_y", 1), ("out", 1, 0), ("out", 1, 1)]
    for t in range(TILES):
        jobs += [("T_h", t, half) for half in range(2)]
        jobs += [("peer_q", t, c) for c in range(4)] + [("key_scores", t, c) for c in range(4)]
    return jobs


def build_layer(nc, x, positions, inv_freq, w_in, conv_w, conv_b, dt_bias, a_log, d_skip, ssm_norm_w,
                w_out, ln1_g, ln1_b, peer_wq, peer_k1, peer_k2, expert_uv, ln2_g, ln2_b, out):
    f32, i32, u32 = mybir.dt.float32, mybir.dt.int32, mybir.dt.uint32
    ALU, ACT, AX = mybir.AluOpType, mybir.ActivationFunctionType, mybir.AxisListType

    jobs = {name: n for n, name in enumerate(psum_jobs())}
    ctx = ExitStack()
    with ctx:
        def sb(name, words, dtype=f32):
            return ctx.enter_context(nc.sbuf_tensor(name, [P, words], dtype))

        def sem(name):
            return ctx.enter_context(nc.semaphore(name))

        CHUNK, SLOT = KT * 512, 2 * D_MODEL
        arena = sb("arena", SLOTS * SLOT)
        SCRATCH = 2 * CHUNK

        def view(tensor, at, *dims):
            size = int(np.prod(dims))
            flat = tensor[:, at:at + size]
            if len(dims) == 2:
                return flat.rearrange("p (a b) -> p a b", a=dims[0])
            if len(dims) == 3:
                return flat.rearrange("p (a b c) -> p a b c", a=dims[0], b=dims[1])
            return flat

        def chunk(position, columns=512):
            return view(arena, position * CHUNK, KT, columns)

        logits = view(arena, SCRATCH, HEADS, SEQ)
        rel = logits
        RAW_LEN = SEQ + CONV_WIDTH - 1
        xbc_raw = view(arena, SCRATCH + 2048, CT, RAW_LEN)
        probs_t = view(arena, SCRATCH + 2048, TILES, HEADS, P)
        rope_a = view(arena, SCRATCH + 2048, 512)
        rope_b = view(arena, SCRATCH + 2560, 512)
        at = SCRATCH + 2048 + CT * RAW_LEN
        decay = view(arena, at, SSD_HEADS, P)
        turns = view(arena, at, 2 * TILES * HALF_FREQS)
        keys_nat = view(arena, at + 256, 2, P)
        conv_nat = view(arena, at + 512, P)
        idx_nat = view(arena, at + 640, 3 * P)
        xs_nat = view(arena, at + 1024, SSD_HEADS, 64)
        xdt = view(arena, at + 1536, SSD_HEADS, 64)
        xdt_end = view(arena, at + 2048, SSD_HEADS, 64)
        state_t = view(arena, at + 2560, SSD_WIDTH)
        y_ssd = view(arena, at + 3072, SSD_HEADS, 64)
        b_nat = view(arena, at + 3584, GROUPS, P)
        assert at + 3584 + GROUPS * P <= SCRATCH + 2 * CHUNK

        x_sb = ctx.enter_context(nc.sbuf_tensor("x_sb", [P, TILES, D_MODEL], f32))
        x_t = ctx.enter_context(nc.sbuf_tensor("x_t", [P, KT, SEQ], f32))
        h_t = x_t
        mix = sb("mix", KT * SEQ)
        mix_t = view(mix, 0, KT, SEQ)
        peer_q_t = view(mix, 0, SIDES, P)
        ffn = view(mix, 0, TILES, D_MODEL)
        big = sb("big", 4096)
        q_t, k_t, xbc = view(big, 0, 4, SEQ), view(big, 1024, 4, SEQ), view(big, 2048, CT, SEQ)
        key_scores = view(big, 0, UNITS, 2, N_KEYS)
        iq_t = ctx.enter_context(nc.sbuf_tensor("iq_t", [P, 2, SEQ], f32))
        ik_t = sb("ik_t", SEQ)
        mid = sb("mid", 3584)
        v_sb, z_silu = view(mid, 0, TILES, 512), view(mid, 1024, TILES, 512)
        qk_nat, attn = view(mid, 2048, 2, 512), view(mid, 3072, HEADS, HEAD_DIM)
        diag = view(mid, 1024, 8, P)
        cand, cand_rest = view(mid, 2048, 16, 16), view(mid, 2304, 256)
        side_scores, side_rest = view(mid, 2560, 2, N_KEYS), view(mid, 2816, 2, N_KEYS)
        one_hot = view(mid, 3072, 2, 16, 16)
        ln_gb = ctx.enter_context(nc.sbuf_tensor("ln_gb", [P, 2, D_MODEL], f32))
        ident, upper = sb("ident", P), sb("upper", P)
        keys_t = ctx.enter_context(nc.sbuf_tensor("keys_t", [P, 2, P], f32))
        conv_t = sb("conv_t", (CONV_WIDTH + 1) * CT)
        cb_masked = ctx.enter_context(nc.sbuf_tensor("cb_masked", [P, GROUPS, P], f32))
        score, score_rest = sb("score", SEQ), sb("score_rest", SEQ)
        causal = sb("causal", SEQ)
        select_bias = ctx.enter_context(nc.sbuf_tensor("select_bias", [P, TILES, SEQ], f32))
        norm_w = sb("norm_w", SSD_WIDTH)
        sin_cos = sb("sin_cos", 2 * TILES * HALF_FREQS)
        sin_cos4 = sin_cos[:, :].rearrange("p (s t f) -> p s t f", s=2, t=TILES)
        freqs, pos_i, pos_f = sb("freqs", HALF_FREQS), sb("pos_i", TILES, i32), sb("pos_f", TILES)
        iw = sb("iw", TILES * IDX_HEADS)
        heads_in = sb("heads_in", 3 * SSD_HEADS)
        dt_x, dt_e = sb("dt_x", TILES * SSD_HEADS), sb("dt_e", TILES * SSD_HEADS)
        dt_w, dt_w2, dt_p = (sb(n, TILES * SSD_HEADS) for n in ("dt_w", "dt_w2", "dt_p"))
        dt, dta, cum = (sb(n, TILES * SSD_HEADS) for n in ("dt", "dta", "cum"))
        neg_a, to_end, exp_cum = sb("neg_a", SSD_HEADS), sb("to_end", SSD_HEADS), sb("exp_cum", SSD_HEADS)
        top8 = sb("top8", 8)
        row_max, row_sum, row_inv = sb("row_max", HEADS), sb("row_sum", HEADS), sb("row_inv", HEADS)
        squares, rms = sb("squares", GROUPS), sb("rms", GROUPS)
        stats, moments, rstd = sb("stats", 12), sb("moments", 2), sb("rstd", 1)
        top_v = ctx.enter_context(nc.sbuf_tensor("top_v", [P, 2, 16], f32))
        top_i = ctx.enter_context(nc.sbuf_tensor("top_i", [P, 2, 16], u32))
        top_if = ctx.enter_context(nc.sbuf_tensor("top_if", [P, 2, 16], f32))
        best, neg_best = sb("best", 16), sb("neg_best", 1)
        best_pos = sb("best_pos", 16, u32)
        pos_ij = ctx.enter_context(nc.sbuf_tensor("pos_ij", [P, 2, 16], u32))
        pos_ijf = ctx.enter_context(nc.sbuf_tensor("pos_ijf", [P, 2, 16], f32))
        picked = ctx.enter_context(nc.sbuf_tensor("picked", [P, 2, 16], f32))
        iota16 = sb("iota16", 16)
        expert = ctx.enter_context(nc.sbuf_tensor("expert", [P, 2, 16], i32))
        gate_e, gate_sum = sb("gate_e", 16), sb("gate_sum", 1)
        gate = ctx.enter_context(nc.sbuf_tensor("gate", [P, 2, 16], f32))
        dots = ctx.enter_context(nc.sbuf_tensor("dots", [P, 2, 16], f32))
        gelu = ctx.enter_context(nc.sbuf_tensor("gelu", [P, 2, 16], f32))
        weight = ctx.enter_context(nc.sbuf_tensor("weight", [P, 2, 16], f32))

        banks = [ctx.enter_context(nc.psum_tensor(f"bank{n}", [P, 512], f32)) for n in range(PSUM_BANKS)]

        bank_full = [sem(f"bank_full{n}") for n in range(PSUM_BANKS)]
        bank_free = [sem(f"bank_free{n}") for n in range(PSUM_BANKS)]
        x_in = [sem(f"x_in{t}") for t in range(TILES)]
        w_names = ["idx", "q", "k", "z", "xbc0", "xbc1", "v", "out0", "out1", "wq0", "wq1", "wq2", "wq3"]
        w_in_sem = {n: sem(f"w_{n}_in") for n in w_names}
        small_in, keys_in, ln1_in, ln2_in = sem("small_in"), sem("keys_in"), sem("ln1_in"), sem("ln2_in")
        consts_ready, ident_step = sem("consts_ready"), sem("ident_step")
        vec_step, act_step, searches = sem("vec_step"), sem("act_step"), sem("searches")
        turns_ready, rope_ready = sem("turns_ready"), sem("rope_ready")
        x_t_vec = sem("x_t_vec")
        dt_arg_ready, dt_exp_ready, dta_ready = sem("dt_arg_ready"), sem("dt_exp_ready"), sem("dta_ready")
        idx_nat_ready, qk_nat_ready = sem("idx_nat_ready"), sem("qk_nat_ready")
        scratch_roped = sem("scratch_roped")
        idx_t_ready, qk_t_ready, rel_ready, rel_used = (sem(n) for n in ("idx_t_ready", "qk_t_ready", "rel_ready", "rel_used"))
        z_ready, raw_ready, conv_ready, silu_ready, v_ready = (sem(n) for n in ("z_ready", "raw_ready", "conv_ready", "silu_ready", "v_ready"))
        consts_t_ready = sem("consts_t_ready")
        decay_arg_ready, decay_ready, decay_masked = (sem(n) for n in ("decay_arg_ready", "decay_ready", "decay_masked"))
        logits_ready, probs_ready, probs_t_act, probs_t_vec = (sem(n) for n in ("logits_ready", "probs_ready", "probs_t_act", "probs_t_vec"))
        xs_ready, b_nat_ready, xdt_ready, state_ready = (sem(n) for n in ("xs_ready", "b_nat_ready", "xdt_ready", "state_ready"))
        attn_ready, attn_t_ready = sem("attn_ready"), sem("attn_t_ready")
        rms_arg_ready, rms_ready, y_ready, y_t_ready = (sem(n) for n in ("rms_arg_ready", "rms_ready", "y_ready", "y_t_ready"))
        var_ready, std_ready, h_ready, ln1_done = (sem(n) for n in ("var_ready", "std_ready", "h_ready", "ln1_done"))
        h_t_ready, peer_q_act, peer_q_vec, scores_ready = (sem(n) for n in ("h_t_ready", "peer_q_act", "peer_q_vec", "scores_ready"))
        experts_ready, best_ready, gate_exp_ready, gate_ready = (sem(n) for n in ("experts_ready", "best_ready", "gate_exp_ready", "gate_ready"))
        rows_in = [sem(f"rows_in{j}") for j in range(SLOTS)]
        rows_asked = sem("rows_asked")
        dots_ready, gelu_ready, weight_ready, diag_ready = (sem(n) for n in ("dots_ready", "gelu_ready", "weight_ready", "diag_ready"))
        slot_used, sum_taken = sem("slot_used"), sem("sum_taken")
        result_ready, out_stored = sem("result_ready"), sem("out_stored")

        def bank(job):
            return banks[jobs[job] % PSUM_BANKS]

        def use(job):
            return jobs[job] // PSUM_BANKS + 1

        def wait_bank(pe, job):
            if use(job) > 1:
                pe.wait_ge(bank_free[jobs[job] % PSUM_BANKS], use(job) - 1)

        def full(job):
            return bank_full[jobs[job] % PSUM_BANKS]

        def free(job):
            return bank_free[jobs[job] % PSUM_BANKS]

        def wait_job(engine, job):
            engine.wait_ge(full(job), use(job))

        def cast_rows(a):
            return a.partition_broadcast(P)

        places = {"idx": 0, "q": 1, "k": 4, "z": 5, "xbc0": 6, "xbc1": 7, "v": 4, "out0": 0, "out1": 1,
                  "wq0": 5, "wq1": 6, "wq2": 7, "wq3": 4}
        w_rows = w_in.rearrange("(k p) n -> p k n", p=P)
        w_out_rows = w_out.rearrange("(k p) n -> p k n", p=P)
        wq_rows = peer_wq.rearrange("(k p) n -> p k n", p=P)
        frees = {"v": ("proj_k", 1), "out0": ("proj_idx", 1), "out1": ("proj_q", 1), "wq0": ("proj_z", 1),
                 "wq1": ("proj_xbc", 1), "wq2": ("proj_xbc", 3), "wq3": ("proj_v", 1)}
        columns = {"q": Q0, "k": K0, "z": Z0, "xbc0": X0, "xbc1": X0 + 512, "v": V0}
        block = ctx.enter_context(nc.Block())

        def pairs_of(n):
            par, jj = n % 2, n // 2
            return par + 4 * jj, par + 4 * jj + 2

        def exp_gate(act, u):
            act.wait_ge(best_ready, u + 1)
            nc.scalar.activation(gate_e[:, :], best[:, :], ACT.Exp, bias=neg_best[:, :],
                                 accum_out=gate_sum[:, :]).then_inc(gate_exp_ready, 1)

        @block.sync
        def _(sp):
            for t in range(TILES):
                sp.dma_start(x_sb[:, t, :], x[t * P:(t + 1) * P, :]).then_inc(x_in[t], 16)
            for name in w_names:
                if name in frees:
                    wait_job(sp, frees[name])
                if name == "idx":
                    place = chunk(places[name], IDX_COLS + SSD_HEADS)
                    sp.dma_start(place[:, :, 0:IDX_COLS], w_rows[:, :, I0:I0 + IDX_COLS]).then_inc(w_in_sem[name], 16)
                    sp.dma_start(place[:, :, IDX_COLS:], w_rows[:, :, DT0:DT0 + SSD_HEADS]).then_inc(w_in_sem[name], 16)
                elif name in columns:
                    sp.dma_start(chunk(places[name]), w_rows[:, :, columns[name]:columns[name] + 512]).then_inc(w_in_sem[name], 16)
                else:
                    source = w_out_rows if name.startswith("out") else wq_rows
                    n = int(name[-1])
                    sp.dma_start(chunk(places[name]), source[:, :, n * 512:(n + 1) * 512]).then_inc(w_in_sem[name], 16)
            sp.wait_ge(ln1_done, 1)
            sp.dma_start(ln_gb[:, 0, :], cast_rows(ln2_g)).then_inc(ln2_in, 16)
            sp.dma_start(ln_gb[:, 1, :], cast_rows(ln2_b)).then_inc(ln2_in, 16)
            for t in range(TILES):
                sp.wait_ge(result_ready, t + 1)
                sp.dma_start(out[t * P:(t + 1) * P, :], x_sb[:, t, :]).then_inc(out_stored, 16)
            sp.wait_ge(out_stored, 16 * TILES)

        @block.gpsimd
        def _(pool):
            pool.memset(ident[:, :], 0.0).then_inc(ident_step, 1)
            pool.memset(upper[:, :], 1.0).then_inc(ident_step, 1)
            pool.memset(causal[:, :], 0.0).then_inc(ident_step, 1)
            pool.wait_ge(ident_step, 3)
            pool.affine_select(out=ident[:, :], in_=ident[:, :], compare_op=ALU.not_equal, fill=1.0, base=0,
                               pattern=[[-1, P]], channel_multiplier=1).then_inc(consts_ready, 1)
            pool.affine_select(out=upper[:, :], in_=upper[:, :], compare_op=ALU.is_ge, fill=0.0, base=0,
                               pattern=[[1, P]], channel_multiplier=-1).then_inc(consts_ready, 1)
            pool.affine_select(out=causal[:, P:SEQ], in_=causal[:, P:SEQ], compare_op=ALU.is_ge, fill=NON_CAUSAL, base=0,
                               pattern=[[-1, P]], channel_multiplier=1).then_inc(consts_ready, 1)
            pool.iota(iota16[:, :], pattern=[[1, 16]], base=0, channel_multiplier=0,
                      allow_small_or_imprecise_dtypes=True).then_inc(consts_ready, 1)

            def gather_unit(u, parity, first=False):
                pool.wait_ge(experts_ready, u + 1)
                for j in range(SLOTS):
                    if not first:
                        pool.wait_ge(slot_used, (u - 1) * SLOTS + j + 1)
                    if not first or j == 0:
                        pool.sem_inc(rows_asked, 1)
                    if first and j == SLOTS // 2:
                        wait_job(pool, ("peer_q", 1, 3))
                    pool.indirect_dma_start(
                        out=arena[:, j * SLOT:(j + 1) * SLOT], out_offset=None, in_=expert_uv,
                        in_offset=bass.IndirectOffsetOnAxis(ap=expert[:, parity, j:j + 1], axis=0),
                    ).then_inc(rows_in[j], 16)

            gather_unit(0, 0, first=True)
            with pool.Fori(0, UNITS // 2 - 1) as i:
                gather_unit(2 * i + 1, 1)
                gather_unit(2 * i + 2, 0)
            gather_unit(UNITS - 1, 1)

        @block.tensor
        def _(pe):
            mm = nc.tensor.matmul

            def transposes(job, sources):
                wait_bank(pe, job)
                for n, source in enumerate(sources):
                    last = nc.tensor.transpose(bank(job)[:, n * P:(n + 1) * P], source, ident[:, :])
                last.then_inc(full(job), 1)

            def project(job, name, t, columns=512, start=True):
                wait_bank(pe, job)
                for k in range(KT):
                    last = mm(bank(job)[:, 0:columns], lhsT=x_t[:, k, t * P:(t + 1) * P],
                              rhs=chunk(places[name], columns)[:, k, :], start=k == 0, stop=k == KT - 1)
                last.then_inc(full(job), 1)

            pe.wait_ge(consts_ready, 4)
            for t in range(TILES):
                pe.wait_ge(x_in[t], 16)
                for half in range(2):
                    transposes(("xT", t, half), [x_sb[:, t, k * P:(k + 1) * P] for k in range(4 * half, 4 * half + 4)])
            job = ("consts",)
            pe.wait_ge(keys_in, 4 * 16)
            wait_bank(pe, job)
            for s in range(2):
                nc.tensor.transpose(bank(job)[:, s * P:(s + 1) * P], keys_nat[:, s, :], ident[:, :])
            rows = (CONV_WIDTH + 1) * CT
            nc.tensor.transpose(bank(job)[:, 2 * P:2 * P + rows], conv_nat[0:rows, :], ident[0:rows, 0:rows]).then_inc(full(job), 1)

            pe.wait_ge(x_t_vec, 2)
            pe.wait_ge(act_step, 2)
            pe.wait_ge(w_in_sem["idx"], 32)
            for t in range(TILES):
                project(("proj_idx", t), "idx", t, IDX_COLS + SSD_HEADS)
            pe.wait_ge(w_in_sem["q"], 16)
            for t in range(TILES):
                project(("proj_q", t), "q", t)
            for t in range(TILES):
                pe.wait_ge(idx_nat_ready, t + 1)
                transposes(("T_idx", t), [idx_nat[:, n * P:(n + 1) * P] for n in range(3)])
            pe.wait_ge(w_in_sem["k"], 16)

            def transposed_qk(s, t):
                pe.wait_ge(qk_nat_ready, 2 * t + s + 1)
                transposes(("T_qk", s, t), [qk_nat[:, s, n * P:(n + 1) * P] for n in range(4)])

            for t in range(TILES):
                project(("proj_k", t), "k", t)
                transposed_qk(t, 0)
            for t in range(TILES):
                pe.wait_ge(idx_t_ready, t + 1)
                nk = (t + 1) * P
                for g in range(4):
                    job = ("idx_dot", t, g)
                    wait_bank(pe, job)
                    rows = slice(32 * g, 32 * g + 32)
                    for n in range(2):
                        last = mm(bank(job)[:, n * nk:(n + 1) * nk], lhsT=iq_t[rows, n, t * P:(t + 1) * P],
                                  rhs=ik_t[rows, 0:nk], start=True, stop=True)
                    last.then_inc(full(job), 1)
            pe.wait_ge(w_in_sem["z"], 16)
            for t in range(TILES):
                project(("proj_z", t), "z", t)
            for s in range(2):
                transposed_qk(s, 1)
            for n in range(CT // 2):
                job, name = ("proj_xbc", n), f"xbc{n // 2}"
                if n % 2 == 0:
                    pe.wait_ge(w_in_sem[name], 16)
                wait_bank(pe, job)
                for c in range(2):
                    col = (2 * (n % 2) + c) * P
                    for k in range(KT):
                        last = mm(bank(job)[:, c * SEQ:(c + 1) * SEQ], lhsT=chunk(places[name])[:, k, col:col + P],
                                  rhs=x_t[:, k, :], start=k == 0, stop=k == KT - 1)
                last.then_inc(full(job), 1)
            pe.wait_ge(w_in_sem["v"], 16)
            for t in range(TILES):
                project(("proj_v", t), "v", t)
            pe.wait_ge(dta_ready, 1)

            def running_sums(t):
                job = ("cum_col", t)
                wait_bank(pe, job)
                mm(bank(job)[:, 0:SSD_HEADS], lhsT=upper[:, :], rhs=dta[:, t * SSD_HEADS:(t + 1) * SSD_HEADS],
                   start=True, stop=True).then_inc(full(job), 1)
                for half in range(2):
                    job = ("cum_row", t, half)
                    wait_bank(pe, job)
                    for n in range(4):
                        col = t * SSD_HEADS + 4 * half + n
                        last = mm(bank(job)[:, n * P:(n + 1) * P], lhsT=dta[:, col:col + 1].broadcast_to([P, P]),
                                  rhs=upper[:, :], start=True, stop=True)
                    last.then_inc(full(job), 1)

            def logits_of(t):
                pe.wait_ge(qk_t_ready, 2 * (t + 1))
                nk = (t + 1) * P
                for n in range(4):
                    job = ("logits", t, n)
                    wait_bank(pe, job)
                    for m, h in enumerate(pairs_of(n)):
                        rows = slice(64 * (h % 2), 64 * (h % 2) + 64)
                        last = mm(bank(job)[:, m * nk:(m + 1) * nk], lhsT=q_t[rows, h // 2, t * P:(t + 1) * P],
                                  rhs=k_t[rows, h // 2, 0:nk], start=True, stop=True)
                    last.then_inc(full(job), 1)

            def cb_and_xs(t):
                now = slice(t * P, (t + 1) * P)
                job = ("cb", t)
                wait_bank(pe, job)
                for g in range(GROUPS):
                    last = mm(bank(job)[:, g * P:(g + 1) * P], lhsT=xbc[:, 4 + g, now], rhs=xbc[:, 6 + g, now],
                              start=True, stop=True)
                last.then_inc(full(job), 1)
                transposes(("T_xs", t), [xbc[:, c, now] for c in range(4)])

            def transposed_probs(t):
                pe.wait_ge(probs_ready, t + 1)
                for n in range(2 * (t + 1)):
                    kb, half = n // 2, n % 2
                    transposes(("T_p", t, n), [logits[:, 4 * half + h, kb * P:(kb + 1) * P] for h in range(4)])

            def attend(t):
                job = ("pv", t)
                pe.wait_ge(probs_t_act, t * (t + 1) // 2 + t + 1)
                pe.wait_ge(probs_t_vec, t * (t + 1) // 2 + t + 1)
                pe.wait_ge(v_ready, TILES)
                wait_bank(pe, job)
                for h in range(HEADS):
                    for kb in range(t + 1):
                        last = mm(bank(job)[:, h * HEAD_DIM:(h + 1) * HEAD_DIM], lhsT=probs_t[:, kb, h, :],
                                  rhs=v_sb[:, kb, h * HEAD_DIM:(h + 1) * HEAD_DIM], start=kb == 0, stop=kb == t)
                last.then_inc(full(job), 1)

            def y_diagonal(t):
                job = ("y_diag", t)
                pe.wait_ge(decay_masked, t + 1)
                pe.wait_ge(xdt_ready, t + 1)
                wait_bank(pe, job)
                for h in range(SSD_HEADS):
                    last = mm(bank(job)[:, h * 64:(h + 1) * 64], lhsT=decay[:, h, :], rhs=xdt[:, h, :],
                              start=True, stop=True)
                last.then_inc(full(job), 1)

            def mixed(t):
                pe.wait_ge(attn_ready, t + 1)
                transposes(("T_attn", t), [attn[:, 2 * n:2 * n + 2, :].rearrange("p a b -> p (a b)") for n in range(4)])
                pe.wait_ge(y_ready, t + 1)
                transposes(("T_y", t), [y_ssd[:, 2 * n:2 * n + 2, :].rearrange("p a b -> p (a b)") for n in range(4)])
                pe.wait_ge(attn_t_ready, t + 1)
                pe.wait_ge(y_t_ready, t + 1)
                for half in range(2):
                    job = ("out", t, half)
                    pe.wait_ge(w_in_sem[f"out{half}"], 16)
                    wait_bank(pe, job)
                    for k in range(KT):
                        last = mm(bank(job)[:, :], lhsT=mix_t[:, k, t * P:(t + 1) * P],
                                  rhs=chunk(places[f"out{half}"])[:, k, :], start=k == 0, stop=k == KT - 1)
                    last.then_inc(full(job), 1)

            running_sums(0)
            logits_of(0)
            pe.wait_ge(silu_ready, CT)
            cb_and_xs(0)
            transposes(("T_b",), [xbc[:, 4 + g, 0:P] for g in range(GROUPS)])
            transposed_probs(0)
            attend(0)
            y_diagonal(0)
            job = ("state",)
            pe.wait_ge(b_nat_ready, 1)
            wait_bank(pe, job)
            for g in range(GROUPS):
                heads = slice(g * GROUP_HEADS, (g + 1) * GROUP_HEADS)
                last = mm(bank(job)[:, g * 256:(g + 1) * 256], lhsT=b_nat[:, g, :],
                          rhs=xdt_end[:, heads, :].rearrange("p a b -> p (a b)"), start=True, stop=True)
            last.then_inc(full(job), 1)
            running_sums(1)
            logits_of(1)
            cb_and_xs(1)
            mixed(0)
            transposed_probs(1)
            attend(1)
            job = ("y_off",)
            pe.wait_ge(state_ready, 1)
            wait_bank(pe, job)
            for g in range(GROUPS):
                last = mm(bank(job)[:, g * 256:(g + 1) * 256], lhsT=xbc[:, 6 + g, P:SEQ],
                          rhs=state_t[:, g * 256:(g + 1) * 256], start=True, stop=True)
            last.then_inc(full(job), 1)
            y_diagonal(1)
            mixed(1)

            pe.wait_ge(consts_t_ready, 1)
            for t in range(TILES):
                pe.wait_ge(h_ready, t + 1)
                for half in range(2):
                    transposes(("T_h", t, half), [x_sb[:, t, k * P:(k + 1) * P] for k in range(4 * half, 4 * half + 4)])
                pe.wait_ge(h_t_ready, 2 * (t + 1))
                for c in range(4):
                    job = ("peer_q", t, c)
                    pe.wait_ge(w_in_sem[f"wq{c}"], 16)
                    wait_bank(pe, job)
                    for n in range(4):
                        for k in range(KT):
                            last = mm(bank(job)[:, n * P:(n + 1) * P], lhsT=chunk(places[f"wq{c}"])[:, k, n * P:(n + 1) * P],
                                      rhs=h_t[:, k, t * P:(t + 1) * P], start=k == 0, stop=k == KT - 1)
                    last.then_inc(full(job), 1)
                for c in range(4):
                    job = ("key_scores", t, c)
                    pe.wait_ge(peer_q_act, 2 * t + c // 2 + 1)
                    if c % 2:
                        pe.wait_ge(peer_q_vec, 2 * t + c // 2 + 1)
                    wait_bank(pe, job)
                    for n in range(4):
                        last = mm(bank(job)[:, n * P:(n + 1) * P], lhsT=peer_q_t[:, 4 * c + n, :],
                                  rhs=keys_t[:, n % 2, :], start=True, stop=True)
                    last.then_inc(full(job), 1)

            for n in range(4):
                pe.wait_ge(bank_free[n], len([j for j in jobs.values() if j % PSUM_BANKS == n]))

            def sum_unit(u, parity, first=False):
                if not first:
                    pe.wait_ge(sum_taken, u)
                for j in range(SLOTS):
                    pe.wait_ge(diag_ready, u * SLOTS + j + 1)
                    for half in range(2):
                        at = j * SLOT + D_MODEL + half * 512
                        last = mm(banks[2 * parity + half][:, :], lhsT=diag[:, j % 8, :], rhs=arena[:, at:at + 512],
                                  start=j == 0, stop=j == SLOTS - 1, skip_group_check=True)
                    last.then_inc(slot_used, 1)

            sum_unit(0, 0, first=True)
            with pe.Fori(0, UNITS // 2 - 1) as i:
                sum_unit(2 * i + 1, 1)
                sum_unit(2 * i + 2, 0)
            sum_unit(UNITS - 1, 1)

        @block.scalar
        def _(act):
            for t in range(TILES):
                act.dma_start(pos_i[:, t:t + 1], positions[t * P:(t + 1) * P].rearrange("(p a) -> p a", a=1)).then_inc(small_in, 16)
            act.dma_start(freqs[:, :], cast_rows(inv_freq)).then_inc(small_in, 16)
            for n, source in enumerate((dt_bias, a_log, d_skip)):
                act.dma_start(heads_in[:, n * SSD_HEADS:(n + 1) * SSD_HEADS], cast_rows(source)).then_inc(small_in, 16)
            act.dma_start(keys_nat[:, 0, :], peer_k1).then_inc(keys_in, 16)
            act.dma_start(keys_nat[:, 1, :], peer_k2).then_inc(keys_in, 16)
            act.dma_start(conv_nat[0:CONV_WIDTH * CT, :], conv_w.rearrange("k (c p) -> (k c) p", p=P)).then_inc(keys_in, 16)
            act.dma_start(conv_nat[CONV_WIDTH * CT:(CONV_WIDTH + 1) * CT, :], conv_b.rearrange("(c p) -> c p", p=P)).then_inc(keys_in, 16)
            act.dma_start(norm_w[:, :], cast_rows(ssm_norm_w)).then_inc(ln1_in, 16)
            act.dma_start(ln_gb[:, 0, :], cast_rows(ln1_g)).then_inc(ln1_in, 16)
            act.dma_start(ln_gb[:, 1, :], cast_rows(ln1_b)).then_inc(ln1_in, 16)
            run = nc.scalar.activation

            def bank_view(job, *dims):
                if len(dims) == 2:
                    return bank(job)[:, 0:dims[0] * dims[1]].rearrange("p (a b) -> p a b", a=dims[0])
                return bank(job)[:, 0:dims[0]]

            act.wait_ge(turns_ready, 1)
            run(sin_cos[:, :], turns, ACT.Sin).then_inc(rope_ready, 1)
            for t in range(TILES):
                job = ("xT", t, 1)
                wait_job(act, job)
                run(x_t[:, 4:8, t * P:(t + 1) * P], bank_view(job, 4, P), ACT.Copy).then_inc(free(job), 1)
            act.wait_ge(free(("xT", 0, 1)), use(("xT", 0, 1)))
            act.wait_ge(free(("xT", 1, 1)), use(("xT", 1, 1)))
            act.sem_inc(act_step, 2)
            act.wait_ge(dt_arg_ready, 1)
            run(neg_a[:, :], heads_in[:, SSD_HEADS:2 * SSD_HEADS], ACT.Exp)
            run(dt_e[:, :], dt_e[:, :], ACT.Exp).then_inc(dt_exp_ready, 1)
            for t in range(TILES):
                job, now = ("T_idx", t), slice(t * P, (t + 1) * P)
                wait_job(act, job)
                run(iq_t[:, :, now], bank_view(job, 2, P), ACT.Copy)
                run(ik_t[:, now], bank(job)[:, 2 * P:3 * P], ACT.Copy).then_inc(idx_t_ready, 1)
                act.wait_ge(idx_t_ready, t + 1)
                act.sem_inc(free(job), 1)

            def take_qk(t):
                for s in range(2):
                    job, now = ("T_qk", s, t), slice(t * P, (t + 1) * P)
                    wait_job(act, job)
                    run((q_t, k_t)[s][:, :, now], bank_view(job, 4, P), ACT.Copy).then_inc(free(job), 1)
                    act.wait_ge(free(job), use(job))
                    act.sem_inc(qk_t_ready, 1)

            take_qk(0)
            for t in range(TILES):
                nk = (t + 1) * P
                if t:
                    act.wait_ge(rel_used, t)
                for g in range(4):
                    job = ("idx_dot", t, g)
                    wait_job(act, job)
                    run(rel[:, g:8:4, 0:nk], bank_view(job, 2, nk), ACT.Relu, scale=IDX_DIM ** -0.5).then_inc(free(job), 1)
                    act.wait_ge(free(job), use(job))
                act.sem_inc(rel_ready, 1)
            for t in range(TILES):
                job = ("proj_z", t)
                wait_job(act, job)
                run(z_silu[:, t, :], bank(job)[:, :], ACT.Silu).then_inc(free(job), 1)
            take_qk(1)
            act.wait_ge(scratch_roped, 1)
            for n in range(CT // 2):
                job = ("proj_xbc", n)
                wait_job(act, job)
                run(xbc_raw[:, 2 * n:2 * n + 2, CONV_WIDTH - 1:], bank_view(job, 2, SEQ), ACT.Copy).then_inc(free(job), 1)
                act.wait_ge(free(job), use(job))
                act.sem_inc(raw_ready, 1)
                if n:
                    for c in (2 * n - 2, 2 * n - 1):
                        act.wait_ge(conv_ready, c + 1)
                        run(xbc[:, c, :], xbc[:, c, :], ACT.Silu).then_inc(silu_ready, 1)
            for c in (CT - 2, CT - 1):
                act.wait_ge(conv_ready, c + 1)
                run(xbc[:, c, :], xbc[:, c, :], ACT.Silu).then_inc(silu_ready, 1)
            for t in range(TILES):
                job = ("proj_v", t)
                wait_job(act, job)
                run(v_sb[:, t, :], bank(job)[:, :], ACT.Copy).then_inc(free(job), 1)
                act.wait_ge(free(job), use(job))
                act.sem_inc(v_ready, 1)

            def exp_decay(t):
                act.wait_ge(decay_arg_ready, t + 1)
                if t == 0:
                    run(to_end[:, :], to_end[:, :], ACT.Exp)
                else:
                    run(exp_cum[:, :], cum[:, SSD_HEADS:], ACT.Exp)
                run(decay, decay, ACT.Exp).then_inc(decay_ready, 1)

            def exp_logits(t):
                nk = (t + 1) * P
                act.wait_ge(logits_ready, t + 1)
                for h in range(HEADS):
                    last = run(logits[:, h, 0:nk], logits[:, h, 0:nk], ACT.Exp, bias=row_max[:, h:h + 1],
                               accum_out=row_sum[:, h:h + 1])
                last.then_inc(probs_ready, 1)

            def take_probs(t):
                if t:
                    wait_job(act, ("pv", t - 1))
                for n in range(0, 2 * (t + 1), 2):
                    job = ("T_p", t, n)
                    wait_job(act, job)
                    run(probs_t[:, n // 2, 0:4, :], bank_view(job, 4, P), ACT.Copy).then_inc(free(job), 1)
                    act.wait_ge(free(job), use(job))
                    act.sem_inc(probs_t_act, 1)

            def take_mixed(t):
                now = slice(t * P, (t + 1) * P)
                job = ("T_attn", t)
                wait_job(act, job)
                run(mix_t[:, 0:4, now], bank_view(job, 4, P), ACT.Copy).then_inc(free(job), 1)
                act.wait_ge(free(job), use(job))
                act.sem_inc(attn_t_ready, 1)
                job = ("T_y", t)
                wait_job(act, job)
                run(mix_t[:, 4:8, now], bank_view(job, 4, P), ACT.Copy).then_inc(free(job), 1)
                act.wait_ge(free(job), use(job))
                act.sem_inc(y_t_ready, 1)

            def root_of_squares(t):
                act.wait_ge(rms_arg_ready, t + 1)
                run(rms[:, :], rms[:, :], ACT.Sqrt).then_inc(rms_ready, 1)

            def root_of_variance(t):
                act.wait_ge(var_ready, t + 1)
                run(rstd[:, :], rstd[:, :], ACT.Sqrt).then_inc(std_ready, 1)

            exp_decay(0)
            exp_logits(0)
            job = ("T_b",)
            wait_job(act, job)
            run(b_nat, bank_view(job, GROUPS, P), ACT.Copy).then_inc(free(job), 1)
            act.wait_ge(free(job), use(job))
            act.sem_inc(b_nat_ready, 1)
            take_probs(0)
            job = ("state",)
            wait_job(act, job)
            run(state_t, bank(job)[:, :], ACT.Copy).then_inc(free(job), 1)
            act.wait_ge(free(job), use(job))
            act.sem_inc(state_ready, 1)
            root_of_squares(0)
            exp_decay(1)
            exp_logits(1)
            take_mixed(0)
            root_of_variance(0)
            take_probs(1)
            root_of_squares(1)
            take_mixed(1)
            root_of_variance(1)
            for t in range(TILES):
                now = slice(t * P, (t + 1) * P)
                for half in range(2):
                    job = ("T_h", t, half)
                    wait_job(act, job)
                    run(h_t[:, 4 * half:4 * half + 4, now], bank_view(job, 4, P), ACT.Copy).then_inc(free(job), 1)
                    act.wait_ge(free(job), use(job))
                    act.sem_inc(h_t_ready, 1)
                if t:
                    wait_job(act, ("key_scores", t - 1, 3))
                for c in (0, 2):
                    job = ("peer_q", t, c)
                    wait_job(act, job)
                    run(peer_q_t[:, 4 * c:4 * c + 4, :], bank_view(job, 4, P), ACT.Copy).then_inc(free(job), 1)
                    act.wait_ge(free(job), use(job))
                    act.sem_inc(peer_q_act, 1)
                for c in range(4):
                    job = ("key_scores", t, c)
                    wait_job(act, job)
                    at = (t * PEER_HEADS + 2 * c) * 2 * N_KEYS
                    run(big[:, at:at + 512], bank(job)[:, :], ACT.Copy).then_inc(free(job), 1)
                    act.wait_ge(free(job), use(job))
                    act.sem_inc(scores_ready, 1)
                if t == 0:
                    exp_gate(act, 0)

            def weigh_unit(u, parity, first=False, last=False):
                if not last:
                    exp_gate(act, u + 1)
                for g in range(4):
                    part = slice(4 * g, 4 * g + 4)
                    act.wait_ge(dots_ready, 4 * u + g + 1)
                    run(gelu[:, parity, part], dots[:, parity, part], ACT.Gelu).then_inc(gelu_ready, 1)
                    if g == 0:
                        act.wait_ge(gate_ready, u + 1)
                    act.wait_ge(gelu_ready, 4 * u + g + 1)
                    for j in range(4 * g, 4 * g + 4):
                        done = run(weight[:, parity, j:j + 1], gelu[:, parity, j:j + 1], ACT.Copy, scale=gate[:, parity, j:j + 1])
                    done.then_inc(weight_ready, 1)
                    act.wait_ge(weight_ready, 4 * u + g + 1)
                    for j in range(4 * g, 4 * g + 4):
                        if not first or j >= 8:
                            act.wait_ge(slot_used, u * SLOTS + j - 7)
                        run(diag[:, j % 8, :], ident[:, :], ACT.Copy, scale=weight[:, parity, j:j + 1]).then_inc(diag_ready, 1)

            weigh_unit(0, 0, first=True)
            with act.Fori(0, UNITS // 2 - 1) as i:
                weigh_unit(2 * i + 1, 1)
                weigh_unit(2 * i + 2, 0)
            weigh_unit(UNITS - 1, 1, last=True)
            for t in range(TILES):
                root_of_variance(TILES + t)

        @block.vector
        def _(dve):
            count = [0, 0]

            def link(ins):
                count[0] += 1
                ins.then_inc(vec_step, 1)
                dve.wait_ge(vec_step, count[1] + count[0])

            def link_to_search(ins):
                link(ins)
                dve.sem_inc(searches, 1)

            tt, ts, stt = nc.vector.tensor_tensor, nc.vector.tensor_scalar, nc.vector.scalar_tensor_tensor
            copy = nc.vector.tensor_copy

            def bank_view(job, *dims):
                n = int(np.prod(dims))
                flat = bank(job)[:, 0:n]
                if len(dims) == 2:
                    return flat.rearrange("p (a b) -> p a b", a=dims[0])
                if len(dims) == 3:
                    return flat.rearrange("p (a b c) -> p a b c", a=dims[0], b=dims[1])
                return flat

            dve.wait_ge(small_in, 6 * 16)
            link(copy(pos_f[:, :], pos_i[:, :]))
            half = TILES * HALF_FREQS
            for t in range(TILES):
                for s in range(2):
                    done = ts(sin_cos4[:, s, t, :], freqs[:, :], pos_f[:, t:t + 1], None, ALU.mult)
            link(done)
            for s in range(2):
                done = ts(turns[:, s * half:(s + 1) * half], sin_cos[:, s * half:(s + 1) * half], 1.0 / TWO_PI, 0.25 * s, ALU.mult, ALU.add)
            link(done)
            link(ts(turns, turns, ROUND_MAGIC, None, ALU.add))
            link(ts(turns, turns, ROUND_MAGIC, None, ALU.subtract))
            for part in (TWO_PI_HI, TWO_PI_MID, TWO_PI_LO):
                link(stt(sin_cos[:, :], turns, -part, sin_cos[:, :], ALU.mult, ALU.add))
            link(ts(sin_cos[:, half:], sin_cos[:, half:], float(np.pi / 2), None, ALU.add))
            ts(turns, sin_cos[:, :], SIN_LIMIT, -SIN_LIMIT, ALU.min, ALU.max).then_inc(turns_ready, 1)
            for t in range(TILES):
                job = ("xT", t, 0)
                wait_job(dve, job)
                link(copy(x_t[:, 0:4, t * P:(t + 1) * P], bank_view(job, 4, P)))
                dve.sem_inc(free(job), 1)
                dve.sem_inc(x_t_vec, 1)
            job = ("consts",)
            wait_job(dve, job)
            copy(keys_t[:, :, :], bank_view(job, 2, P))
            copy(conv_t[:, :], bank(job)[:, 2 * P:2 * P + (CONV_WIDTH + 1) * CT]).then_inc(consts_t_ready, 1)
            dve.wait_ge(consts_t_ready, 1)
            dve.sem_inc(free(job), 1)
            dve.wait_ge(rope_ready, 1)

            def rope(source, dest, heads, dim, t):
                first, n = (0, HEAD_DIM // 2) if dim == HEAD_DIM else (HEAD_DIM // 2, IDX_DIM // 2)
                sin, cos = (sin_cos4[:, s, t, first:first + n].unsqueeze(1).broadcast_to([P, 2 * heads, n]) for s in range(2))
                src = source.rearrange("p (h f) -> p h f", f=n)
                a, b = (r[:, 0:2 * heads * n].rearrange("p (h f) -> p h f", f=n) for r in (rope_a, rope_b))
                tt(a, src, cos, ALU.mult)
                link(tt(b, src, sin, ALU.mult))
                a4, b4 = (r[:, 0:2 * heads * n].rearrange("p (h s f) -> p h s f", s=2, f=n) for r in (rope_a, rope_b))
                d4 = dest.rearrange("p (h s f) -> p h s f", s=2, f=n)
                tt(d4[:, :, 0, :], a4[:, :, 0, :], b4[:, :, 1, :], ALU.subtract)
                return tt(d4[:, :, 1, :], a4[:, :, 1, :], b4[:, :, 0, :], ALU.add)

            IQ, IK = IDX_HEADS * IDX_DIM, IDX_DIM
            for t in range(TILES):
                job = ("proj_idx", t)
                wait_job(dve, job)
                if t:
                    wait_job(dve, ("T_idx", t - 1))
                link(rope(bank(job)[:, 0:IQ + IK], idx_nat[:, 0:IQ + IK], IDX_HEADS + 1, IDX_DIM, t))
                copy(idx_nat[:, IQ + IK:].rearrange("p (a b) -> p a b", a=3),
                     idx_nat[:, IQ:IQ + IK].unsqueeze(1).broadcast_to([P, 3, IK])).then_inc(idx_nat_ready, 1)
                ts(iw[:, t * IDX_HEADS:(t + 1) * IDX_HEADS], bank(job)[:, IQ + IK:IDX_COLS], IDX_HEADS ** -0.5, None, ALU.mult)
                link(tt(dt_x[:, t * SSD_HEADS:(t + 1) * SSD_HEADS], bank(job)[:, IDX_COLS:IDX_COLS + SSD_HEADS], heads_in[:, 0:SSD_HEADS], ALU.add))
                dve.sem_inc(free(job), 1)
            link(ts(dt_w[:, :], dt_x[:, :], -1.0, None, ALU.mult))
            tt(dt_e[:, :], dt_x[:, :], dt_w[:, :], ALU.min).then_inc(dt_arg_ready, 1)
            dve.wait_ge(dt_exp_ready, 1)
            link(ts(dt_w[:, :], dt_e[:, :], 2.0, None, ALU.add))
            link(nc.vector.reciprocal(dt_p[:, :], dt_w[:, :]))
            link(tt(dt_w[:, :], dt_e[:, :], dt_p[:, :], ALU.mult))
            link(tt(dt_w2[:, :], dt_w[:, :], dt_w[:, :], ALU.mult))
            link(ts(dt_p[:, :], dt_w2[:, :], 1.0 / 15.0, None, ALU.mult))
            for k in range(6, 0, -1):
                link(stt(dt_p[:, :], dt_p[:, :], 1.0 / (2 * k + 1), dt_w2[:, :], ALU.add, ALU.mult))
            link(stt(dt_p[:, :], dt_p[:, :], 1.0, dt_w[:, :], ALU.add, ALU.mult))
            link(ts(dt_x[:, :], dt_x[:, :], 0.0, None, ALU.max))
            link(stt(dt[:, :], dt_p[:, :], 2.0, dt_x[:, :], ALU.mult, ALU.add))
            link(ts(neg_a[:, :], neg_a[:, :], -1.0, None, ALU.mult))
            tt(dta[:, :].rearrange("p (t h) -> p t h", t=TILES), dt[:, :].rearrange("p (t h) -> p t h", t=TILES),
               neg_a[:, :].unsqueeze(1).broadcast_to([P, TILES, SSD_HEADS]), ALU.mult).then_inc(dta_ready, 1)

            def rope_qk(s, t):
                job = (("proj_q", "proj_k")[s], t)
                wait_job(dve, job)
                if t:
                    wait_job(dve, ("T_qk", s, t - 1))
                rope(bank(job)[:, :], qk_nat[:, s, :], HEADS, HEAD_DIM, t).then_inc(qk_nat_ready, 1)
                dve.wait_ge(qk_nat_ready, 2 * t + s + 1)
                dve.sem_inc(free(job), 1)

            def score_tile(t):
                nk = (t + 1) * P
                dve.wait_ge(rel_ready, t + 1)
                penalty = causal[:, SEQ - nk:]
                for h in range(IDX_HEADS):
                    before = penalty if h == 0 else score[:, 0:nk]
                    ins = stt(score[:, 0:nk], rel[:, h, 0:nk], iw[:, t * IDX_HEADS + h:t * IDX_HEADS + h + 1], before, ALU.mult, ALU.add)
                    if h < IDX_HEADS - 1:
                        link(ins)
                ins.then_inc(rel_used, 1)
                dve.wait_ge(rel_used, t + 1)
                for n in range(TOPK_KEYS // 8):
                    work = score if n == 0 else score_rest
                    link(nc.vector.max(top8[:, :], work[:, 0:nk]))
                    link(nc.vector.match_replace(score_rest[:, 0:nk], top8[:, :], work[:, 0:nk], TAKEN))
                link(ts(score[:, 0:nk], score_rest[:, 0:nk], TAKEN_BELOW, NOT_SELECTED, ALU.is_ge, ALU.mult))
                link(tt(select_bias[:, t, 0:nk], score[:, 0:nk], penalty, ALU.min))

            for t in range(TILES):
                for s in range(2):
                    rope_qk(s, t)
            dve.sem_inc(scratch_roped, 1)
            link(nc.vector.memset(xbc_raw[:, :, 0:CONV_WIDTH - 1], 0.0))
            score_tile(0)
            score_tile(1)
            for c in range(CT):
                if c % 2 == 0:
                    dve.wait_ge(raw_ready, c // 2 + 1)
                tap = lambda k: conv_t[:, k * CT + c:k * CT + c + 1]
                link(ts(xbc[:, c, :], xbc_raw[:, c, 0:SEQ], tap(0), tap(CONV_WIDTH), ALU.mult, ALU.add))
                for k in range(1, CONV_WIDTH):
                    ins = stt(xbc[:, c, :], xbc_raw[:, c, k:k + SEQ], tap(k), xbc[:, c, :], ALU.mult, ALU.add)
                    if k < CONV_WIDTH - 1:
                        link(ins)
                ins.then_inc(conv_ready, 1)

            def decay_argument(t):
                mine = slice(t * SSD_HEADS, (t + 1) * SSD_HEADS)
                job = ("cum_col", t)
                wait_job(dve, job)
                link(copy(cum[:, mine], bank(job)[:, 0:SSD_HEADS]))
                dve.sem_inc(free(job), 1)
                if t:
                    wait_job(dve, ("y_diag", t - 1))
                for half in range(2):
                    job = ("cum_row", t, half)
                    wait_job(dve, job)
                    if t == 0:
                        link(tt(to_end[:, 4 * half:4 * half + 4], bank(job)[:, P - 1:4 * P:P], cum[:, 4 * half:4 * half + 4], ALU.subtract))
                    for n in range(4):
                        h = 4 * half + n
                        ins = ts(decay[:, h, :], bank(job)[:, n * P:(n + 1) * P], cum[:, t * SSD_HEADS + h:t * SSD_HEADS + h + 1],
                                 0.0, ALU.subtract, ALU.min)
                    ins.then_inc(free(job), 1)
                    dve.wait_ge(free(job), use(job))
                dve.sem_inc(decay_arg_ready, 1)

            def take_logits(t):
                nk = (t + 1) * P
                if t:
                    wait_job(dve, ("T_p", t - 1, 2 * t - 1))
                for n in range(4):
                    job = ("logits", t, n)
                    wait_job(dve, job)
                    h = pairs_of(n)[0]
                    stt(logits[:, h:h + 3:2, 0:nk], bank_view(job, 2, nk), HEAD_DIM ** -0.5,
                        select_bias[:, t, 0:nk].unsqueeze(1).broadcast_to([P, 2, nk]), ALU.mult, ALU.add).then_inc(free(job), 1)
                    dve.wait_ge(free(job), use(job))
                link(nc.vector.tensor_reduce(row_max[:, :], logits[:, :, 0:nk], AX.X, ALU.max))
                ts(row_max[:, :], row_max[:, :], -1.0, None, ALU.mult).then_inc(logits_ready, 1)

            def source_side(t):
                job = ("cb", t)
                wait_job(dve, job)
                tt(cb_masked[:, :, :], bank_view(job, GROUPS, P), upper[:, :].unsqueeze(1).broadcast_to([P, GROUPS, P]),
                   ALU.mult).then_inc(free(job), 1)
                dve.wait_ge(free(job), use(job))
                job = ("T_xs", t)
                wait_job(dve, job)
                mine = slice(t * SSD_HEADS, (t + 1) * SSD_HEADS)
                copy(xs_nat, bank_view(job, SSD_HEADS, 64))
                link(tt(xdt, bank_view(job, SSD_HEADS, 64), dt[:, mine].unsqueeze(2).broadcast_to([P, SSD_HEADS, 64]), ALU.mult))
                dve.sem_inc(free(job), 1)
                dve.wait_ge(decay_ready, t + 1)
                if t == 0:
                    link(tt(xdt_end, xdt, to_end[:, :].unsqueeze(2).broadcast_to([P, SSD_HEADS, 64]), ALU.mult))
                dve.sem_inc(xdt_ready, 1)
                for g in range(GROUPS):
                    heads = slice(g * GROUP_HEADS, (g + 1) * GROUP_HEADS)
                    ins = tt(decay[:, heads, :], decay[:, heads, :], cb_masked[:, g, :].unsqueeze(1).broadcast_to([P, GROUP_HEADS, P]), ALU.mult)
                ins.then_inc(decay_masked, 1)

            def take_probs(t):
                if t:
                    wait_job(dve, ("pv", t - 1))
                for n in range(1, 2 * (t + 1), 2):
                    job = ("T_p", t, n)
                    wait_job(dve, job)
                    copy(probs_t[:, n // 2, 4:8, :], bank_view(job, 4, P)).then_inc(free(job), 1)
                    dve.wait_ge(free(job), use(job))
                    dve.sem_inc(probs_t_vec, 1)

            def take_attention(t):
                dve.wait_ge(probs_ready, t + 1)
                link(nc.vector.reciprocal(row_inv[:, :], row_sum[:, :]))
                job = ("pv", t)
                wait_job(dve, job)
                if t:
                    wait_job(dve, ("T_attn", t - 1))
                tt(attn, bank_view(job, HEADS, HEAD_DIM), row_inv[:, :].unsqueeze(2).broadcast_to([P, HEADS, HEAD_DIM]),
                   ALU.mult).then_inc(free(job), 1)
                dve.wait_ge(free(job), use(job))
                dve.sem_inc(attn_ready, 1)

            def take_ssd(t):
                if t:
                    wait_job(dve, ("T_y", t - 1))
                wide = lambda a: a.unsqueeze(2).broadcast_to([P, SSD_HEADS, 64])
                link(tt(y_ssd, xs_nat, wide(heads_in[:, 2 * SSD_HEADS:]), ALU.mult))
                if t:
                    job = ("y_off",)
                    wait_job(dve, job)
                    link(tt(xdt_end, bank_view(job, SSD_HEADS, 64), wide(exp_cum[:, :]), ALU.mult))
                    dve.sem_inc(free(job), 1)
                    link(tt(y_ssd, y_ssd, xdt_end, ALU.add))
                job = ("y_diag", t)
                wait_job(dve, job)
                link(tt(y_ssd, bank_view(job, SSD_HEADS, 64), y_ssd, ALU.add))
                dve.sem_inc(free(job), 1)
                flat = y_ssd.rearrange("p a b -> p (a b)")
                link(tt(flat, flat, z_silu[:, t, :], ALU.mult))
                for g in range(GROUPS):
                    part = flat[:, g * 256:(g + 1) * 256]
                    ins = stt(xdt.rearrange("p a b -> p (a b)")[:, g * 256:(g + 1) * 256], part, 1.0, part, ALU.mult, ALU.mult,
                              accum_out=squares[:, g:g + 1])
                link(ins)
                ts(rms[:, :], squares[:, :], 1.0 / 256, LN_EPS, ALU.mult, ALU.add).then_inc(rms_arg_ready, 1)
                dve.wait_ge(rms_ready, t + 1)
                link(nc.vector.reciprocal(rms[:, :], rms[:, :]))
                for g in range(GROUPS):
                    part = slice(g * 256, (g + 1) * 256)
                    ins = stt(flat[:, part], flat[:, part], rms[:, g:g + 1], norm_w[:, part], ALU.mult, ALU.mult)
                ins.then_inc(y_ready, 1)

            def layer_norm(t, n, done):
                row = x_sb[:, t, :]
                for half in range(2):
                    ins = nc.vector.bn_stats(stats[:, 6 * half:6 * half + 6], row[:, half * 512:(half + 1) * 512])
                link(ins)
                link(nc.vector.bn_aggr(moments[:, :], stats[:, :]))
                ts(rstd[:, :], moments[:, 1:2], LN_EPS, None, ALU.add).then_inc(var_ready, 1)
                dve.wait_ge(std_ready, n + 1)
                link(nc.vector.reciprocal(rstd[:, :], rstd[:, :]))
                link(ts(row, row, moments[:, 0:1], rstd[:, :], ALU.subtract, ALU.mult))
                link(tt(row, row, ln_gb[:, 0, :], ALU.mult))
                tt(row, row, ln_gb[:, 1, :], ALU.add).then_inc(done, 1)

            def residual(t):
                for half in range(2):
                    job, part = ("out", t, half), slice(half * 512, (half + 1) * 512)
                    wait_job(dve, job)
                    stt(x_sb[:, t, part], x_sb[:, t, part], ALPHA, bank(job)[:, :], ALU.mult, ALU.add).then_inc(free(job), 1)
                    dve.wait_ge(free(job), use(job))

            decay_argument(0)
            take_logits(0)
            dve.wait_ge(ln1_in, 3 * 16)
            source_side(0)
            take_probs(0)
            take_attention(0)
            take_ssd(0)
            decay_argument(1)
            take_logits(1)
            source_side(1)
            residual(0)
            layer_norm(0, 0, h_ready)
            take_probs(1)
            take_attention(1)
            take_ssd(1)
            residual(1)
            layer_norm(1, 1, h_ready)
            dve.wait_ge(h_ready, TILES)
            dve.sem_inc(ln1_done, 1)

            def take_queries(t):
                if t:
                    wait_job(dve, ("key_scores", t - 1, 3))
                for c in (1, 3):
                    job = ("peer_q", t, c)
                    wait_job(dve, job)
                    copy(peer_q_t[:, 4 * c:4 * c + 4, :], bank_view(job, 4, P)).then_inc(free(job), 1)
                    dve.wait_ge(free(job), use(job))
                    dve.sem_inc(peer_q_vec, 1)

            def route(u, parity):
                link_to_search(copy(side_scores.rearrange("p a b -> p (a b)"), big[:, bass.ds(u * 2 * N_KEYS, 2 * N_KEYS)]))
                for s in range(2):
                    ins = nc.vector.max(top_v[:, s, 0:8], side_scores[:, s, :])
                link_to_search(ins)
                for s in range(2):
                    nc.vector.max_index(top_i[:, s, 0:8], top_v[:, s, 0:8], side_scores[:, s, :])
                for s in range(2):
                    ins = nc.vector.match_replace(side_rest[:, s, :], top_v[:, s, 0:8], side_scores[:, s, :], TAKEN)
                link_to_search(ins)
                for s in range(2):
                    ins = nc.vector.max(top_v[:, s, 8:16], side_rest[:, s, :])
                link_to_search(ins)
                for s in range(2):
                    nc.vector.max_index(top_i[:, s, 8:16], top_v[:, s, 8:16], side_rest[:, s, :])
                link(tt(cand, top_v[:, 0, :].unsqueeze(2).broadcast_to([P, 16, 16]),
                        top_v[:, 1, :].unsqueeze(1).broadcast_to([P, 16, 16]), ALU.add))
                flat = cand.rearrange("p a b -> p (a b)")
                copy(top_if[:, :, :], top_i[:, :, :])
                link_to_search(nc.vector.max(best[:, 0:8], flat))
                nc.vector.max_index(best_pos[:, 0:8], best[:, 0:8], flat)
                link_to_search(nc.vector.match_replace(cand_rest, best[:, 0:8], flat, TAKEN))
                link(nc.vector.max(best[:, 8:16], cand_rest))
                ts(neg_best[:, :], best[:, 0:1], -1.0, None, ALU.mult).then_inc(best_ready, 1)
                link(nc.vector.max_index(best_pos[:, 8:16], best[:, 8:16], cand_rest))
                nc.vector.tensor_single_scalar(pos_ij[:, 0, :], best_pos[:, :], 4, ALU.logical_shift_right)
                link(nc.vector.tensor_single_scalar(pos_ij[:, 1, :], best_pos[:, :], 15, ALU.bitwise_and))
                link(copy(pos_ijf[:, :, :], pos_ij[:, :, :]))
                oh = one_hot.rearrange("p s k c -> p (s k) c")
                link(tt(oh, pos_ijf[:, :, :].rearrange("p s k -> p (s k)").unsqueeze(2).broadcast_to([P, 32, 16]),
                        iota16[:, :].unsqueeze(1).broadcast_to([P, 32, 16]), ALU.is_equal))
                link(tt(one_hot, one_hot, top_if[:, :, :].unsqueeze(2).broadcast_to([P, 2, 16, 16]), ALU.mult))
                link(nc.vector.tensor_reduce(picked[:, :, :].rearrange("p s k -> p (s k)"), oh, AX.X, ALU.add))
                stt(expert[:, parity, :], picked[:, 0, :], float(N_KEYS), picked[:, 1, :], ALU.mult, ALU.add).then_inc(experts_ready, 1)

            def finish_gate(u, parity):
                dve.wait_ge(gate_exp_ready, u + 1)
                link(nc.vector.reciprocal(gate_sum[:, :], gate_sum[:, :]))
                ts(gate[:, parity, :], gate_e[:, :], gate_sum[:, :], None, ALU.mult).then_inc(gate_ready, 1)

            def take_sum(u, tile, parity):
                dve.wait_ge(slot_used, (u + 1) * SLOTS)
                for half in range(2):
                    where = mix[:, bass.ds(tile * D_MODEL + half * 512, 512)]
                    ins = tt(where, banks[2 * parity + half][:, :], where, ALU.add)
                ins.then_inc(sum_taken, 1)

            def dot_unit(u, tile, parity, former_tile=None, last=False):
                if not last:
                    route(u + 1, 1 - parity)
                for g in range(4):
                    for j in range(4 * g, 4 * g + 4):
                        dve.wait_ge(rows_in[j], 16 * (u + 1))
                        rows = arena[:, j * SLOT:j * SLOT + D_MODEL]
                        ins = stt(rows, x_rows[:, bass.ds(tile * D_MODEL, D_MODEL)], 1.0, rows,
                                  ALU.mult, ALU.mult, accum_out=dots[:, parity, j:j + 1])
                    ins.then_inc(dots_ready, 1)
                    if g == 0:
                        if former_tile is not None:
                            take_sum(u - 1, former_tile, 1 - parity)
                        if not last:
                            finish_gate(u + 1, 1 - parity)

            x_rows = x_sb[:, :, :].rearrange("p a b -> p (a b)")
            take_queries(0)
            dve.wait_ge(scores_ready, 1)
            route(0, 0)
            finish_gate(0, 0)
            take_queries(1)
            dve.wait_ge(scores_ready, 8)
            link(nc.vector.memset(mix[:, :], 0.0))
            dve.sem_inc(sum_taken, 1)
            before = count[0]
            dot_unit(0, 0, 0)
            per_unit = count[0] - before
            with dve.Fori(0, UNITS // 2 - 1) as i:
                for n in (1, 2):
                    u = 2 * i + n
                    count[1] = i * 2 * per_unit
                    dot_unit(u, u // PEER_HEADS, n % 2, (u - 1) // PEER_HEADS)
            count[1] = (UNITS // 2 - 2) * 2 * per_unit
            dot_unit(UNITS - 1, TILES - 1, 1, TILES - 1, last=True)
            take_sum(UNITS - 1, TILES - 1, 1)
            dve.wait_ge(sum_taken, UNITS + 1)
            dve.wait_ge(ln2_in, 32)
            for t in range(TILES):
                link(stt(x_sb[:, t, :], x_sb[:, t, :], ALPHA, ffn[:, t, :], ALU.mult, ALU.add))
                layer_norm(t, TILES + t, result_ready)


def kernel(**inputs):
    import concourse.bacc as bacc
    from concourse.bass_utils import run_bass_kernel_spmd

    row = lambda name: np.ascontiguousarray(np.asarray(inputs[name])[0])
    freqs = lambda d: (np.float32(ROPE_THETA) ** (-np.arange(0, d, 2, dtype=np.float32) / np.float32(d))).astype(np.float32)
    arrays = {"x": row("x"), "positions": row("positions")}
    arrays["inv_freq"] = np.concatenate([freqs(HEAD_DIM), freqs(IDX_DIM)])
    for name in ("w_in", "conv_w", "conv_b", "dt_bias", "a_log", "d_skip", "ssm_norm_w", "w_out",
                 "ln1_g", "ln1_b", "peer_wq", "peer_k1", "peer_k2"):
        arrays[name] = row(name)
    arrays["expert_uv"] = np.concatenate([row("peer_u"), row("peer_v")], axis=1)
    arrays["ln2_g"], arrays["ln2_b"] = row("ln2_g"), row("ln2_b")

    nc = bacc.Bacc("TRN2", target_bir_lowering=False, num_devices=1)
    args = [nc.dram_tensor(f"in_{n}", a.shape, mybir.dt.from_np(a.dtype), kind="ExternalInput").ap() for n, a in arrays.items()]
    out = nc.dram_tensor("out", (SEQ, D_MODEL), mybir.dt.float32, kind="ExternalOutput").ap()
    build_layer(nc, *args, out)
    got = run_bass_kernel_spmd(nc, [{f"in_{n}": a for n, a in arrays.items()}], core_ids=[0])
    return got.results[0]["out"].reshape(1, SEQ, D_MODEL)
```

```python
from contextlib import ExitStack

import concourse.bass as bass
import numpy as np
from concourse import mybir

P = 128
D_MODEL, SEQ = 1024, 256
TILES = SEQ // P
KT = D_MODEL // P
HEADS, HEAD_DIM = 8, 64
ATTN_WIDTH = HEADS * HEAD_DIM
IDX_HEADS, IDX_DIM = 8, 32
TOPK_KEYS = min(256, SEQ // 4)
SSD_HEADS, SSD_WIDTH, GROUPS, CONV_WIDTH = 8, 512, 2, 4
GROUP_HEADS = SSD_HEADS // GROUPS
IDX_COLS = IDX_HEADS * IDX_DIM + IDX_DIM + IDX_HEADS
XBC_WIDTH = SSD_WIDTH + 2 * GROUPS * P
CT = XBC_WIDTH // P
Q0, K0, V0, I0 = 0, ATTN_WIDTH, 2 * ATTN_WIDTH, 3 * ATTN_WIDTH
Z0 = I0 + IDX_COLS
X0 = Z0 + SSD_WIDTH
DT0 = X0 + XBC_WIDTH
PEER_HEADS, N_KEYS, PEER_TOPK = 8, 128, 16
SIDES = 2 * PEER_HEADS
UNITS = TILES * PEER_HEADS
SLOTS = PEER_TOPK
ROPE_THETA, LN_EPS = 10000.0, 1e-5
ALPHA = 2.0 ** 0.25
TWO_PI = 2.0 * np.pi
TWO_PI_HI = 6.28125
TWO_PI_MID = float(np.float32(np.round((TWO_PI - TWO_PI_HI) * 2.0 ** 20) / 2.0 ** 20))
TWO_PI_LO = float(np.float32(TWO_PI - TWO_PI_HI - TWO_PI_MID))
ROUND_MAGIC = 1.5 * 2.0 ** 23
SIN_LIMIT = 3.1415925
NON_CAUSAL, TAKEN, TAKEN_BELOW, NOT_SELECTED = -3.0e38, -3.4e38, -3.2e38, -1.0e30
HALF_FREQS = HEAD_DIM // 2 + IDX_DIM // 2

PSUM_BANKS = 8


def psum_jobs():
    both = range(TILES)
    sums = [[("cum_col", t), ("cum_row", t, 0), ("cum_row", t, 1)] for t in both]
    idx_dots = [[("idx_dot", t, g) for g in range(4)] for t in both]
    logits = [[("logits", t, n) for n in range(4)] for t in both]
    jobs = [("xT", t, half) for t in both for half in range(2)]
    jobs += [("proj_idx", t) for t in both] + [("proj_q", t) for t in both] + [("T_idx", t) for t in both]
    jobs += [("proj_k", 0)] + idx_dots[0] + [("proj_k", 1)] + idx_dots[1]
    jobs += [("consts",), ("T_qk", 0, 0), ("T_qk", 0, 1), ("proj_xbc", 0), ("proj_xbc", 1)]
    jobs += [("T_qk", 1, 0), ("T_qk", 1, 1), ("proj_xbc", 2), ("proj_xbc", 3)]
    jobs += sums[0] + logits[0] + [("proj_z", t) for t in both]
    jobs += [("cb", 0), ("T_xs", 0), ("T_b",), ("T_p", 0, 0), ("T_p", 0, 1)] + logits[1]
    jobs += [("proj_v", 0), ("y_diag", 0), ("state",)] + sums[1] + [("pv", 0), ("proj_v", 1)]
    jobs += [("T_y", 0), ("T_attn", 0), ("cb", 1), ("T_xs", 1), ("out", 0, 0)]
    jobs += [("T_p", 1, n) for n in range(4)] + [("out", 0, 1), ("y_off",), ("y_diag", 1), ("pv", 1)]
    queries = [[("peer_q", t, c) for c in range(4)] for t in both]
    key_scores = [[("key_scores", t, c) for c in range(4)] for t in both]
    jobs += [("T_h", 0, half) for half in range(2)] + queries[0][:2] + [("T_y", 1)] + queries[0][2:3]
    jobs += [("T_attn", 1)] + queries[0][3:] + key_scores[0] + [("out", 1, half) for half in range(2)]
    jobs += [("T_h", 1, half) for half in range(2)] + queries[1] + key_scores[1]
    return jobs


def build_layer(nc, x, positions, inv_freq, w_in, conv_w, conv_b, dt_bias, a_log, d_skip, ssm_norm_w,
                w_out, ln1_g, ln1_b, peer_wq, peer_k1, peer_k2, expert_uv, ln2_g, ln2_b, out):
    f32, i32, u32 = mybir.dt.float32, mybir.dt.int32, mybir.dt.uint32
    ALU, ACT, AX = mybir.AluOpType, mybir.ActivationFunctionType, mybir.AxisListType

    jobs = {name: n for n, name in enumerate(psum_jobs())}
    ctx = ExitStack()
    with ctx:
        def sb(name, words, dtype=f32):
            return ctx.enter_context(nc.sbuf_tensor(name, [P, words], dtype))

        def sem(name):
            return ctx.enter_context(nc.semaphore(name))

        CHUNK, SLOT = KT * 512, 2 * D_MODEL
        arena = sb("arena", SLOTS * SLOT)
        SCRATCH = 0

        def view(tensor, at, *dims):
            size = int(np.prod(dims))
            flat = tensor[:, at:at + size]
            if len(dims) == 2:
                return flat.rearrange("p (a b) -> p a b", a=dims[0])
            if len(dims) == 3:
                return flat.rearrange("p (a b c) -> p a b c", a=dims[0], b=dims[1])
            return flat

        def chunk(position, columns=512):
            return view(arena, position * CHUNK, KT, columns)

        logits = view(arena, SCRATCH, HEADS, SEQ)
        rel = logits
        RAW_LEN = SEQ + CONV_WIDTH - 1
        xbc_raw = view(arena, SCRATCH + 2048, CT, RAW_LEN)
        rope_a = view(arena, SCRATCH + 2048, 512)
        rope_b = view(arena, SCRATCH + 2560, 512)
        at = SCRATCH + 2048 + CT * RAW_LEN
        decay = view(arena, at, SSD_HEADS, P)
        turns = view(arena, at, 2 * TILES * HALF_FREQS)
        keys_nat = view(arena, at + 256, 2, P)
        conv_nat = view(arena, at + 512, P)
        idx_nat = view(arena, at + 640, 3 * P)
        xs_nat = view(arena, at + 1024, SSD_HEADS, 64)
        xdt = view(arena, at + 1536, SSD_HEADS, 64)
        xdt_end = view(arena, at + 2048, SSD_HEADS, 64)
        state_t = view(arena, at + 2560, SSD_WIDTH)
        y_ssd = view(arena, at + 3072, SSD_HEADS, 64)
        b_nat = view(arena, at + 3584, GROUPS, P)
        assert at + 3584 + GROUPS * P <= SCRATCH + 2 * CHUNK

        x_sb = ctx.enter_context(nc.sbuf_tensor("x_sb", [P, TILES, D_MODEL], f32))
        x_t = ctx.enter_context(nc.sbuf_tensor("x_t", [P, KT, SEQ], f32))
        h_t = x_t
        mix = sb("mix", KT * SEQ)
        peer_q_t = view(mix, 0, SIDES, P)
        ffn = view(mix, 0, TILES, D_MODEL)
        big = sb("big", 4096)
        q_t, k_t, xbc = view(big, 0, 4, SEQ), view(big, 1024, 4, SEQ), view(big, 2048, CT, SEQ)
        mix_t = [view(mix, 0, KT, P), view(big, 2048, KT, P)]
        iq_t = ctx.enter_context(nc.sbuf_tensor("iq_t", [P, 2, SEQ], f32))
        ik_t = sb("ik_t", SEQ)
        mid = sb("mid", 3584)
        v_sb, z_silu = view(mid, 0, TILES, 512), view(mid, 1024, TILES, 512)
        qk_nat = [view(mid, 2048, 2, 512), view(mid, 1024, 2, 512)]
        attn = view(mid, 3072, HEADS, HEAD_DIM)
        probs_t = [view(mid, 2048, 1, HEADS, P), view(arena, SCRATCH + 2048, TILES, HEADS, P)]
        diag = view(mid, 1024, 8, P)
        cand, cand_rest = view(mid, 2048, 16, 16), view(mid, 2304, 256)
        side_scores, side_rest = view(mid, 2560, 2, N_KEYS), view(mid, 2816, 2, N_KEYS)
        one_hot = view(mid, 3072, 2, 16, 16)
        ln_gb = ctx.enter_context(nc.sbuf_tensor("ln_gb", [P, 2, D_MODEL], f32))
        ident, upper = sb("ident", P), sb("upper", P)
        keys_t = ctx.enter_context(nc.sbuf_tensor("keys_t", [P, 2, P], f32))
        conv_t = sb("conv_t", (CONV_WIDTH + 1) * CT)
        cb_masked = ctx.enter_context(nc.sbuf_tensor("cb_masked", [P, GROUPS, P], f32))
        score, score_rest = sb("score", SEQ), sb("score_rest", SEQ)
        causal = sb("causal", SEQ)
        select_bias = ctx.enter_context(nc.sbuf_tensor("select_bias", [P, TILES, SEQ], f32))
        norm_w = sb("norm_w", SSD_WIDTH)
        sin_cos = sb("sin_cos", 2 * TILES * HALF_FREQS)
        sin_cos4 = sin_cos[:, :].rearrange("p (s t f) -> p s t f", s=2, t=TILES)
        freqs, pos_i, pos_f = sb("freqs", HALF_FREQS), sb("pos_i", TILES, i32), sb("pos_f", TILES)
        iw = sb("iw", TILES * IDX_HEADS)
        heads_in = sb("heads_in", 3 * SSD_HEADS)
        dt_x, dt_e = sb("dt_x", TILES * SSD_HEADS), sb("dt_e", TILES * SSD_HEADS)
        dt_w, dt_w2, dt_p = (sb(n, TILES * SSD_HEADS) for n in ("dt_w", "dt_w2", "dt_p"))
        dt, dta, cum = (sb(n, TILES * SSD_HEADS) for n in ("dt", "dta", "cum"))
        neg_a, to_end, exp_cum = sb("neg_a", SSD_HEADS), sb("to_end", SSD_HEADS), sb("exp_cum", SSD_HEADS)
        top8 = sb("top8", 8)
        row_max, row_sum, row_inv = sb("row_max", HEADS), sb("row_sum", TILES * HEADS), sb("row_inv", HEADS)
        squares, rms = sb("squares", GROUPS), sb("rms", GROUPS)
        stats, moments, rstd = sb("stats", 12), sb("moments", 2), sb("rstd", 1)
        top_v = ctx.enter_context(nc.sbuf_tensor("top_v", [P, 2, 16], f32))
        top_i = ctx.enter_context(nc.sbuf_tensor("top_i", [P, 2, 16], u32))
        top_if = ctx.enter_context(nc.sbuf_tensor("top_if", [P, 2, 16], f32))
        best, neg_best = sb("best", 16), sb("neg_best", 1)
        best_pos = sb("best_pos", 16, u32)
        pos_ij = ctx.enter_context(nc.sbuf_tensor("pos_ij", [P, 2, 16], u32))
        pos_ijf = ctx.enter_context(nc.sbuf_tensor("pos_ijf", [P, 2, 16], f32))
        picked = ctx.enter_context(nc.sbuf_tensor("picked", [P, 2, 16], f32))
        iota16 = sb("iota16", 16)
        expert = ctx.enter_context(nc.sbuf_tensor("expert", [P, 2, 16], i32))
        gate_e, gate_sum = sb("gate_e", 16), sb("gate_sum", 1)
        gate = ctx.enter_context(nc.sbuf_tensor("gate", [P, 2, 16], f32))
        dots = ctx.enter_context(nc.sbuf_tensor("dots", [P, 2, 16], f32))
        gelu = ctx.enter_context(nc.sbuf_tensor("gelu", [P, 2, 16], f32))
        weight = ctx.enter_context(nc.sbuf_tensor("weight", [P, 2, 16], f32))

        banks = [ctx.enter_context(nc.psum_tensor(f"bank{n}", [P, 512], f32)) for n in range(PSUM_BANKS)]

        bank_full = [sem(f"bank_full{n}") for n in range(PSUM_BANKS)]
        bank_free = [sem(f"bank_free{n}") for n in range(PSUM_BANKS)]
        x_in = [sem(f"x_in{t}") for t in range(TILES)]
        w_names = ["idx", "q", "k", "xbc0", "xbc1", "z", "v", "out0", "wq0", "wq1", "wq2", "wq3", "out1"]
        w_in_sem = {n: sem(f"w_{n}_in") for n in w_names}
        small_in, keys_in, ln1_in, ln2_in = sem("small_in"), sem("keys_in"), sem("ln1_in"), sem("ln2_in")
        consts_ready, ident_step = sem("consts_ready"), sem("ident_step")
        vec_step, act_step, searches = sem("vec_step"), sem("act_step"), sem("searches")
        turns_ready, rope_ready = sem("turns_ready"), sem("rope_ready")
        x_t_vec = sem("x_t_vec")
        dt_arg_ready, dt_exp_ready, dta_ready = sem("dt_arg_ready"), sem("dt_exp_ready"), sem("dta_ready")
        idx_nat_ready = sem("idx_nat_ready")
        qk_nat_ready = [sem("q_nat_ready"), sem("k_nat_ready")]
        scratch_roped = sem("scratch_roped")
        idx_t_ready, qk_t_ready, rel_ready, rel_used = (sem(n) for n in ("idx_t_ready", "qk_t_ready", "rel_ready", "rel_used"))
        z_ready, raw_ready, conv_ready, silu_ready, v_ready = (sem(n) for n in ("z_ready", "raw_ready", "conv_ready", "silu_ready", "v_ready"))
        consts_t_ready = sem("consts_t_ready")
        decay_arg_ready, decay_ready, decay_masked = (sem(n) for n in ("decay_arg_ready", "decay_ready", "decay_masked"))
        logits_ready, probs_ready, probs_t_act, probs_t_vec = (sem(n) for n in ("logits_ready", "probs_ready", "probs_t_act", "probs_t_vec"))
        xs_ready, b_nat_ready, xdt_ready, state_ready = (sem(n) for n in ("xs_ready", "b_nat_ready", "xdt_ready", "state_ready"))
        attn_ready, attn_t_ready = sem("attn_ready"), sem("attn_t_ready")
        rms_arg_ready, rms_ready, y_ready, y_t_ready = (sem(n) for n in ("rms_arg_ready", "rms_ready", "y_ready", "y_t_ready"))
        var_ready, std_ready, h_ready, ln1_done = (sem(n) for n in ("var_ready", "std_ready", "h_ready", "ln1_done"))
        h_t_ready, peer_q_act, peer_q_vec, scores_ready = (sem(n) for n in ("h_t_ready", "peer_q_act", "peer_q_vec", "scores_ready"))
        experts_ready, best_ready, gate_exp_ready, gate_ready = (sem(n) for n in ("experts_ready", "best_ready", "gate_exp_ready", "gate_ready"))
        rows_in = [sem(f"rows_in{j}") for j in range(SLOTS)]
        rows_asked = sem("rows_asked")
        dots_ready, gelu_ready, weight_ready, diag_ready = (sem(n) for n in ("dots_ready", "gelu_ready", "weight_ready", "diag_ready"))
        slot_used, sum_taken = sem("slot_used"), sem("sum_taken")
        result_ready, out_stored = sem("result_ready"), sem("out_stored")

        def bank(job):
            return banks[jobs[job] % PSUM_BANKS]

        def use(job):
            return jobs[job] // PSUM_BANKS + 1

        def wait_bank(pe, job):
            if use(job) > 1:
                pe.wait_ge(bank_free[jobs[job] % PSUM_BANKS], use(job) - 1)

        def full(job):
            return bank_full[jobs[job] % PSUM_BANKS]

        def free(job):
            return bank_free[jobs[job] % PSUM_BANKS]

        def wait_job(engine, job):
            engine.wait_ge(full(job), use(job))

        def cast_rows(a):
            return a.partition_broadcast(P)

        places = {"idx": 3, "q": 2, "k": 4, "xbc0": 5, "xbc1": 6, "z": 7, "v": 3, "out0": 2, "out1": 3,
                  "wq0": 4, "wq1": 5, "wq2": 6, "wq3": 7}
        w_rows = w_in.rearrange("(k p) n -> p k n", p=P)
        w_out_rows = w_out.rearrange("(k p) n -> p k n", p=P)
        wq_rows = peer_wq.rearrange("(k p) n -> p k n", p=P)
        frees = {"v": ("proj_idx", 1), "out0": ("proj_q", 1), "wq0": ("proj_k", 1), "wq1": ("proj_xbc", 1),
                 "wq2": ("proj_xbc", 3), "wq3": ("proj_z", 1), "out1": ("proj_v", 1)}
        columns = {"q": Q0, "k": K0, "z": Z0, "xbc0": X0, "xbc1": X0 + 512, "v": V0}
        block = ctx.enter_context(nc.Block())

        def pairs_of(n):
            par, jj = n % 2, n // 2
            return par + 4 * jj, par + 4 * jj + 2

        def slot_groups(last):
            sizes = (4, 4, 4, 2, 1, 1) if last else (4, 4, 4, 4)
            ends = np.cumsum(sizes).tolist()
            return [range(end - size, end) for size, end in zip(sizes, ends)]

        def exp_gate(act, u):
            act.wait_ge(best_ready, u + 1)
            nc.scalar.activation(gate_e[:, :], best[:, :], ACT.Exp, bias=neg_best[:, :],
                                 accum_out=gate_sum[:, :]).then_inc(gate_exp_ready, 1)

        @block.sync
        def _(sp):
            for t in range(TILES):
                sp.dma_start(x_sb[:, t, :], x[t * P:(t + 1) * P, :]).then_inc(x_in[t], 16)
            for name in w_names:
                if name in frees:
                    wait_job(sp, frees[name])
                if name == "z":
                    for place, source in ((norm_w[:, :], ssm_norm_w), (ln_gb[:, 0, :], ln1_g), (ln_gb[:, 1, :], ln1_b)):
                        sp.dma_start(place, cast_rows(source)).then_inc(ln1_in, 16)
                if name == "q":
                    sp.wait_ge(small_in, 6 * 16)
                    sp.wait_ge(keys_in, 4 * 16)
                if name == "idx":
                    place = chunk(places[name], IDX_COLS + SSD_HEADS)
                    sp.dma_start(place[:, :, 0:IDX_COLS], w_rows[:, :, I0:I0 + IDX_COLS]).then_inc(w_in_sem[name], 16)
                    sp.dma_start(place[:, :, IDX_COLS:], w_rows[:, :, DT0:DT0 + SSD_HEADS]).then_inc(w_in_sem[name], 16)
                elif name in columns:
                    sp.dma_start(chunk(places[name]), w_rows[:, :, columns[name]:columns[name] + 512]).then_inc(w_in_sem[name], 16)
                else:
                    source = w_out_rows if name.startswith("out") else wq_rows
                    n = int(name[-1])
                    sp.dma_start(chunk(places[name]), source[:, :, n * 512:(n + 1) * 512]).then_inc(w_in_sem[name], 16)
            sp.wait_ge(ln1_done, 1)
            sp.dma_start(ln_gb[:, 0, :], cast_rows(ln2_g)).then_inc(ln2_in, 16)
            sp.dma_start(ln_gb[:, 1, :], cast_rows(ln2_b)).then_inc(ln2_in, 16)
            for t in range(TILES):
                for half in range(2):
                    part = slice(half * 512, (half + 1) * 512)
                    sp.wait_ge(result_ready, 2 * t + half + 1)
                    sp.dma_start(out[t * P:(t + 1) * P, part], x_sb[:, t, part]).then_inc(out_stored, 16)
            sp.wait_ge(out_stored, 2 * 16 * TILES)

        @block.gpsimd
        def _(pool):
            pool.memset(ident[:, :], 0.0).then_inc(ident_step, 1)
            pool.memset(upper[:, :], 1.0).then_inc(ident_step, 1)
            pool.memset(causal[:, :], 0.0).then_inc(ident_step, 1)
            pool.wait_ge(ident_step, 3)
            pool.affine_select(out=ident[:, :], in_=ident[:, :], compare_op=ALU.not_equal, fill=1.0, base=0,
                               pattern=[[-1, P]], channel_multiplier=1).then_inc(consts_ready, 1)
            pool.affine_select(out=upper[:, :], in_=upper[:, :], compare_op=ALU.is_ge, fill=0.0, base=0,
                               pattern=[[1, P]], channel_multiplier=-1).then_inc(consts_ready, 1)
            pool.affine_select(out=causal[:, P:SEQ], in_=causal[:, P:SEQ], compare_op=ALU.is_ge, fill=NON_CAUSAL, base=0,
                               pattern=[[-1, P]], channel_multiplier=1).then_inc(consts_ready, 1)
            pool.iota(iota16[:, :], pattern=[[1, 16]], base=0, channel_multiplier=0,
                      allow_small_or_imprecise_dtypes=True).then_inc(consts_ready, 1)

            last_readers = {4: ("out", 1, 0), 6: ("out", 1, 1), 8: ("peer_q", 1, 0), 10: ("peer_q", 1, 1),
                            12: ("peer_q", 1, 2), 14: ("peer_q", 1, 3)}

            def gather_unit(u, parity, first=False):
                pool.wait_ge(experts_ready, u + 1)
                for j in range(SLOTS):
                    if not first:
                        pool.wait_ge(slot_used, (u - 1) * SLOTS + j + 1)
                    if not first or j == 0:
                        pool.sem_inc(rows_asked, 1)
                    if first and j in last_readers:
                        wait_job(pool, last_readers[j])
                    pool.indirect_dma_start(
                        out=arena[:, j * SLOT:(j + 1) * SLOT], out_offset=None, in_=expert_uv,
                        in_offset=bass.IndirectOffsetOnAxis(ap=expert[:, parity, j:j + 1], axis=0),
                    ).then_inc(rows_in[j], 16)

            gather_unit(0, 0, first=True)
            with pool.Fori(0, UNITS // 2 - 1) as i:
                gather_unit(2 * i + 1, 1)
                gather_unit(2 * i + 2, 0)
            gather_unit(UNITS - 1, 1)

        @block.tensor
        def _(pe):
            mm = nc.tensor.matmul

            def transposes(job, sources):
                wait_bank(pe, job)
                for n, source in enumerate(sources):
                    last = nc.tensor.transpose(bank(job)[:, n * P:(n + 1) * P], source, ident[:, :])
                last.then_inc(full(job), 1)

            def project(job, name, t, columns=512, start=True):
                wait_bank(pe, job)
                for k in range(KT):
                    last = mm(bank(job)[:, 0:columns], lhsT=x_t[:, k, t * P:(t + 1) * P],
                              rhs=chunk(places[name], columns)[:, k, :], start=k == 0, stop=k == KT - 1)
                last.then_inc(full(job), 1)

            pe.wait_ge(consts_ready, 4)
            for t in range(TILES):
                pe.wait_ge(x_in[t], 16)
                for half in range(2):
                    transposes(("xT", t, half), [x_sb[:, t, k * P:(k + 1) * P] for k in range(4 * half, 4 * half + 4)])
            pe.wait_ge(x_t_vec, 2)
            pe.wait_ge(act_step, 2)
            pe.wait_ge(w_in_sem["idx"], 32)
            for t in range(TILES):
                project(("proj_idx", t), "idx", t, IDX_COLS + SSD_HEADS)
            pe.wait_ge(w_in_sem["q"], 16)
            for t in range(TILES):
                project(("proj_q", t), "q", t)
            for t in range(TILES):
                pe.wait_ge(idx_nat_ready, t + 1)
                transposes(("T_idx", t), [idx_nat[:, n * P:(n + 1) * P] for n in range(3)])

            def transposed_qk(s, t):
                pe.wait_ge(qk_nat_ready[s], t + 1)
                transposes(("T_qk", s, t), [qk_nat[t][:, s, n * P:(n + 1) * P] for n in range(4)])

            pe.wait_ge(w_in_sem["k"], 16)
            for t in range(TILES):
                project(("proj_k", t), "k", t)
                pe.wait_ge(idx_t_ready, t + 1)
                nk = (t + 1) * P
                for g in range(4):
                    job = ("idx_dot", t, g)
                    wait_bank(pe, job)
                    rows = slice(32 * g, 32 * g + 32)
                    for n in range(2):
                        last = mm(bank(job)[:, n * nk:(n + 1) * nk], lhsT=iq_t[rows, n, t * P:(t + 1) * P],
                                  rhs=ik_t[rows, 0:nk], start=True, stop=True)
                    last.then_inc(full(job), 1)
            job = ("consts",)
            pe.wait_ge(keys_in, 4 * 16)
            wait_bank(pe, job)
            for s in range(2):
                nc.tensor.transpose(bank(job)[:, s * P:(s + 1) * P], keys_nat[:, s, :], ident[:, :])
            rows = (CONV_WIDTH + 1) * CT
            nc.tensor.transpose(bank(job)[:, 2 * P:2 * P + rows], conv_nat[0:rows, :], ident[0:rows, 0:rows]).then_inc(full(job), 1)

            for n in range(CT // 2):
                if n % 2 == 0:
                    for t in range(TILES):
                        transposed_qk(n // 2, t)
                    pe.wait_ge(w_in_sem[f"xbc{n // 2}"], 16)
                job, name = ("proj_xbc", n), f"xbc{n // 2}"
                wait_bank(pe, job)
                for c in range(2):
                    col = (2 * (n % 2) + c) * P
                    for k in range(KT):
                        last = mm(bank(job)[:, c * SEQ:(c + 1) * SEQ], lhsT=chunk(places[name])[:, k, col:col + P],
                                  rhs=x_t[:, k, :], start=k == 0, stop=k == KT - 1)
                last.then_inc(full(job), 1)
            pe.wait_ge(dta_ready, 1)

            def running_sums(t):
                job = ("cum_col", t)
                wait_bank(pe, job)
                mm(bank(job)[:, 0:SSD_HEADS], lhsT=upper[:, :], rhs=dta[:, t * SSD_HEADS:(t + 1) * SSD_HEADS],
                   start=True, stop=True).then_inc(full(job), 1)
                for half in range(2):
                    job = ("cum_row", t, half)
                    wait_bank(pe, job)
                    for n in range(4):
                        col = t * SSD_HEADS + 4 * half + n
                        last = mm(bank(job)[:, n * P:(n + 1) * P], lhsT=dta[:, col:col + 1].broadcast_to([P, P]),
                                  rhs=upper[:, :], start=True, stop=True)
                    last.then_inc(full(job), 1)

            def logits_of(t):
                pe.wait_ge(qk_t_ready, 2 * TILES)
                nk = (t + 1) * P
                for n in range(4):
                    job = ("logits", t, n)
                    wait_bank(pe, job)
                    for m, h in enumerate(pairs_of(n)):
                        rows = slice(64 * (h % 2), 64 * (h % 2) + 64)
                        last = mm(bank(job)[:, m * nk:(m + 1) * nk], lhsT=q_t[rows, h // 2, t * P:(t + 1) * P],
                                  rhs=k_t[rows, h // 2, 0:nk], start=True, stop=True)
                    last.then_inc(full(job), 1)

            def cb_and_xs(t):
                now = slice(t * P, (t + 1) * P)
                job = ("cb", t)
                wait_bank(pe, job)
                for g in range(GROUPS):
                    last = mm(bank(job)[:, g * P:(g + 1) * P], lhsT=xbc[:, 4 + g, now], rhs=xbc[:, 6 + g, now],
                              start=True, stop=True)
                last.then_inc(full(job), 1)
                transposes(("T_xs", t), [xbc[:, c, now] for c in range(4)])

            def transposed_probs(t):
                pe.wait_ge(probs_ready, t + 1)
                for n in range(2 * (t + 1)):
                    kb, half = n // 2, n % 2
                    transposes(("T_p", t, n), [logits[:, 4 * half + h, kb * P:(kb + 1) * P] for h in range(4)])

            def attend(t):
                job = ("pv", t)
                pe.wait_ge(probs_t_act, t * (t + 1) // 2 + t + 1)
                pe.wait_ge(probs_t_vec, t * (t + 1) // 2 + t + 1)
                pe.wait_ge(v_ready, t + 1)
                wait_bank(pe, job)
                for h in range(HEADS):
                    for kb in range(t + 1):
                        last = mm(bank(job)[:, h * HEAD_DIM:(h + 1) * HEAD_DIM], lhsT=probs_t[t][:, kb, h, :],
                                  rhs=v_sb[:, kb, h * HEAD_DIM:(h + 1) * HEAD_DIM], start=kb == 0, stop=kb == t)
                last.then_inc(full(job), 1)

            def y_diagonal(t):
                job = ("y_diag", t)
                pe.wait_ge(decay_masked, t + 1)
                pe.wait_ge(xdt_ready, t + 1)
                wait_bank(pe, job)
                for h in range(SSD_HEADS):
                    last = mm(bank(job)[:, h * 64:(h + 1) * 64], lhsT=decay[:, h, :], rhs=xdt[:, h, :],
                              start=True, stop=True)
                last.then_inc(full(job), 1)

            def transposed_attention(t):
                pe.wait_ge(attn_ready, t + 1)
                transposes(("T_attn", t), [attn[:, 2 * n:2 * n + 2, :].rearrange("p a b -> p (a b)") for n in range(4)])

            def transposed_y(t):
                pe.wait_ge(y_ready, t + 1)
                transposes(("T_y", t), [y_ssd[:, 2 * n:2 * n + 2, :].rearrange("p a b -> p (a b)") for n in range(4)])

            def project_out(t, half):
                job = ("out", t, half)
                pe.wait_ge(attn_t_ready, t + 1)
                pe.wait_ge(y_t_ready, t + 1)
                pe.wait_ge(w_in_sem[f"out{half}"], 16)
                wait_bank(pe, job)
                for k in range(KT):
                    last = mm(bank(job)[:, :], lhsT=mix_t[t][:, k, :], rhs=chunk(places[f"out{half}"])[:, k, :],
                              start=k == 0, stop=k == KT - 1)
                last.then_inc(full(job), 1)

            running_sums(0)
            logits_of(0)
            pe.wait_ge(w_in_sem["z"], 16)
            for t in range(TILES):
                project(("proj_z", t), "z", t)
            pe.wait_ge(silu_ready, CT)
            cb_and_xs(0)
            transposes(("T_b",), [xbc[:, 4 + g, 0:P] for g in range(GROUPS)])
            transposed_probs(0)
            logits_of(1)
            pe.wait_ge(w_in_sem["v"], 16)
            project(("proj_v", 0), "v", 0)
            y_diagonal(0)
            job = ("state",)
            pe.wait_ge(b_nat_ready, 1)
            wait_bank(pe, job)
            for g in range(GROUPS):
                heads = slice(g * GROUP_HEADS, (g + 1) * GROUP_HEADS)
                last = mm(bank(job)[:, g * 256:(g + 1) * 256], lhsT=b_nat[:, g, :],
                          rhs=xdt_end[:, heads, :].rearrange("p a b -> p (a b)"), start=True, stop=True)
            last.then_inc(full(job), 1)
            running_sums(1)
            attend(0)
            project(("proj_v", 1), "v", 1)
            transposed_y(0)
            transposed_attention(0)
            cb_and_xs(1)
            project_out(0, 0)
            transposed_probs(1)
            project_out(0, 1)
            job = ("y_off",)
            pe.wait_ge(state_ready, 1)
            wait_bank(pe, job)
            for g in range(GROUPS):
                last = mm(bank(job)[:, g * 256:(g + 1) * 256], lhsT=xbc[:, 6 + g, P:SEQ],
                          rhs=state_t[:, g * 256:(g + 1) * 256], start=True, stop=True)
            last.then_inc(full(job), 1)
            y_diagonal(1)
            attend(1)

            def transposed_h(t):
                for half in range(2):
                    pe.wait_ge(h_ready, 2 * t + half + 1)
                    transposes(("T_h", t, half), [x_sb[:, t, k * P:(k + 1) * P] for k in range(4 * half, 4 * half + 4)])
                pe.wait_ge(h_t_ready, 2 * (t + 1))

            def queries(t, c):
                job = ("peer_q", t, c)
                pe.wait_ge(w_in_sem[f"wq{c}"], 16)
                wait_bank(pe, job)
                for n in range(4):
                    for k in range(KT):
                        last = mm(bank(job)[:, n * P:(n + 1) * P], lhsT=chunk(places[f"wq{c}"])[:, k, n * P:(n + 1) * P],
                                  rhs=h_t[:, k, t * P:(t + 1) * P], start=k == 0, stop=k == KT - 1)
                last.then_inc(full(job), 1)

            def scores_of_keys(t):
                for c in range(4):
                    job = ("key_scores", t, c)
                    if t:
                        pe.wait_ge(peer_q_act, 2 + c + 1)
                    else:
                        pe.wait_ge(peer_q_act, c // 2 + 1)
                        if c:
                            pe.wait_ge(peer_q_vec, (c + 1) // 2)
                    wait_bank(pe, job)
                    for n in range(4):
                        last = mm(bank(job)[:, n * P:(n + 1) * P], lhsT=peer_q_t[:, 4 * c + n, :],
                                  rhs=keys_t[:, n % 2, :], start=True, stop=True)
                    last.then_inc(full(job), 1)

            transposed_h(0)
            queries(0, 0)
            queries(0, 1)
            transposed_y(1)
            queries(0, 2)
            transposed_attention(1)
            queries(0, 3)
            pe.wait_ge(consts_t_ready, 1)
            scores_of_keys(0)
            for half in range(2):
                project_out(1, half)
            transposed_h(1)
            for c in range(4):
                queries(1, c)
            scores_of_keys(1)

            for n in range(4):
                pe.wait_ge(bank_free[n], len([j for j in jobs.values() if j % PSUM_BANKS == n]))

            def sum_unit(u, parity, first=False):
                if not first:
                    pe.wait_ge(sum_taken, u)
                for j in range(SLOTS):
                    pe.wait_ge(diag_ready, u * SLOTS + j + 1)
                    for half in range(2):
                        at = j * SLOT + D_MODEL + half * 512
                        last = mm(banks[2 * parity + half][:, :], lhsT=diag[:, j % 8, :], rhs=arena[:, at:at + 512],
                                  start=j == 0, stop=j == SLOTS - 1, skip_group_check=True)
                    last.then_inc(slot_used, 1)

            sum_unit(0, 0, first=True)
            with pe.Fori(0, UNITS // 2 - 1) as i:
                sum_unit(2 * i + 1, 1)
                sum_unit(2 * i + 2, 0)
            sum_unit(UNITS - 1, 1)

        @block.scalar
        def _(act):
            for t in range(TILES):
                act.dma_start(pos_i[:, t:t + 1], positions[t * P:(t + 1) * P].rearrange("(p a) -> p a", a=1)).then_inc(small_in, 16)
            act.dma_start(freqs[:, :], cast_rows(inv_freq)).then_inc(small_in, 16)
            for n, source in enumerate((dt_bias, a_log, d_skip)):
                act.dma_start(heads_in[:, n * SSD_HEADS:(n + 1) * SSD_HEADS], cast_rows(source)).then_inc(small_in, 16)
            act.dma_start(keys_nat[:, 0, :], peer_k1).then_inc(keys_in, 16)
            act.dma_start(keys_nat[:, 1, :], peer_k2).then_inc(keys_in, 16)
            act.dma_start(conv_nat[0:CONV_WIDTH * CT, :], conv_w.rearrange("k (c p) -> (k c) p", p=P)).then_inc(keys_in, 16)
            act.dma_start(conv_nat[CONV_WIDTH * CT:(CONV_WIDTH + 1) * CT, :], conv_b.rearrange("(c p) -> c p", p=P)).then_inc(keys_in, 16)
            run = nc.scalar.activation

            def bank_view(job, *dims):
                if len(dims) == 2:
                    return bank(job)[:, 0:dims[0] * dims[1]].rearrange("p (a b) -> p a b", a=dims[0])
                return bank(job)[:, 0:dims[0]]

            act.wait_ge(turns_ready, 1)
            run(sin_cos[:, :], turns, ACT.Sin).then_inc(rope_ready, 1)
            for t in range(TILES):
                job = ("xT", t, 1)
                wait_job(act, job)
                run(x_t[:, 4:8, t * P:(t + 1) * P], bank_view(job, 4, P), ACT.Copy).then_inc(free(job), 1)
            act.wait_ge(free(("xT", 0, 1)), use(("xT", 0, 1)))
            act.wait_ge(free(("xT", 1, 1)), use(("xT", 1, 1)))
            act.sem_inc(act_step, 2)
            act.wait_ge(dt_arg_ready, 1)
            run(neg_a[:, :], heads_in[:, SSD_HEADS:2 * SSD_HEADS], ACT.Exp)
            run(dt_e[:, :], dt_e[:, :], ACT.Exp).then_inc(dt_exp_ready, 1)
            for t in range(TILES):
                job, now = ("T_idx", t), slice(t * P, (t + 1) * P)
                wait_job(act, job)
                run(iq_t[:, :, now], bank_view(job, 2, P), ACT.Copy)
                run(ik_t[:, now], bank(job)[:, 2 * P:3 * P], ACT.Copy).then_inc(idx_t_ready, 1)
                act.wait_ge(idx_t_ready, t + 1)
                act.sem_inc(free(job), 1)

            for t in range(TILES):
                nk = (t + 1) * P
                if t:
                    act.wait_ge(rel_used, t)
                for g in range(4):
                    job = ("idx_dot", t, g)
                    wait_job(act, job)
                    run(rel[:, g:8:4, 0:nk], bank_view(job, 2, nk), ACT.Relu, scale=IDX_DIM ** -0.5).then_inc(free(job), 1)
                    act.wait_ge(free(job), use(job))
                act.sem_inc(rel_ready, 1)

            def take_qk(s):
                for t in range(TILES):
                    job, now = ("T_qk", s, t), slice(t * P, (t + 1) * P)
                    wait_job(act, job)
                    run((q_t, k_t)[s][:, :, now], bank_view(job, 4, P), ACT.Copy).then_inc(free(job), 1)
                    act.wait_ge(free(job), use(job))
                    act.sem_inc(qk_t_ready, 1)

            for n in range(CT // 2):
                if n % 2 == 0:
                    take_qk(n // 2)
                if n == 0:
                    act.wait_ge(scratch_roped, 1)
                job = ("proj_xbc", n)
                wait_job(act, job)
                run(xbc_raw[:, 2 * n:2 * n + 2, CONV_WIDTH - 1:], bank_view(job, 2, SEQ), ACT.Copy).then_inc(free(job), 1)
                act.wait_ge(free(job), use(job))
                act.sem_inc(raw_ready, 1)
                if n:
                    for c in (2 * n - 2, 2 * n - 1):
                        act.wait_ge(conv_ready, c + 1)
                        run(xbc[:, c, :], xbc[:, c, :], ACT.Silu).then_inc(silu_ready, 1)
            for c in (CT - 2, CT - 1):
                act.wait_ge(conv_ready, c + 1)
                run(xbc[:, c, :], xbc[:, c, :], ACT.Silu).then_inc(silu_ready, 1)

            def take_v(t):
                job = ("proj_v", t)
                wait_job(act, job)
                run(v_sb[:, t, :], bank(job)[:, :], ACT.Copy).then_inc(free(job), 1)
                act.wait_ge(free(job), use(job))
                act.sem_inc(v_ready, 1)

            def exp_decay(t):
                act.wait_ge(decay_arg_ready, t + 1)
                if t == 0:
                    run(to_end[:, :], to_end[:, :], ACT.Exp)
                else:
                    run(exp_cum[:, :], cum[:, SSD_HEADS:], ACT.Exp)
                run(decay, decay, ACT.Exp).then_inc(decay_ready, 1)

            def exp_logits(t):
                nk = (t + 1) * P
                act.wait_ge(logits_ready, t + 1)
                for h in range(HEADS):
                    last = run(logits[:, h, 0:nk], logits[:, h, 0:nk], ACT.Exp, bias=row_max[:, h:h + 1],
                               accum_out=row_sum[:, t * HEADS + h:t * HEADS + h + 1])
                last.then_inc(probs_ready, 1)

            def take_probs(t):
                for n in range(0, 2 * (t + 1), 2):
                    job = ("T_p", t, n)
                    wait_job(act, job)
                    run(probs_t[t][:, n // 2, 0:4, :], bank_view(job, 4, P), ACT.Copy).then_inc(free(job), 1)
                    act.wait_ge(free(job), use(job))
                    act.sem_inc(probs_t_act, 1)

            def take_mixed(kind, first, signal, t):
                job = (kind, t)
                wait_job(act, job)
                run(mix_t[t][:, first:first + 4, :], bank_view(job, 4, P), ACT.Copy).then_inc(free(job), 1)
                act.wait_ge(free(job), use(job))
                act.sem_inc(signal, 1)

            def root_of_squares(t):
                act.wait_ge(rms_arg_ready, t + 1)
                run(rms[:, :], rms[:, :], ACT.Sqrt).then_inc(rms_ready, 1)

            def root_of_variance(t):
                act.wait_ge(var_ready, t + 1)
                run(rstd[:, :], rstd[:, :], ACT.Sqrt).then_inc(std_ready, 1)

            exp_decay(0)
            exp_logits(0)
            for t in range(TILES):
                job = ("proj_z", t)
                wait_job(act, job)
                run(z_silu[:, t, :], bank(job)[:, :], ACT.Silu).then_inc(free(job), 1)
                act.wait_ge(free(job), use(job))
                act.sem_inc(z_ready, 1)
            job = ("T_b",)
            wait_job(act, job)
            run(b_nat, bank_view(job, GROUPS, P), ACT.Copy).then_inc(free(job), 1)
            act.wait_ge(free(job), use(job))
            act.sem_inc(b_nat_ready, 1)
            take_probs(0)
            exp_logits(1)
            take_v(0)
            job = ("state",)
            wait_job(act, job)
            run(state_t, bank(job)[:, :], ACT.Copy).then_inc(free(job), 1)
            act.wait_ge(free(job), use(job))
            act.sem_inc(state_ready, 1)
            root_of_squares(0)
            exp_decay(1)
            take_v(1)
            take_mixed("T_y", 4, y_t_ready, 0)
            take_mixed("T_attn", 0, attn_t_ready, 0)
            take_probs(1)

            def take_h(t):
                for half in range(2):
                    job = ("T_h", t, half)
                    wait_job(act, job)
                    run(h_t[:, 4 * half:4 * half + 4, t * P:(t + 1) * P], bank_view(job, 4, P), ACT.Copy).then_inc(free(job), 1)
                    act.wait_ge(free(job), use(job))
                    act.sem_inc(h_t_ready, 1)

            def take_queries(t, c):
                job = ("peer_q", t, c)
                wait_job(act, job)
                run(peer_q_t[:, 4 * c:4 * c + 4, :], bank_view(job, 4, P), ACT.Copy).then_inc(free(job), 1)
                act.wait_ge(free(job), use(job))
                act.sem_inc(peer_q_act, 1)

            def take_scores(t):
                for c in range(4):
                    job = ("key_scores", t, c)
                    wait_job(act, job)
                    at = (t * PEER_HEADS + 2 * c) * 2 * N_KEYS
                    run(big[:, at:at + 512], bank(job)[:, :], ACT.Copy).then_inc(free(job), 1)
                    act.wait_ge(free(job), use(job))
                    act.sem_inc(scores_ready, 1)

            root_of_variance(0)
            take_h(0)
            root_of_squares(1)
            take_queries(0, 0)
            take_mixed("T_y", 4, y_t_ready, 1)
            take_queries(0, 2)
            take_mixed("T_attn", 0, attn_t_ready, 1)
            take_scores(0)
            exp_gate(act, 0)
            root_of_variance(1)
            take_h(1)
            wait_job(act, ("key_scores", 0, 3))
            for c in range(4):
                take_queries(1, c)
            take_scores(1)

            def weigh_unit(u, parity, first=False, last=False):
                if not last:
                    exp_gate(act, u + 1)
                for g, group in enumerate(slot_groups(last)):
                    part = slice(group[0], group[-1] + 1)
                    act.wait_ge(dots_ready, 4 * u + g + 1)
                    run(gelu[:, parity, part], dots[:, parity, part], ACT.Gelu).then_inc(gelu_ready, 1)
                    if g == 0:
                        act.wait_ge(gate_ready, u + 1)
                    act.wait_ge(gelu_ready, 4 * u + g + 1)
                    for j in group:
                        done = run(weight[:, parity, j:j + 1], gelu[:, parity, j:j + 1], ACT.Copy, scale=gate[:, parity, j:j + 1])
                    done.then_inc(weight_ready, 1)
                    act.wait_ge(weight_ready, 4 * u + g + 1)
                    for j in group:
                        if not first or j >= 8:
                            act.wait_ge(slot_used, u * SLOTS + j - 7)
                        run(diag[:, j % 8, :], ident[:, :], ACT.Copy, scale=weight[:, parity, j:j + 1]).then_inc(diag_ready, 1)

            weigh_unit(0, 0, first=True)
            with act.Fori(0, UNITS // 2 - 1) as i:
                weigh_unit(2 * i + 1, 1)
                weigh_unit(2 * i + 2, 0)
            root_of_variance(TILES)
            weigh_unit(UNITS - 1, 1, last=True)
            root_of_variance(2 * TILES - 1)

        @block.vector
        def _(dve):
            count = [0, 0]

            def link(ins):
                count[0] += 1
                ins.then_inc(vec_step, 1)
                dve.wait_ge(vec_step, count[1] + count[0])

            def link_to_search(ins):
                link(ins)
                dve.sem_inc(searches, 1)

            tt, ts, stt = nc.vector.tensor_tensor, nc.vector.tensor_scalar, nc.vector.scalar_tensor_tensor
            copy = nc.vector.tensor_copy

            def bank_view(job, *dims):
                n = int(np.prod(dims))
                flat = bank(job)[:, 0:n]
                if len(dims) == 2:
                    return flat.rearrange("p (a b) -> p a b", a=dims[0])
                if len(dims) == 3:
                    return flat.rearrange("p (a b c) -> p a b c", a=dims[0], b=dims[1])
                return flat

            dve.wait_ge(small_in, 6 * 16)
            link(copy(pos_f[:, :], pos_i[:, :]))
            half = TILES * HALF_FREQS
            for t in range(TILES):
                for s in range(2):
                    done = ts(sin_cos4[:, s, t, :], freqs[:, :], pos_f[:, t:t + 1], None, ALU.mult)
            link(done)
            for s in range(2):
                done = ts(turns[:, s * half:(s + 1) * half], sin_cos[:, s * half:(s + 1) * half], 1.0 / TWO_PI, 0.25 * s, ALU.mult, ALU.add)
            link(done)
            link(ts(turns, turns, ROUND_MAGIC, None, ALU.add))
            link(ts(turns, turns, ROUND_MAGIC, None, ALU.subtract))
            for part in (TWO_PI_HI, TWO_PI_MID, TWO_PI_LO):
                link(stt(sin_cos[:, :], turns, -part, sin_cos[:, :], ALU.mult, ALU.add))
            link(ts(sin_cos[:, half:], sin_cos[:, half:], float(np.pi / 2), None, ALU.add))
            ts(turns, sin_cos[:, :], SIN_LIMIT, -SIN_LIMIT, ALU.min, ALU.max).then_inc(turns_ready, 1)
            for t in range(TILES):
                job = ("xT", t, 0)
                wait_job(dve, job)
                link(copy(x_t[:, 0:4, t * P:(t + 1) * P], bank_view(job, 4, P)))
                dve.sem_inc(free(job), 1)
                dve.sem_inc(x_t_vec, 1)
            dve.wait_ge(rope_ready, 1)

            def rope(source, dest, heads, dim, t):
                first, n = (0, HEAD_DIM // 2) if dim == HEAD_DIM else (HEAD_DIM // 2, IDX_DIM // 2)
                sin, cos = (sin_cos4[:, s, t, first:first + n].unsqueeze(1).broadcast_to([P, 2 * heads, n]) for s in range(2))
                src = source.rearrange("p (h f) -> p h f", f=n)
                a, b = (r[:, 0:2 * heads * n].rearrange("p (h f) -> p h f", f=n) for r in (rope_a, rope_b))
                tt(a, src, cos, ALU.mult)
                link(tt(b, src, sin, ALU.mult))
                a4, b4 = (r[:, 0:2 * heads * n].rearrange("p (h s f) -> p h s f", s=2, f=n) for r in (rope_a, rope_b))
                d4 = dest.rearrange("p (h s f) -> p h s f", s=2, f=n)
                tt(d4[:, :, 0, :], a4[:, :, 0, :], b4[:, :, 1, :], ALU.subtract)
                return tt(d4[:, :, 1, :], a4[:, :, 1, :], b4[:, :, 0, :], ALU.add)

            IQ, IK = IDX_HEADS * IDX_DIM, IDX_DIM
            for t in range(TILES):
                job = ("proj_idx", t)
                wait_job(dve, job)
                if t:
                    wait_job(dve, ("T_idx", t - 1))
                link(rope(bank(job)[:, 0:IQ + IK], idx_nat[:, 0:IQ + IK], IDX_HEADS + 1, IDX_DIM, t))
                copy(idx_nat[:, IQ + IK:].rearrange("p (a b) -> p a b", a=3),
                     idx_nat[:, IQ:IQ + IK].unsqueeze(1).broadcast_to([P, 3, IK])).then_inc(idx_nat_ready, 1)
                ts(iw[:, t * IDX_HEADS:(t + 1) * IDX_HEADS], bank(job)[:, IQ + IK:IDX_COLS], IDX_HEADS ** -0.5, None, ALU.mult)
                link(tt(dt_x[:, t * SSD_HEADS:(t + 1) * SSD_HEADS], bank(job)[:, IDX_COLS:IDX_COLS + SSD_HEADS], heads_in[:, 0:SSD_HEADS], ALU.add))
                dve.sem_inc(free(job), 1)
            link(ts(dt_w[:, :], dt_x[:, :], -1.0, None, ALU.mult))
            tt(dt_e[:, :], dt_x[:, :], dt_w[:, :], ALU.min).then_inc(dt_arg_ready, 1)
            dve.wait_ge(dt_exp_ready, 1)
            link(ts(dt_w[:, :], dt_e[:, :], 2.0, None, ALU.add))
            link(nc.vector.reciprocal(dt_p[:, :], dt_w[:, :]))
            link(tt(dt_w[:, :], dt_e[:, :], dt_p[:, :], ALU.mult))
            link(tt(dt_w2[:, :], dt_w[:, :], dt_w[:, :], ALU.mult))
            link(ts(dt_p[:, :], dt_w2[:, :], 1.0 / 15.0, None, ALU.mult))
            for k in range(6, 0, -1):
                link(stt(dt_p[:, :], dt_p[:, :], 1.0 / (2 * k + 1), dt_w2[:, :], ALU.add, ALU.mult))
            link(stt(dt_p[:, :], dt_p[:, :], 1.0, dt_w[:, :], ALU.add, ALU.mult))
            link(ts(dt_x[:, :], dt_x[:, :], 0.0, None, ALU.max))
            link(stt(dt[:, :], dt_p[:, :], 2.0, dt_x[:, :], ALU.mult, ALU.add))
            link(ts(neg_a[:, :], neg_a[:, :], -1.0, None, ALU.mult))
            tt(dta[:, :].rearrange("p (t h) -> p t h", t=TILES), dt[:, :].rearrange("p (t h) -> p t h", t=TILES),
               neg_a[:, :].unsqueeze(1).broadcast_to([P, TILES, SSD_HEADS]), ALU.mult).then_inc(dta_ready, 1)

            def rope_qk(s, t):
                job = (("proj_q", "proj_k")[s], t)
                wait_job(dve, job)
                rope(bank(job)[:, :], qk_nat[t][:, s, :], HEADS, HEAD_DIM, t).then_inc(qk_nat_ready[s], 1)
                dve.wait_ge(qk_nat_ready[s], t + 1)
                dve.sem_inc(free(job), 1)

            def score_tile(t):
                nk = (t + 1) * P
                dve.wait_ge(rel_ready, t + 1)
                penalty = causal[:, SEQ - nk:]
                for h in range(IDX_HEADS):
                    before = penalty if h == 0 else score[:, 0:nk]
                    ins = stt(score[:, 0:nk], rel[:, h, 0:nk], iw[:, t * IDX_HEADS + h:t * IDX_HEADS + h + 1], before, ALU.mult, ALU.add)
                    if h < IDX_HEADS - 1:
                        link(ins)
                ins.then_inc(rel_used, 1)
                dve.wait_ge(rel_used, t + 1)
                for n in range(TOPK_KEYS // 8):
                    work = score if n == 0 else score_rest
                    link(nc.vector.max(top8[:, :], work[:, 0:nk]))
                    link(nc.vector.match_replace(score_rest[:, 0:nk], top8[:, :], work[:, 0:nk], TAKEN))
                link(ts(score[:, 0:nk], score_rest[:, 0:nk], TAKEN_BELOW, NOT_SELECTED, ALU.is_ge, ALU.mult))
                link(tt(select_bias[:, t, 0:nk], score[:, 0:nk], penalty, ALU.min))

            for t in range(TILES):
                rope_qk(0, t)
            rope_qk(1, 0)
            score_tile(0)
            rope_qk(1, 1)
            dve.sem_inc(scratch_roped, 1)
            link(nc.vector.memset(xbc_raw[:, :, 0:CONV_WIDTH - 1], 0.0))
            score_tile(1)
            job = ("consts",)
            wait_job(dve, job)
            copy(keys_t[:, :, :], bank_view(job, 2, P))
            copy(conv_t[:, :], bank(job)[:, 2 * P:2 * P + (CONV_WIDTH + 1) * CT]).then_inc(consts_t_ready, 1)
            dve.wait_ge(consts_t_ready, 1)
            dve.sem_inc(free(job), 1)
            for c in range(CT):
                if c % 2 == 0:
                    dve.wait_ge(raw_ready, c // 2 + 1)
                tap = lambda k: conv_t[:, k * CT + c:k * CT + c + 1]
                link(ts(xbc[:, c, :], xbc_raw[:, c, 0:SEQ], tap(0), tap(CONV_WIDTH), ALU.mult, ALU.add))
                for k in range(1, CONV_WIDTH):
                    ins = stt(xbc[:, c, :], xbc_raw[:, c, k:k + SEQ], tap(k), xbc[:, c, :], ALU.mult, ALU.add)
                    if k < CONV_WIDTH - 1:
                        link(ins)
                ins.then_inc(conv_ready, 1)

            def decay_argument(t):
                mine = slice(t * SSD_HEADS, (t + 1) * SSD_HEADS)
                job = ("cum_col", t)
                wait_job(dve, job)
                link(copy(cum[:, mine], bank(job)[:, 0:SSD_HEADS]))
                dve.sem_inc(free(job), 1)
                if t:
                    wait_job(dve, ("y_diag", t - 1))
                for half in range(2):
                    job = ("cum_row", t, half)
                    wait_job(dve, job)
                    if t == 0:
                        link(tt(to_end[:, 4 * half:4 * half + 4], bank(job)[:, P - 1:4 * P:P], cum[:, 4 * half:4 * half + 4], ALU.subtract))
                    for n in range(4):
                        h = 4 * half + n
                        ins = ts(decay[:, h, :], bank(job)[:, n * P:(n + 1) * P], cum[:, t * SSD_HEADS + h:t * SSD_HEADS + h + 1],
                                 0.0, ALU.subtract, ALU.min)
                    ins.then_inc(free(job), 1)
                    dve.wait_ge(free(job), use(job))
                dve.sem_inc(decay_arg_ready, 1)

            def take_logits(t):
                nk = (t + 1) * P
                if t:
                    wait_job(dve, ("T_p", t - 1, 2 * t - 1))
                for n in range(4):
                    job = ("logits", t, n)
                    wait_job(dve, job)
                    h = pairs_of(n)[0]
                    stt(logits[:, h:h + 3:2, 0:nk], bank_view(job, 2, nk), HEAD_DIM ** -0.5,
                        select_bias[:, t, 0:nk].unsqueeze(1).broadcast_to([P, 2, nk]), ALU.mult, ALU.add).then_inc(free(job), 1)
                    dve.wait_ge(free(job), use(job))
                link(nc.vector.tensor_reduce(row_max[:, :], logits[:, :, 0:nk], AX.X, ALU.max))
                ts(row_max[:, :], row_max[:, :], -1.0, None, ALU.mult).then_inc(logits_ready, 1)

            def source_side(t):
                job = ("cb", t)
                wait_job(dve, job)
                tt(cb_masked[:, :, :], bank_view(job, GROUPS, P), upper[:, :].unsqueeze(1).broadcast_to([P, GROUPS, P]),
                   ALU.mult).then_inc(free(job), 1)
                dve.wait_ge(free(job), use(job))
                job = ("T_xs", t)
                wait_job(dve, job)
                mine = slice(t * SSD_HEADS, (t + 1) * SSD_HEADS)
                copy(xs_nat, bank_view(job, SSD_HEADS, 64))
                link(tt(xdt, bank_view(job, SSD_HEADS, 64), dt[:, mine].unsqueeze(2).broadcast_to([P, SSD_HEADS, 64]), ALU.mult))
                dve.sem_inc(free(job), 1)
                dve.wait_ge(decay_ready, t + 1)
                if t == 0:
                    link(tt(xdt_end, xdt, to_end[:, :].unsqueeze(2).broadcast_to([P, SSD_HEADS, 64]), ALU.mult))
                dve.sem_inc(xdt_ready, 1)
                for g in range(GROUPS):
                    heads = slice(g * GROUP_HEADS, (g + 1) * GROUP_HEADS)
                    ins = tt(decay[:, heads, :], decay[:, heads, :], cb_masked[:, g, :].unsqueeze(1).broadcast_to([P, GROUP_HEADS, P]), ALU.mult)
                ins.then_inc(decay_masked, 1)

            def take_probs(t):
                for n in range(1, 2 * (t + 1), 2):
                    job = ("T_p", t, n)
                    wait_job(dve, job)
                    copy(probs_t[t][:, n // 2, 4:8, :], bank_view(job, 4, P)).then_inc(free(job), 1)
                    dve.wait_ge(free(job), use(job))
                    dve.sem_inc(probs_t_vec, 1)

            def take_attention(t):
                dve.wait_ge(probs_ready, t + 1)
                link(nc.vector.reciprocal(row_inv[:, :], row_sum[:, t * HEADS:(t + 1) * HEADS]))
                job = ("pv", t)
                wait_job(dve, job)
                if t:
                    wait_job(dve, ("T_attn", t - 1))
                tt(attn, bank_view(job, HEADS, HEAD_DIM), row_inv[:, :].unsqueeze(2).broadcast_to([P, HEADS, HEAD_DIM]),
                   ALU.mult).then_inc(free(job), 1)
                dve.wait_ge(free(job), use(job))
                dve.sem_inc(attn_ready, 1)

            def take_ssd(t):
                if t:
                    wait_job(dve, ("T_y", t - 1))
                dve.wait_ge(z_ready, t + 1)
                wide = lambda a: a.unsqueeze(2).broadcast_to([P, SSD_HEADS, 64])
                link(tt(y_ssd, xs_nat, wide(heads_in[:, 2 * SSD_HEADS:]), ALU.mult))
                if t:
                    job = ("y_off",)
                    wait_job(dve, job)
                    link(tt(xdt_end, bank_view(job, SSD_HEADS, 64), wide(exp_cum[:, :]), ALU.mult))
                    dve.sem_inc(free(job), 1)
                    link(tt(y_ssd, y_ssd, xdt_end, ALU.add))
                job = ("y_diag", t)
                wait_job(dve, job)
                link(tt(y_ssd, bank_view(job, SSD_HEADS, 64), y_ssd, ALU.add))
                dve.sem_inc(free(job), 1)
                flat = y_ssd.rearrange("p a b -> p (a b)")
                link(tt(flat, flat, z_silu[:, t, :], ALU.mult))
                for g in range(GROUPS):
                    part = flat[:, g * 256:(g + 1) * 256]
                    ins = stt(xdt.rearrange("p a b -> p (a b)")[:, g * 256:(g + 1) * 256], part, 1.0, part, ALU.mult, ALU.mult,
                              accum_out=squares[:, g:g + 1])
                link(ins)
                ts(rms[:, :], squares[:, :], 1.0 / 256, LN_EPS, ALU.mult, ALU.add).then_inc(rms_arg_ready, 1)
                dve.wait_ge(rms_ready, t + 1)
                link(nc.vector.reciprocal(rms[:, :], rms[:, :]))
                for g in range(GROUPS):
                    part = slice(g * 256, (g + 1) * 256)
                    ins = stt(flat[:, part], flat[:, part], rms[:, g:g + 1], norm_w[:, part], ALU.mult, ALU.mult)
                ins.then_inc(y_ready, 1)

            def layer_norm(t, n, done, add_half):
                for half in range(2):
                    part = slice(half * 512, (half + 1) * 512)
                    add_half(half, part)
                    ins = nc.vector.bn_stats(stats[:, 6 * half:6 * half + 6], x_sb[:, t, part])
                link(ins)
                link(nc.vector.bn_aggr(moments[:, :], stats[:, :]))
                ts(rstd[:, :], moments[:, 1:2], LN_EPS, None, ALU.add).then_inc(var_ready, 1)
                dve.wait_ge(std_ready, n + 1)
                link(nc.vector.reciprocal(rstd[:, :], rstd[:, :]))
                for half in range(2):
                    row, part = x_sb[:, t, half * 512:(half + 1) * 512], slice(half * 512, (half + 1) * 512)
                    link(stt(row, row, moments[:, 0:1], ln_gb[:, 0, part], ALU.subtract, ALU.mult))
                    stt(row, row, rstd[:, :], ln_gb[:, 1, part], ALU.mult, ALU.add).then_inc(done, 1)

            def mixer_norm(t):
                def add_half(half, part):
                    job = ("out", t, half)
                    wait_job(dve, job)
                    stt(x_sb[:, t, part], x_sb[:, t, part], ALPHA, bank(job)[:, :], ALU.mult, ALU.add).then_inc(free(job), 1)
                    dve.wait_ge(free(job), use(job))

                layer_norm(t, t, h_ready, add_half)

            decay_argument(0)
            take_logits(0)
            dve.wait_ge(ln1_in, 3 * 16)
            source_side(0)
            take_probs(0)
            take_logits(1)
            take_ssd(0)
            decay_argument(1)
            take_attention(0)
            source_side(1)
            take_probs(1)
            mixer_norm(0)
            take_ssd(1)
            take_attention(1)

            for c in (1, 3):
                job = ("peer_q", 0, c)
                wait_job(dve, job)
                copy(peer_q_t[:, 4 * c:4 * c + 4, :], bank_view(job, 4, P)).then_inc(free(job), 1)
                dve.wait_ge(free(job), use(job))
                dve.sem_inc(peer_q_vec, 1)

            def route(u, parity):
                link_to_search(copy(side_scores.rearrange("p a b -> p (a b)"), big[:, bass.ds(u * 2 * N_KEYS, 2 * N_KEYS)]))
                for s in range(2):
                    ins = nc.vector.max(top_v[:, s, 0:8], side_scores[:, s, :])
                link_to_search(ins)
                for s in range(2):
                    nc.vector.max_index(top_i[:, s, 0:8], top_v[:, s, 0:8], side_scores[:, s, :])
                for s in range(2):
                    ins = nc.vector.match_replace(side_rest[:, s, :], top_v[:, s, 0:8], side_scores[:, s, :], TAKEN)
                link_to_search(ins)
                for s in range(2):
                    ins = nc.vector.max(top_v[:, s, 8:16], side_rest[:, s, :])
                link_to_search(ins)
                for s in range(2):
                    nc.vector.max_index(top_i[:, s, 8:16], top_v[:, s, 8:16], side_rest[:, s, :])
                link(tt(cand, top_v[:, 0, :].unsqueeze(2).broadcast_to([P, 16, 16]),
                        top_v[:, 1, :].unsqueeze(1).broadcast_to([P, 16, 16]), ALU.add))
                flat = cand.rearrange("p a b -> p (a b)")
                copy(top_if[:, :, :], top_i[:, :, :])
                link_to_search(nc.vector.max(best[:, 0:8], flat))
                nc.vector.max_index(best_pos[:, 0:8], best[:, 0:8], flat)
                link_to_search(nc.vector.match_replace(cand_rest, best[:, 0:8], flat, TAKEN))
                link(nc.vector.max(best[:, 8:16], cand_rest))
                ts(neg_best[:, :], best[:, 0:1], -1.0, None, ALU.mult).then_inc(best_ready, 1)
                link(nc.vector.max_index(best_pos[:, 8:16], best[:, 8:16], cand_rest))
                nc.vector.tensor_single_scalar(pos_ij[:, 0, :], best_pos[:, :], 4, ALU.logical_shift_right)
                link(nc.vector.tensor_single_scalar(pos_ij[:, 1, :], best_pos[:, :], 15, ALU.bitwise_and))
                link(copy(pos_ijf[:, :, :], pos_ij[:, :, :]))
                oh = one_hot.rearrange("p s k c -> p (s k) c")
                link(tt(oh, pos_ijf[:, :, :].rearrange("p s k -> p (s k)").unsqueeze(2).broadcast_to([P, 32, 16]),
                        iota16[:, :].unsqueeze(1).broadcast_to([P, 32, 16]), ALU.is_equal))
                link(tt(one_hot, one_hot, top_if[:, :, :].unsqueeze(2).broadcast_to([P, 2, 16, 16]), ALU.mult))
                link(nc.vector.tensor_reduce(picked[:, :, :].rearrange("p s k -> p (s k)"), oh, AX.X, ALU.add))
                stt(expert[:, parity, :], picked[:, 0, :], float(N_KEYS), picked[:, 1, :], ALU.mult, ALU.add).then_inc(experts_ready, 1)

            def finish_gate(u, parity):
                dve.wait_ge(gate_exp_ready, u + 1)
                link(nc.vector.reciprocal(gate_sum[:, :], gate_sum[:, :]))
                ts(gate[:, parity, :], gate_e[:, :], gate_sum[:, :], None, ALU.mult).then_inc(gate_ready, 1)

            def take_sum(u, tile, parity):
                dve.wait_ge(slot_used, (u + 1) * SLOTS)
                for half in range(2):
                    where = mix[:, bass.ds(tile * D_MODEL + half * 512, 512)]
                    ins = tt(where, banks[2 * parity + half][:, :], where, ALU.add)
                ins.then_inc(sum_taken, 1)

            def add_experts(t):
                link(stt(x_sb[:, t, :], x_sb[:, t, :], ALPHA, ffn[:, t, :], ALU.mult, ALU.add))

            def dot_unit(u, tile, parity, former_tile=None, last=False):
                if not last:
                    route(u + 1, 1 - parity)
                for g, group in enumerate(slot_groups(last)):
                    for j in group:
                        dve.wait_ge(rows_in[j], 16 * (u + 1))
                        rows = arena[:, j * SLOT:j * SLOT + D_MODEL]
                        ins = stt(rows, x_rows[:, bass.ds(tile * D_MODEL, D_MODEL)], 1.0, rows,
                                  ALU.mult, ALU.mult, accum_out=dots[:, parity, j:j + 1])
                    ins.then_inc(dots_ready, 1)
                    if g == 0:
                        if former_tile is not None:
                            take_sum(u - 1, former_tile, 1 - parity)
                        if not last:
                            finish_gate(u + 1, 1 - parity)

            x_rows = x_sb[:, :, :].rearrange("p a b -> p (a b)")
            dve.wait_ge(scores_ready, 1)
            route(0, 0)
            finish_gate(0, 0)
            mixer_norm(1)
            dve.wait_ge(h_ready, 2 * TILES)
            dve.sem_inc(ln1_done, 1)
            dve.wait_ge(scores_ready, 4)
            before = count[0]
            dot_unit(0, 0, 0)
            per_unit = count[0] - before
            dve.wait_ge(scores_ready, 8)
            nc.vector.memset(mix[:, :], 0.0).then_inc(sum_taken, 1)
            dve.wait_ge(sum_taken, 1)
            with dve.Fori(0, UNITS // 2 - 1) as i:
                for n in (1, 2):
                    u = 2 * i + n
                    count[1] = i * 2 * per_unit
                    dot_unit(u, u // PEER_HEADS, n % 2, (u - 1) // PEER_HEADS)
            count[1] = (UNITS // 2 - 2) * 2 * per_unit
            dve.wait_ge(ln2_in, 32)
            add_experts(0)
            layer_norm(0, TILES, result_ready, lambda half, part: None)
            dot_unit(UNITS - 1, TILES - 1, 1, TILES - 1, last=True)
            dve.wait_ge(sum_taken, UNITS)
            add_experts(TILES - 1)
            dve.wait_ge(slot_used, UNITS * SLOTS)
            layer_norm(TILES - 1, 2 * TILES - 1, result_ready, lambda half, part: link(
                tt(x_sb[:, TILES - 1, part], banks[2 + half][:, :], x_sb[:, TILES - 1, part], ALU.add)))


def kernel(**inputs):
    import concourse.bacc as bacc
    from concourse.bass_utils import run_bass_kernel_spmd

    row = lambda name: np.ascontiguousarray(np.asarray(inputs[name])[0])
    freqs = lambda d: (np.float32(ROPE_THETA) ** (-np.arange(0, d, 2, dtype=np.float32) / np.float32(d))).astype(np.float32)
    arrays = {"x": row("x"), "positions": row("positions")}
    arrays["inv_freq"] = np.concatenate([freqs(HEAD_DIM), freqs(IDX_DIM)])
    for name in ("w_in", "conv_w", "conv_b", "dt_bias", "a_log", "d_skip", "ssm_norm_w", "w_out",
                 "ln1_g", "ln1_b", "peer_wq", "peer_k1", "peer_k2"):
        arrays[name] = row(name)
    arrays["expert_uv"] = np.concatenate([row("peer_u"), row("peer_v")], axis=1)
    arrays["ln2_g"], arrays["ln2_b"] = row("ln2_g"), row("ln2_b")

    nc = bacc.Bacc("TRN2", target_bir_lowering=False, num_devices=1)
    args = [nc.dram_tensor(f"in_{n}", a.shape, mybir.dt.from_np(a.dtype), kind="ExternalInput").ap() for n, a in arrays.items()]
    out = nc.dram_tensor("out", (SEQ, D_MODEL), mybir.dt.float32, kind="ExternalOutput").ap()
    build_layer(nc, *args, out)
    got = run_bass_kernel_spmd(nc, [{f"in_{n}": a for n, a in arrays.items()}], core_ids=[0])
    return got.results[0]["out"].reshape(1, SEQ, D_MODEL)
```

```python
from contextlib import ExitStack

import concourse.bass as bass
import numpy as np
from concourse import mybir

P = 128
D_MODEL, SEQ = 1024, 256
TILES = SEQ // P
KT = D_MODEL // P
HEADS, HEAD_DIM = 8, 64
ATTN_WIDTH = HEADS * HEAD_DIM
IDX_HEADS, IDX_DIM = 8, 32
TOPK_KEYS = min(256, SEQ // 4)
SSD_HEADS, SSD_WIDTH, GROUPS, CONV_WIDTH = 8, 512, 2, 4
GROUP_HEADS = SSD_HEADS // GROUPS
IDX_COLS = IDX_HEADS * IDX_DIM + IDX_DIM + IDX_HEADS
XBC_WIDTH = SSD_WIDTH + 2 * GROUPS * P
CT = XBC_WIDTH // P
Q0, K0, V0, I0 = 0, ATTN_WIDTH, 2 * ATTN_WIDTH, 3 * ATTN_WIDTH
Z0 = I0 + IDX_COLS
X0 = Z0 + SSD_WIDTH
DT0 = X0 + XBC_WIDTH
PEER_HEADS, N_KEYS, PEER_TOPK = 8, 128, 16
UNITS = TILES * PEER_HEADS
SLOTS = PEER_TOPK
ROPE_THETA, LN_EPS = 10000.0, 1e-5
ALPHA = 2.0 ** 0.25
TWO_PI = 2.0 * np.pi
TWO_PI_HI = 6.28125
TWO_PI_MID = float(np.float32(np.round((TWO_PI - TWO_PI_HI) * 2.0 ** 20) / 2.0 ** 20))
TWO_PI_LO = float(np.float32(TWO_PI - TWO_PI_HI - TWO_PI_MID))
ROUND_MAGIC = 1.5 * 2.0 ** 23
SIN_LIMIT = 3.1415925
NON_CAUSAL, TAKEN, TAKEN_BELOW, NOT_SELECTED = -3.0e38, -3.4e38, -3.2e38, -1.0e30
HALF_FREQS = HEAD_DIM // 2 + IDX_DIM // 2

PSUM_BANKS = 8


def psum_jobs():
    both = range(TILES)
    sums = [[("cum_col", t), ("cum_row", t, 0), ("cum_row", t, 1)] for t in both]
    idx_dots = [[("idx_dot", t, g) for g in range(4)] for t in both]
    logits = [[("logits", t, n) for n in range(4)] for t in both]
    jobs = [("proj_idx", t) for t in both] + [("proj_q", t) for t in both] + [("T_idx", t) for t in both]
    jobs += [("proj_k", 0)] + idx_dots[0] + [("proj_k", 1)] + idx_dots[1]
    jobs += [("T_qk", 0, 0), ("T_qk", 0, 1), ("proj_xbc", 0), ("consts",), ("proj_xbc", 1)]
    jobs += [("T_qk", 1, 0), ("T_qk", 1, 1), ("proj_xbc", 2), ("proj_xbc", 3)]
    jobs += sums[0] + logits[0] + [("proj_z", t) for t in both]
    jobs += [("cb", 0), ("T_xs", 0), ("T_b",), ("T_p", 0, 0), ("T_p", 0, 1)] + logits[1]
    jobs += [("proj_v", 0), ("y_diag", 0), ("state",), ("pv", 0)] + [("T_p", 1, n) for n in range(4)]
    jobs += [("T_y", 0), ("T_attn", 0)] + sums[1] + [("cb", 1), ("T_xs", 1)] + [("out", 0, half) for half in range(2)]
    jobs += [("proj_v", 1)] + [("T_h", 0, half) for half in range(2)] + [("y_off",), ("y_diag", 1), ("first_q",)]
    jobs += [("pv", 1), ("first_scores",), ("T_y", 1), ("T_attn", 1), ("peer_q", 0, 0)]
    jobs += [("out", 1, half) for half in range(2)] + [("key_scores", 0, 0), ("peer_q", 0, 1)] + [("T_h", 1, half) for half in range(2)]
    jobs += [("peer_q", 1, 0), ("key_scores", 0, 1), ("peer_q", 1, 1), ("key_scores", 1, 0), ("key_scores", 1, 1)]
    for c in (2, 3):
        jobs += [("peer_q", 0, c), ("key_scores", 0, c), ("peer_q", 1, c), ("key_scores", 1, c)]
    return jobs


def bank_plan():
    jobs = psum_jobs()
    shared_from = jobs.index(("peer_q", 1, 1))
    place, uses, filled = {}, {}, [0] * PSUM_BANKS
    for n, job in enumerate(jobs):
        place[job] = n % PSUM_BANKS if n < shared_from else 4 + n % 4
        filled[place[job]] += 1
        uses[job] = filled[place[job]]
    return place, uses, filled


def first_slots():
    first = list(range(12))
    return 3 * first + list(range(12, SLOTS)) + list(range(8))


def build_layer(nc, x, x_columns, positions, inv_freq, w_idx, w_in, conv_w, conv_b, dt_bias, a_log, d_skip, ssm_norm_w,
                w_out, ln1_g, ln1_b, peer_wq, peer_k1, peer_k2, expert_uv, ln2_g, ln2_b, out):
    f32, i32, u32 = mybir.dt.float32, mybir.dt.int32, mybir.dt.uint32
    ALU, ACT, AX = mybir.AluOpType, mybir.ActivationFunctionType, mybir.AxisListType

    job_bank, job_use, bank_uses = bank_plan()
    early = first_slots()
    EARLY_UNITS = len(early) // SLOTS
    LOOP_TURNS = (UNITS - 1 - EARLY_UNITS) // 2
    turn = [(j + early[-1] + 1) % SLOTS for j in range(SLOTS)]
    ctx = ExitStack()
    with ctx:
        def sb(name, words, dtype=f32):
            return ctx.enter_context(nc.sbuf_tensor(name, [P, words], dtype))

        def sem(name):
            return ctx.enter_context(nc.semaphore(name))

        CHUNK, SLOT = KT * 512, 2 * D_MODEL
        arena = sb("arena", SLOTS * SLOT)
        SCRATCH = 0

        def view(tensor, at, *dims):
            size = int(np.prod(dims))
            flat = tensor[:, at:at + size]
            if len(dims) == 2:
                return flat.rearrange("p (a b) -> p a b", a=dims[0])
            if len(dims) == 3:
                return flat.rearrange("p (a b c) -> p a b c", a=dims[0], b=dims[1])
            return flat

        def chunk(position, columns=512):
            return view(arena, position * CHUNK, KT, columns)

        logits = view(arena, SCRATCH, HEADS, SEQ)
        rel = logits
        RAW_LEN = SEQ + CONV_WIDTH - 1
        xbc_raw = view(arena, SCRATCH + 2048, CT, RAW_LEN)
        rope_a = view(arena, SCRATCH + 2048, 512)
        rope_b = view(arena, SCRATCH + 2560, 512)
        at = SCRATCH + 2048 + CT * RAW_LEN
        decay = view(arena, at, SSD_HEADS, P)
        turns = view(arena, at, 2 * TILES * HALF_FREQS)
        keys_nat = view(arena, at + 256, 2, P)
        conv_nat = view(arena, at + 512, P)
        idx_nat = view(arena, at + 640, TILES, 3 * P)
        xs_nat = view(arena, at + 1024, SSD_HEADS, 64)
        xdt = view(arena, at + 1536, SSD_HEADS, 64)
        xdt_end = view(arena, at + 2048, SSD_HEADS, 64)
        state_t = view(arena, at + 2560, SSD_WIDTH)
        y_ssd = view(arena, at + 3072, SSD_HEADS, 64)
        b_nat = view(arena, at + 3584, GROUPS, P)
        assert at + 3584 + GROUPS * P <= SCRATCH + 2 * CHUNK

        x_sb = ctx.enter_context(nc.sbuf_tensor("x_sb", [P, TILES, D_MODEL], f32))
        x_t = ctx.enter_context(nc.sbuf_tensor("x_t", [P, KT, SEQ], f32))
        h_t = x_t
        mix = sb("mix", KT * SEQ)
        peer_q_t = view(mix, D_MODEL, 2, 4, P)
        ffn = view(mix, 0, TILES, D_MODEL)
        big = sb("big", 4096)
        q_t, k_t, xbc = view(big, 0, 4, SEQ), view(big, 1024, 4, SEQ), view(big, 2048, CT, SEQ)
        mix_t = [view(mix, 0, KT, P), view(big, 2048, KT, P)]
        iq_t = ctx.enter_context(nc.sbuf_tensor("iq_t", [P, 2, SEQ], f32))
        ik_t = sb("ik_t", SEQ)
        mid = sb("mid", 3584)
        v_sb, z_silu = view(mid, 0, TILES, 512), view(mid, 1024, TILES, 512)
        qk_nat = [view(mid, 2048, 2, 512), view(mid, 1024, 2, 512)]
        attn = view(mid, 3072, HEADS, HEAD_DIM)
        probs_t = [view(mid, 2048, 1, HEADS, P), view(arena, SCRATCH + 2048, TILES, HEADS, P)]
        diag = view(mid, 1024, 8, P)
        cand, cand_rest = view(mid, 2048, 16, 16), view(mid, 2304, 256)
        side_scores, side_rest = view(mid, 2560, 2, N_KEYS), view(mid, 2816, 2, N_KEYS)
        one_hot = view(mid, 0, 2, 16, 16)
        ln_gb = ctx.enter_context(nc.sbuf_tensor("ln_gb", [P, 2, D_MODEL], f32))
        ident, upper = sb("ident", P), sb("upper", P)
        keys_t = ctx.enter_context(nc.sbuf_tensor("keys_t", [P, 2, P], f32))
        conv_t = sb("conv_t", (CONV_WIDTH + 1) * CT)
        cb_masked = ctx.enter_context(nc.sbuf_tensor("cb_masked", [P, GROUPS, P], f32))
        score, score_rest = sb("score", SEQ), sb("score_rest", SEQ)
        causal = sb("causal", SEQ)
        select_bias = ctx.enter_context(nc.sbuf_tensor("select_bias", [P, TILES, SEQ], f32))
        norm_w = sb("norm_w", SSD_WIDTH)
        sin_cos = sb("sin_cos", 2 * TILES * HALF_FREQS)
        sin_cos4 = sin_cos[:, :].rearrange("p (s t f) -> p s t f", s=2, t=TILES)
        freqs, pos_i, pos_f = sb("freqs", HALF_FREQS), sb("pos_i", TILES, i32), sb("pos_f", TILES)
        iw = sb("iw", TILES * IDX_HEADS)
        heads_in = sb("heads_in", 3 * SSD_HEADS)
        dt_x, dt_e = sb("dt_x", TILES * SSD_HEADS), sb("dt_e", TILES * SSD_HEADS)
        dt_w, dt_w2, dt_p = (sb(n, TILES * SSD_HEADS) for n in ("dt_w", "dt_w2", "dt_p"))
        dt, dta, cum = (sb(n, TILES * SSD_HEADS) for n in ("dt", "dta", "cum"))
        neg_a, to_end, exp_cum = sb("neg_a", SSD_HEADS), sb("to_end", SSD_HEADS), sb("exp_cum", SSD_HEADS)
        top8 = sb("top8", 8)
        row_max, row_sum, row_inv = sb("row_max", HEADS), sb("row_sum", TILES * HEADS), sb("row_inv", HEADS)
        squares, rms = sb("squares", GROUPS), sb("rms", GROUPS)
        stats, moments, rstd = sb("stats", 12), sb("moments", 2), sb("rstd", 1)
        top_v = ctx.enter_context(nc.sbuf_tensor("top_v", [P, 2, 16], f32))
        top_i = ctx.enter_context(nc.sbuf_tensor("top_i", [P, 2, 16], u32))
        top_if = ctx.enter_context(nc.sbuf_tensor("top_if", [P, 2, 16], f32))
        best, neg_best = sb("best", 16), sb("neg_best", 1)
        best_pos = sb("best_pos", 16, u32)
        pos_ij = ctx.enter_context(nc.sbuf_tensor("pos_ij", [P, 2, 16], u32))
        pos_ijf = ctx.enter_context(nc.sbuf_tensor("pos_ijf", [P, 2, 16], f32))
        picked = ctx.enter_context(nc.sbuf_tensor("picked", [P, 2, 16], f32))
        iota16 = sb("iota16", 16)
        expert = ctx.enter_context(nc.sbuf_tensor("expert", [P, 2, 16], i32))
        gate_e, gate_sum = sb("gate_e", 16), sb("gate_sum", 1)
        gate = ctx.enter_context(nc.sbuf_tensor("gate", [P, 2, 16], f32))
        dots = ctx.enter_context(nc.sbuf_tensor("dots", [P, 2, 16], f32))
        gelu = ctx.enter_context(nc.sbuf_tensor("gelu", [P, 2, 16], f32))
        weight = ctx.enter_context(nc.sbuf_tensor("weight", [P, 2, 16], f32))

        banks = [ctx.enter_context(nc.psum_tensor(f"bank{n}", [P, 512], f32)) for n in range(PSUM_BANKS)]

        bank_full = [sem(f"bank_full{n}") for n in range(PSUM_BANKS)]
        bank_free = [sem(f"bank_free{n}") for n in range(PSUM_BANKS)]
        x_in = sem("x_in")
        idx_in = [sem(f"x_t_and_idx_in{half}") for half in range(2)]
        w_names = ["idx", "q", "k", "xbc0", "xbc1", "z", "out1", "out0", "wq0", "wq1", "v", "wq3", "wq2"]
        w_in_sem = {n: sem(f"w_{n}_in") for n in w_names[1:]}
        small_in, keys_in, ln1_in, ln2_in = sem("small_in"), sem("keys_in"), sem("ln1_in"), sem("ln2_in")
        consts_ready, ident_step = sem("consts_ready"), sem("ident_step")
        vec_step, searches = sem("vec_step"), sem("searches")
        turns_ready, rope_ready = sem("turns_ready"), sem("rope_ready")
        dt_arg_ready, dt_exp_ready, dta_ready = sem("dt_arg_ready"), sem("dt_exp_ready"), sem("dta_ready")
        idx_nat_ready = sem("idx_nat_ready")
        qk_nat_ready = [sem("q_nat_ready"), sem("k_nat_ready")]
        scratch_roped = sem("scratch_roped")
        idx_t_ready, qk_t_ready, rel_ready, rel_used = (sem(n) for n in ("idx_t_ready", "qk_t_ready", "rel_ready", "rel_used"))
        z_ready, raw_ready, conv_ready, silu_ready, v_ready = (sem(n) for n in ("z_ready", "raw_ready", "conv_ready", "silu_ready", "v_ready"))
        consts_t_ready = sem("consts_t_ready")
        decay_arg_ready, decay_ready, decay_masked = (sem(n) for n in ("decay_arg_ready", "decay_ready", "decay_masked"))
        logits_ready, probs_ready, probs_t_act, probs_t_vec = (sem(n) for n in ("logits_ready", "probs_ready", "probs_t_act", "probs_t_vec"))
        b_nat_ready, xdt_ready, state_ready = (sem(n) for n in ("b_nat_ready", "xdt_ready", "state_ready"))
        attn_ready, attn_t_ready = sem("attn_ready"), sem("attn_t_ready")
        rms_arg_ready, rms_ready, y_ready, y_t_ready = (sem(n) for n in ("rms_arg_ready", "rms_ready", "y_ready", "y_t_ready"))
        var_ready, std_ready, h_ready, ln1_done = (sem(n) for n in ("var_ready", "std_ready", "h_ready", "ln1_done"))
        h_t_ready, peer_q_ready, scores_ready = (sem(n) for n in ("h_t_ready", "peer_q_ready", "scores_ready"))
        experts_ready, best_ready, gate_exp_ready, gate_ready = (sem(n) for n in ("experts_ready", "best_ready", "gate_exp_ready", "gate_ready"))
        rows_in = [sem(f"rows_in{j}") for j in range(SLOTS)]
        rows_asked = sem("rows_asked")
        dots_ready, gelu_ready, weight_ready, diag_ready = (sem(n) for n in ("dots_ready", "gelu_ready", "weight_ready", "diag_ready"))
        slot_used, half_summed, sum_taken = sem("slot_used"), sem("half_summed"), sem("sum_taken")
        result_ready, out_stored = sem("result_ready"), sem("out_stored")

        def bank(job):
            return banks[job_bank[job]]

        def use(job):
            return job_use[job]

        def wait_bank(pe, job):
            if use(job) > 1:
                pe.wait_ge(bank_free[job_bank[job]], use(job) - 1)

        def full(job):
            return bank_full[job_bank[job]]

        def free(job):
            return bank_free[job_bank[job]]

        def wait_job(engine, job):
            engine.wait_ge(full(job), use(job))

        def broadcast_rows(a):
            return a.partition_broadcast(P)

        places = {"idx": 3, "q": 2, "k": 4, "xbc0": 5, "xbc1": 6, "z": 7, "v": 6, "out0": 2, "out1": 3,
                  "wq0": 4, "wq1": 5, "wq2": 6, "wq3": 7}
        w_rows = w_in.rearrange("(k p) n -> p k n", p=P)
        w_out_rows = w_out.rearrange("(k p) n -> p k n", p=P)
        wq_rows = peer_wq.rearrange("(k p) n -> p k n", p=P)
        frees = {"out1": ("proj_idx", 1), "out0": ("proj_q", 1), "wq0": ("proj_k", 1), "wq1": ("proj_xbc", 1),
                 "v": ("proj_xbc", 3), "wq3": ("proj_z", 1), "wq2": ("proj_v", 1)}
        columns = {"q": Q0, "k": K0, "z": Z0, "xbc0": X0, "xbc1": X0 + 512, "v": V0}
        block = ctx.enter_context(nc.Block())

        def pairs_of(n):
            par, jj = n % 2, n // 2
            return par + 4 * jj, par + 4 * jj + 2

        query_order = [job[1:] for job in job_bank if job[0] == "peer_q"]
        score_order = [job[1:] for job in job_bank if job[0] == "key_scores"]

        def queries_taken(t, c):
            return query_order.index((t, c)) + 2

        def queries_of(t, c):
            return peer_q_t[:, query_order.index((t, c)) % 2, :, :]

        def slots_of(u):
            return early[u * SLOTS:(u + 1) * SLOTS] if isinstance(u, int) and u < EARLY_UNITS else turn

        def fills(u, j):
            slot = slots_of(u)[j]
            if isinstance(u, int) and u < EARLY_UNITS:
                return early[:u * SLOTS + j + 1].count(slot)
            return u - EARLY_UNITS + 1 + early.count(slot)

        def slot_groups(last):
            sizes = (4, 4, 2, 2, 1, 1, 1, 1) if last else (4, 4, 4, 4)
            ends = np.cumsum(sizes).tolist()
            return [range(end - size, end) for size, end in zip(sizes, ends)]

        def exp_gate(act, u):
            act.wait_ge(best_ready, u + 1)
            nc.scalar.activation(gate_e[:, :], best[:, :], ACT.Exp, bias=neg_best[:, :],
                                 accum_out=gate_sum[:, :]).then_inc(gate_exp_ready, 1)

        @block.sync
        def _(sp):
            for half in range(2):
                ks = slice(4 * half, 4 * half + 4)
                sp.dma_start(x_t[:, ks, :], x_columns.rearrange("(k p) n -> p k n", p=P)[:, ks, :]).then_inc(idx_in[half], 16)
                sp.dma_start(chunk(places["idx"], IDX_COLS + SSD_HEADS)[:, ks, :],
                             w_idx.rearrange("(k p) n -> p k n", p=P)[:, ks, :]).then_inc(idx_in[half], 16)
            for name in w_names[1:]:
                if name in frees:
                    wait_job(sp, frees[name])
                if name == "z":
                    sp.dma_start(x_sb[:, :, :], x.rearrange("(t p) n -> p t n", p=P)).then_inc(x_in, 16)
                    for place, source in ((norm_w[:, :], ssm_norm_w), (ln_gb[:, 0, :], ln1_g), (ln_gb[:, 1, :], ln1_b)):
                        sp.dma_start(place, broadcast_rows(source)).then_inc(ln1_in, 16)
                if name == "k":
                    sp.wait_ge(small_in, 6 * 16)
                    sp.wait_ge(keys_in, 4 * 16)
                if name in columns:
                    sp.dma_start(chunk(places[name]), w_rows[:, :, columns[name]:columns[name] + 512]).then_inc(w_in_sem[name], 16)
                else:
                    source = w_out_rows if name.startswith("out") else wq_rows
                    n = int(name[-1])
                    sp.dma_start(chunk(places[name]), source[:, :, n * 512:(n + 1) * 512]).then_inc(w_in_sem[name], 16)
            sp.wait_ge(ln1_done, 1)
            sp.dma_start(ln_gb[:, 0, :], broadcast_rows(ln2_g)).then_inc(ln2_in, 16)
            sp.dma_start(ln_gb[:, 1, :], broadcast_rows(ln2_b)).then_inc(ln2_in, 16)
            for t in range(TILES):
                for half in range(2):
                    part = slice(half * 512, (half + 1) * 512)
                    sp.wait_ge(result_ready, 2 * t + half + 1)
                    sp.dma_start(out[t * P:(t + 1) * P, part], x_sb[:, t, part]).then_inc(out_stored, 16)
            sp.wait_ge(out_stored, 2 * 16 * TILES)

        @block.gpsimd
        def _(pool):
            pool.memset(ident[:, :], 0.0).then_inc(ident_step, 1)
            pool.memset(upper[:, :], 1.0).then_inc(ident_step, 1)
            pool.memset(causal[:, :], 0.0).then_inc(ident_step, 1)
            pool.wait_ge(ident_step, 3)
            pool.affine_select(out=ident[:, :], in_=ident[:, :], compare_op=ALU.not_equal, fill=1.0, base=0,
                               pattern=[[-1, P]], channel_multiplier=1).then_inc(consts_ready, 1)
            pool.affine_select(out=upper[:, :], in_=upper[:, :], compare_op=ALU.is_ge, fill=0.0, base=0,
                               pattern=[[1, P]], channel_multiplier=-1).then_inc(consts_ready, 1)
            pool.affine_select(out=causal[:, P:SEQ], in_=causal[:, P:SEQ], compare_op=ALU.is_ge, fill=NON_CAUSAL, base=0,
                               pattern=[[-1, P]], channel_multiplier=1).then_inc(consts_ready, 1)
            pool.iota(iota16[:, :], pattern=[[1, 16]], base=0, channel_multiplier=0,
                      allow_small_or_imprecise_dtypes=True).then_inc(consts_ready, 1)

            last_readers = {0: ("T_y", 1), 2: ("pv", 1), 4: ("out", 1, 0), 6: ("out", 1, 1), 8: ("peer_q", 1, 0),
                            10: ("peer_q", 1, 1), 12: ("peer_q", 1, 2), 14: ("peer_q", 1, 3)}

            def gather_unit(u, parity):
                pool.wait_ge(experts_ready, u + 1)
                for j, slot in enumerate(slots_of(u)):
                    if isinstance(u, int) and u < EARLY_UNITS:
                        if j == 0:
                            pool.sem_inc(rows_asked, 1)
                        before = early[:u * SLOTS + j]
                        if slot in before:
                            pool.wait_ge(slot_used, len(before) - before[::-1].index(slot))
                        elif slot in last_readers:
                            wait_job(pool, last_readers[slot])
                    else:
                        pool.wait_ge(slot_used, (u - 1) * SLOTS + j + 1)
                        pool.sem_inc(rows_asked, 1)
                    pool.indirect_dma_start(
                        out=arena[:, slot * SLOT:(slot + 1) * SLOT], out_offset=None, in_=expert_uv,
                        in_offset=bass.IndirectOffsetOnAxis(ap=expert[:, parity, j:j + 1], axis=0),
                    ).then_inc(rows_in[slot], 16)

            for u in range(EARLY_UNITS):
                gather_unit(u, u % 2)
            with pool.Fori(0, LOOP_TURNS) as i:
                gather_unit(2 * i + EARLY_UNITS, EARLY_UNITS % 2)
                gather_unit(2 * i + EARLY_UNITS + 1, 1 - EARLY_UNITS % 2)
            gather_unit(UNITS - 1, 1)

        @block.tensor
        def _(pe):
            mm = nc.tensor.matmul

            def transposes(job, sources):
                wait_bank(pe, job)
                for n, source in enumerate(sources):
                    last = nc.tensor.transpose(bank(job)[:, n * P:(n + 1) * P], source, ident[:, :])
                last.then_inc(full(job), 1)

            def project(job, name, t, columns=512, start=True):
                wait_bank(pe, job)
                for k in range(KT):
                    if name == "idx" and k % 4 == 0:
                        pe.wait_ge(idx_in[k // 4], 32)
                    last = mm(bank(job)[:, 0:columns], lhsT=x_t[:, k, t * P:(t + 1) * P],
                              rhs=chunk(places[name], columns)[:, k, :], start=k == 0, stop=k == KT - 1)
                last.then_inc(full(job), 1)

            pe.wait_ge(consts_ready, 4)
            for t in range(TILES):
                project(("proj_idx", t), "idx", t, IDX_COLS + SSD_HEADS)
            pe.wait_ge(w_in_sem["q"], 16)
            for t in range(TILES):
                project(("proj_q", t), "q", t)
            for t in range(TILES):
                pe.wait_ge(idx_nat_ready, t + 1)
                transposes(("T_idx", t), [idx_nat[:, t, n * P:(n + 1) * P] for n in range(3)])

            def transposed_qk(s, t):
                pe.wait_ge(qk_nat_ready[s], t + 1)
                transposes(("T_qk", s, t), [qk_nat[t][:, s, n * P:(n + 1) * P] for n in range(4)])

            pe.wait_ge(w_in_sem["k"], 16)
            for t in range(TILES):
                project(("proj_k", t), "k", t)
                pe.wait_ge(idx_t_ready, t + 1)
                nk = (t + 1) * P
                for g in range(4):
                    job = ("idx_dot", t, g)
                    wait_bank(pe, job)
                    rows = slice(32 * g, 32 * g + 32)
                    for n in range(2):
                        last = mm(bank(job)[:, n * nk:(n + 1) * nk], lhsT=iq_t[rows, n, t * P:(t + 1) * P],
                                  rhs=ik_t[rows, 0:nk], start=True, stop=True)
                    last.then_inc(full(job), 1)
            for n in range(CT // 2):
                if n % 2 == 0:
                    for t in range(TILES):
                        transposed_qk(n // 2, t)
                    pe.wait_ge(w_in_sem[f"xbc{n // 2}"], 16)
                job, name = ("proj_xbc", n), f"xbc{n // 2}"
                wait_bank(pe, job)
                for c in range(2):
                    col = (2 * (n % 2) + c) * P
                    for k in range(KT):
                        last = mm(bank(job)[:, c * SEQ:(c + 1) * SEQ], lhsT=chunk(places[name])[:, k, col:col + P],
                                  rhs=x_t[:, k, :], start=k == 0, stop=k == KT - 1)
                last.then_inc(full(job), 1)
                if n == 0:
                    job = ("consts",)
                    pe.wait_ge(keys_in, 4 * 16)
                    wait_bank(pe, job)
                    for s in range(2):
                        nc.tensor.transpose(bank(job)[:, s * P:(s + 1) * P], keys_nat[:, s, :], ident[:, :])
                    rows = (CONV_WIDTH + 1) * CT
                    nc.tensor.transpose(bank(job)[:, 2 * P:2 * P + rows], conv_nat[0:rows, :], ident[0:rows, 0:rows]).then_inc(full(job), 1)
            pe.wait_ge(dta_ready, 1)

            def running_sums(t):
                job = ("cum_col", t)
                wait_bank(pe, job)
                mm(bank(job)[:, 0:SSD_HEADS], lhsT=upper[:, :], rhs=dta[:, t * SSD_HEADS:(t + 1) * SSD_HEADS],
                   start=True, stop=True).then_inc(full(job), 1)
                for half in range(2):
                    job = ("cum_row", t, half)
                    wait_bank(pe, job)
                    for n in range(4):
                        col = t * SSD_HEADS + 4 * half + n
                        last = mm(bank(job)[:, n * P:(n + 1) * P], lhsT=dta[:, col:col + 1].broadcast_to([P, P]),
                                  rhs=upper[:, :], start=True, stop=True)
                    last.then_inc(full(job), 1)

            def logits_of(t):
                pe.wait_ge(qk_t_ready, 2 * TILES)
                nk = (t + 1) * P
                for n in range(4):
                    job = ("logits", t, n)
                    wait_bank(pe, job)
                    for m, h in enumerate(pairs_of(n)):
                        rows = slice(64 * (h % 2), 64 * (h % 2) + 64)
                        last = mm(bank(job)[:, m * nk:(m + 1) * nk], lhsT=q_t[rows, h // 2, t * P:(t + 1) * P],
                                  rhs=k_t[rows, h // 2, 0:nk], start=True, stop=True)
                    last.then_inc(full(job), 1)

            def cb_and_xs(t):
                now = slice(t * P, (t + 1) * P)
                job = ("cb", t)
                wait_bank(pe, job)
                for g in range(GROUPS):
                    last = mm(bank(job)[:, g * P:(g + 1) * P], lhsT=xbc[:, 4 + g, now], rhs=xbc[:, 6 + g, now],
                              start=True, stop=True)
                last.then_inc(full(job), 1)
                transposes(("T_xs", t), [xbc[:, c, now] for c in range(4)])

            def transposed_probs(t):
                pe.wait_ge(probs_ready, t + 1)
                for n in range(2 * (t + 1)):
                    kb, half = n // 2, n % 2
                    transposes(("T_p", t, n), [logits[:, 4 * half + h, kb * P:(kb + 1) * P] for h in range(4)])

            def attend(t):
                job = ("pv", t)
                pe.wait_ge(probs_t_act, t * (t + 1) // 2 + t + 1)
                pe.wait_ge(probs_t_vec, t * (t + 1) // 2 + t + 1)
                pe.wait_ge(v_ready, t + 1)
                wait_bank(pe, job)
                for h in range(HEADS):
                    for kb in range(t + 1):
                        last = mm(bank(job)[:, h * HEAD_DIM:(h + 1) * HEAD_DIM], lhsT=probs_t[t][:, kb, h, :],
                                  rhs=v_sb[:, kb, h * HEAD_DIM:(h + 1) * HEAD_DIM], start=kb == 0, stop=kb == t)
                last.then_inc(full(job), 1)

            def y_diagonal(t):
                job = ("y_diag", t)
                pe.wait_ge(decay_masked, t + 1)
                pe.wait_ge(xdt_ready, t + 1)
                wait_bank(pe, job)
                for h in range(SSD_HEADS):
                    last = mm(bank(job)[:, h * 64:(h + 1) * 64], lhsT=decay[:, h, :], rhs=xdt[:, h, :],
                              start=True, stop=True)
                last.then_inc(full(job), 1)

            def transposed_attention(t):
                pe.wait_ge(attn_ready, t + 1)
                transposes(("T_attn", t), [attn[:, 2 * n:2 * n + 2, :].rearrange("p a b -> p (a b)") for n in range(4)])

            def transposed_y(t):
                pe.wait_ge(y_ready, t + 1)
                transposes(("T_y", t), [y_ssd[:, 2 * n:2 * n + 2, :].rearrange("p a b -> p (a b)") for n in range(4)])

            def project_out(t, half):
                job = ("out", t, half)
                pe.wait_ge(attn_t_ready, t + 1)
                pe.wait_ge(y_t_ready, t + 1)
                pe.wait_ge(w_in_sem[f"out{half}"], 16)
                wait_bank(pe, job)
                for k in range(KT):
                    last = mm(bank(job)[:, :], lhsT=mix_t[t][:, k, :], rhs=chunk(places[f"out{half}"])[:, k, :],
                              start=k == 0, stop=k == KT - 1)
                last.then_inc(full(job), 1)

            running_sums(0)
            logits_of(0)
            pe.wait_ge(w_in_sem["z"], 16)
            for t in range(TILES):
                project(("proj_z", t), "z", t)
            pe.wait_ge(silu_ready, CT)
            cb_and_xs(0)
            transposes(("T_b",), [xbc[:, 4 + g, 0:P] for g in range(GROUPS)])
            transposed_probs(0)
            logits_of(1)
            pe.wait_ge(w_in_sem["v"], 16)
            project(("proj_v", 0), "v", 0)
            y_diagonal(0)
            job = ("state",)
            pe.wait_ge(b_nat_ready, 1)
            wait_bank(pe, job)
            for g in range(GROUPS):
                heads = slice(g * GROUP_HEADS, (g + 1) * GROUP_HEADS)
                last = mm(bank(job)[:, g * 256:(g + 1) * 256], lhsT=b_nat[:, g, :],
                          rhs=xdt_end[:, heads, :].rearrange("p a b -> p (a b)"), start=True, stop=True)
            last.then_inc(full(job), 1)
            attend(0)
            transposed_probs(1)
            transposed_y(0)
            transposed_attention(0)
            running_sums(1)
            cb_and_xs(1)
            for half in range(2):
                project_out(0, half)
            project(("proj_v", 1), "v", 1)

            def transposed_h(t):
                for half in range(2):
                    pe.wait_ge(h_ready, 2 * t + half + 1)
                    transposes(("T_h", t, half), [x_sb[:, t, k * P:(k + 1) * P] for k in range(4 * half, 4 * half + 4)])

            def queries(job, t, c, blocks=range(4)):
                pe.wait_ge(w_in_sem[f"wq{c}"], 16)
                wait_bank(pe, job)
                for n in blocks:
                    for k in range(KT):
                        last = mm(bank(job)[:, n * P:(n + 1) * P], lhsT=chunk(places[f"wq{c}"])[:, k, n * P:(n + 1) * P],
                                  rhs=h_t[:, k, t * P:(t + 1) * P], start=k == 0, stop=k == KT - 1)
                last.then_inc(full(job), 1)

            def scores_of_keys(job, t, c, blocks=range(4)):
                pe.wait_ge(peer_q_ready, queries_taken(t, c) - (job == ("first_scores",)))
                wait_bank(pe, job)
                for n in blocks:
                    last = mm(bank(job)[:, n * P:(n + 1) * P], lhsT=queries_of(t, c)[:, n, :],
                              rhs=keys_t[:, n % 2, :], start=True, stop=True)
                last.then_inc(full(job), 1)

            def sum_slots(u, parity, some=range(SLOTS), last_unit=False):
                if some[0] == 0 and not (isinstance(u, int) and u == 0):
                    pe.wait_ge(sum_taken, u)
                for j in some:
                    pe.wait_ge(diag_ready, u * SLOTS + j + 1)
                    for half in range(2):
                        at = slots_of(u)[j] * SLOT + D_MODEL + half * 512
                        last = mm(banks[2 * parity + half][:, :], lhsT=diag[:, j % 8, :], rhs=arena[:, at:at + 512],
                                  start=j == 0, stop=j == SLOTS - 1, skip_group_check=True)
                        if last_unit and j == SLOTS - 1 and half == 0:
                            last.then_inc(half_summed, 1)
                    last.then_inc(slot_used, 1)

            pe.wait_ge(consts_t_ready, 1)
            transposed_h(0)
            job = ("y_off",)
            pe.wait_ge(state_ready, 1)
            wait_bank(pe, job)
            for g in range(GROUPS):
                last = mm(bank(job)[:, g * 256:(g + 1) * 256], lhsT=xbc[:, 6 + g, P:SEQ],
                          rhs=state_t[:, g * 256:(g + 1) * 256], start=True, stop=True)
            last.then_inc(full(job), 1)
            y_diagonal(1)
            pe.wait_ge(h_t_ready, 2)
            queries(("first_q",), 0, 0, range(2))
            attend(1)
            scores_of_keys(("first_scores",), 0, 0, range(2))
            transposed_y(1)
            transposed_attention(1)
            queries(("peer_q", 0, 0), 0, 0, range(2, 4))
            for half in range(2):
                project_out(1, half)
            scores_of_keys(("key_scores", 0, 0), 0, 0, range(2, 4))
            queries(("peer_q", 0, 1), 0, 1)
            transposed_h(1)
            pe.wait_ge(h_t_ready, 2 * TILES)
            queries(("peer_q", 1, 0), 1, 0)
            scores_of_keys(("key_scores", 0, 1), 0, 1)
            queries(("peer_q", 1, 1), 1, 1)
            scores_of_keys(("key_scores", 1, 0), 1, 0)
            for n in range(4):
                pe.wait_ge(bank_free[n], bank_uses[n])
            groups = slot_groups(False)
            sum_slots(0, 0, groups[0])
            scores_of_keys(("key_scores", 1, 1), 1, 1)
            sum_slots(0, 0, groups[1])
            queries(("peer_q", 0, 2), 0, 2)
            sum_slots(0, 0, groups[2])
            scores_of_keys(("key_scores", 0, 2), 0, 2)
            queries(("peer_q", 1, 2), 1, 2)
            sum_slots(0, 0, groups[3])
            scores_of_keys(("key_scores", 1, 2), 1, 2)
            sum_slots(1, 1, groups[0])
            queries(("peer_q", 0, 3), 0, 3)
            sum_slots(1, 1, groups[1])
            scores_of_keys(("key_scores", 0, 3), 0, 3)
            queries(("peer_q", 1, 3), 1, 3)
            sum_slots(1, 1, groups[2])
            scores_of_keys(("key_scores", 1, 3), 1, 3)
            sum_slots(1, 1, groups[3])
            for u in range(2, EARLY_UNITS):
                sum_slots(u, u % 2)
            with pe.Fori(0, LOOP_TURNS) as i:
                sum_slots(2 * i + EARLY_UNITS, EARLY_UNITS % 2)
                sum_slots(2 * i + EARLY_UNITS + 1, 1 - EARLY_UNITS % 2)
            sum_slots(UNITS - 1, 1, last_unit=True)

        @block.scalar
        def _(act):
            for t in range(TILES):
                act.dma_start(pos_i[:, t:t + 1], positions[t * P:(t + 1) * P].rearrange("(p a) -> p a", a=1)).then_inc(small_in, 16)
            act.dma_start(freqs[:, :], broadcast_rows(inv_freq)).then_inc(small_in, 16)
            for n, source in enumerate((dt_bias, a_log, d_skip)):
                act.dma_start(heads_in[:, n * SSD_HEADS:(n + 1) * SSD_HEADS], broadcast_rows(source)).then_inc(small_in, 16)
            act.dma_start(keys_nat[:, 0, :], peer_k1).then_inc(keys_in, 16)
            act.dma_start(keys_nat[:, 1, :], peer_k2).then_inc(keys_in, 16)
            act.dma_start(conv_nat[0:CONV_WIDTH * CT, :], conv_w.rearrange("k (c p) -> (k c) p", p=P)).then_inc(keys_in, 16)
            act.dma_start(conv_nat[CONV_WIDTH * CT:(CONV_WIDTH + 1) * CT, :], conv_b.rearrange("(c p) -> c p", p=P)).then_inc(keys_in, 16)
            run = nc.scalar.activation

            def bank_view(job, *dims):
                if len(dims) == 2:
                    return bank(job)[:, 0:dims[0] * dims[1]].rearrange("p (a b) -> p a b", a=dims[0])
                return bank(job)[:, 0:dims[0]]

            act.wait_ge(turns_ready, 1)
            run(sin_cos[:, :], turns, ACT.Sin).then_inc(rope_ready, 1)
            act.wait_ge(dt_arg_ready, 1)
            run(neg_a[:, :], heads_in[:, SSD_HEADS:2 * SSD_HEADS], ACT.Exp)
            run(dt_e[:, :], dt_e[:, :], ACT.Exp).then_inc(dt_exp_ready, 1)
            for t in range(TILES):
                job, now = ("T_idx", t), slice(t * P, (t + 1) * P)
                wait_job(act, job)
                run(iq_t[:, :, now], bank_view(job, 2, P), ACT.Copy)
                run(ik_t[:, now], bank(job)[:, 2 * P:3 * P], ACT.Copy).then_inc(idx_t_ready, 1)
                act.wait_ge(idx_t_ready, t + 1)
                act.sem_inc(free(job), 1)

            for t in range(TILES):
                nk = (t + 1) * P
                if t:
                    act.wait_ge(rel_used, t)
                for g in range(4):
                    job = ("idx_dot", t, g)
                    wait_job(act, job)
                    run(rel[:, g:8:4, 0:nk], bank_view(job, 2, nk), ACT.Relu, scale=IDX_DIM ** -0.5).then_inc(free(job), 1)
                    act.wait_ge(free(job), use(job))
                act.sem_inc(rel_ready, 1)

            def take_qk(s):
                for t in range(TILES):
                    job, now = ("T_qk", s, t), slice(t * P, (t + 1) * P)
                    wait_job(act, job)
                    run((q_t, k_t)[s][:, :, now], bank_view(job, 4, P), ACT.Copy).then_inc(free(job), 1)
                    act.wait_ge(free(job), use(job))
                    act.sem_inc(qk_t_ready, 1)

            for n in range(CT // 2):
                if n % 2 == 0:
                    take_qk(n // 2)
                if n == 0:
                    act.wait_ge(scratch_roped, 1)
                job = ("proj_xbc", n)
                wait_job(act, job)
                run(xbc_raw[:, 2 * n:2 * n + 2, CONV_WIDTH - 1:], bank_view(job, 2, SEQ), ACT.Copy).then_inc(free(job), 1)
                act.wait_ge(free(job), use(job))
                act.sem_inc(raw_ready, 1)
                if n:
                    for c in (2 * n - 2, 2 * n - 1):
                        act.wait_ge(conv_ready, c + 1)
                        run(xbc[:, c, :], xbc[:, c, :], ACT.Silu).then_inc(silu_ready, 1)
            for c in (CT - 2, CT - 1):
                act.wait_ge(conv_ready, c + 1)
                run(xbc[:, c, :], xbc[:, c, :], ACT.Silu).then_inc(silu_ready, 1)

            def take_v(t):
                job = ("proj_v", t)
                wait_job(act, job)
                run(v_sb[:, t, :], bank(job)[:, :], ACT.Copy).then_inc(free(job), 1)
                act.wait_ge(free(job), use(job))
                act.sem_inc(v_ready, 1)

            def exp_decay(t):
                act.wait_ge(decay_arg_ready, t + 1)
                if t == 0:
                    run(to_end[:, :], to_end[:, :], ACT.Exp)
                else:
                    run(exp_cum[:, :], cum[:, SSD_HEADS:], ACT.Exp)
                run(decay, decay, ACT.Exp).then_inc(decay_ready, 1)

            def exp_logits(t):
                nk = (t + 1) * P
                act.wait_ge(logits_ready, t + 1)
                for h in range(HEADS):
                    last = run(logits[:, h, 0:nk], logits[:, h, 0:nk], ACT.Exp, bias=row_max[:, h:h + 1],
                               accum_out=row_sum[:, t * HEADS + h:t * HEADS + h + 1])
                last.then_inc(probs_ready, 1)

            def take_probs(t):
                for n in range(0, 2 * (t + 1), 2):
                    job = ("T_p", t, n)
                    wait_job(act, job)
                    run(probs_t[t][:, n // 2, 0:4, :], bank_view(job, 4, P), ACT.Copy).then_inc(free(job), 1)
                    act.wait_ge(free(job), use(job))
                    act.sem_inc(probs_t_act, 1)

            def take_mixed(kind, first, signal, t):
                job = (kind, t)
                wait_job(act, job)
                run(mix_t[t][:, first:first + 4, :], bank_view(job, 4, P), ACT.Copy).then_inc(free(job), 1)
                act.wait_ge(free(job), use(job))
                act.sem_inc(signal, 1)

            def root_of_squares(t):
                act.wait_ge(rms_arg_ready, t + 1)
                run(rms[:, :], rms[:, :], ACT.Sqrt).then_inc(rms_ready, 1)

            def root_of_variance(t):
                act.wait_ge(var_ready, t + 1)
                run(rstd[:, :], rstd[:, :], ACT.Sqrt).then_inc(std_ready, 1)

            exp_decay(0)
            exp_logits(0)
            for t in range(TILES):
                job = ("proj_z", t)
                wait_job(act, job)
                run(z_silu[:, t, :], bank(job)[:, :], ACT.Silu).then_inc(free(job), 1)
                act.wait_ge(free(job), use(job))
                act.sem_inc(z_ready, 1)
            job = ("T_b",)
            wait_job(act, job)
            run(b_nat, bank_view(job, GROUPS, P), ACT.Copy).then_inc(free(job), 1)
            act.wait_ge(free(job), use(job))
            act.sem_inc(b_nat_ready, 1)
            take_probs(0)
            exp_logits(1)
            take_v(0)
            job = ("state",)
            wait_job(act, job)
            run(state_t, bank(job)[:, :], ACT.Copy).then_inc(free(job), 1)
            act.wait_ge(free(job), use(job))
            act.sem_inc(state_ready, 1)
            root_of_squares(0)
            take_probs(1)
            take_mixed("T_y", 4, y_t_ready, 0)
            take_mixed("T_attn", 0, attn_t_ready, 0)
            exp_decay(1)

            def take_h(t):
                for half in range(2):
                    job = ("T_h", t, half)
                    wait_job(act, job)
                    run(h_t[:, 4 * half:4 * half + 4, t * P:(t + 1) * P], bank_view(job, 4, P), ACT.Copy).then_inc(free(job), 1)
                    act.wait_ge(free(job), use(job))
                    act.sem_inc(h_t_ready, 1)

            def take_queries(job, t, c, first=0, last=4):
                n = query_order.index((t, c))
                if n >= 2:
                    wait_job(act, ("key_scores", *query_order[n - 2]))
                wait_job(act, job)
                run(queries_of(t, c)[:, first:last, :], bank(job)[:, first * P:last * P].rearrange("p (a b) -> p a b", b=P),
                    ACT.Copy).then_inc(free(job), 1)
                act.wait_ge(free(job), use(job))
                act.sem_inc(peer_q_ready, 1)

            def take_scores(job, t, c, first=0, last=4):
                wait_job(act, job)
                at = (t * PEER_HEADS + 2 * c) * 2 * N_KEYS
                run(big[:, at + first * N_KEYS:at + last * N_KEYS], bank(job)[:, first * N_KEYS:last * N_KEYS],
                    ACT.Copy).then_inc(free(job), 1)
                act.wait_ge(free(job), use(job))
                act.sem_inc(scores_ready, 1)

            def weigh_slots(u, parity, g, group):
                part = slice(group[0], group[-1] + 1)
                act.wait_ge(dots_ready, 4 * u + g + 1)
                run(gelu[:, parity, part], dots[:, parity, part], ACT.Gelu).then_inc(gelu_ready, 1)
                if g == 0:
                    act.wait_ge(gate_ready, u + 1)
                act.wait_ge(gelu_ready, 4 * u + g + 1)
                for j in group:
                    done = run(weight[:, parity, j:j + 1], gelu[:, parity, j:j + 1], ACT.Copy, scale=gate[:, parity, j:j + 1])
                done.then_inc(weight_ready, 1)
                act.wait_ge(weight_ready, 4 * u + g + 1)
                for j in group:
                    if not (isinstance(u, int) and u == 0) or j >= 8:
                        act.wait_ge(slot_used, u * SLOTS + j - 7)
                    run(diag[:, j % 8, :], ident[:, :], ACT.Copy, scale=weight[:, parity, j:j + 1]).then_inc(diag_ready, 1)

            def weigh_unit(u, parity, last=False):
                if not last:
                    exp_gate(act, u + 1)
                for g, group in enumerate(slot_groups(last)):
                    weigh_slots(u, parity, g, group)

            root_of_variance(0)
            take_v(1)
            take_h(0)
            root_of_squares(1)
            take_queries(("first_q",), 0, 0, 0, 2)
            take_scores(("first_scores",), 0, 0, 0, 2)
            take_mixed("T_y", 4, y_t_ready, 1)
            take_mixed("T_attn", 0, attn_t_ready, 1)
            take_queries(("peer_q", 0, 0), 0, 0, 2, 4)
            exp_gate(act, 0)
            root_of_variance(1)
            take_scores(("key_scores", 0, 0), 0, 0, 2, 4)
            take_queries(("peer_q", 0, 1), 0, 1)
            take_h(1)
            take_queries(("peer_q", 1, 0), 1, 0)
            take_scores(("key_scores", 0, 1), 0, 1)
            groups = slot_groups(False)
            weigh_slots(0, 0, 0, groups[0])
            exp_gate(act, 1)
            take_queries(("peer_q", 1, 1), 1, 1)
            take_scores(("key_scores", 1, 0), 1, 0)
            weigh_slots(0, 0, 1, groups[1])
            take_scores(("key_scores", 1, 1), 1, 1)
            weigh_slots(0, 0, 2, groups[2])
            take_queries(("peer_q", 0, 2), 0, 2)
            take_scores(("key_scores", 0, 2), 0, 2)
            weigh_slots(0, 0, 3, groups[3])
            take_queries(("peer_q", 1, 2), 1, 2)
            exp_gate(act, 2)
            weigh_slots(1, 1, 0, groups[0])
            take_scores(("key_scores", 1, 2), 1, 2)
            weigh_slots(1, 1, 1, groups[1])
            take_queries(("peer_q", 0, 3), 0, 3)
            take_scores(("key_scores", 0, 3), 0, 3)
            weigh_slots(1, 1, 2, groups[2])
            take_queries(("peer_q", 1, 3), 1, 3)
            take_scores(("key_scores", 1, 3), 1, 3)
            weigh_slots(1, 1, 3, groups[3])
            for u in range(2, EARLY_UNITS):
                weigh_unit(u, u % 2)
            with act.Fori(0, LOOP_TURNS) as i:
                weigh_unit(2 * i + EARLY_UNITS, EARLY_UNITS % 2)
                weigh_unit(2 * i + EARLY_UNITS + 1, 1 - EARLY_UNITS % 2)
            root_of_variance(TILES)
            weigh_unit(UNITS - 1, 1, last=True)
            root_of_variance(2 * TILES - 1)

        @block.vector
        def _(dve):
            count = [0, 0]

            def link(ins):
                count[0] += 1
                ins.then_inc(vec_step, 1)
                dve.wait_ge(vec_step, count[1] + count[0])

            def link_to_search(ins):
                link(ins)
                dve.sem_inc(searches, 1)

            tt, ts, stt = nc.vector.tensor_tensor, nc.vector.tensor_scalar, nc.vector.scalar_tensor_tensor
            copy = nc.vector.tensor_copy

            def bank_view(job, *dims):
                n = int(np.prod(dims))
                flat = bank(job)[:, 0:n]
                if len(dims) == 2:
                    return flat.rearrange("p (a b) -> p a b", a=dims[0])
                if len(dims) == 3:
                    return flat.rearrange("p (a b c) -> p a b c", a=dims[0], b=dims[1])
                return flat

            dve.wait_ge(small_in, 6 * 16)
            link(copy(pos_f[:, :], pos_i[:, :]))
            half = TILES * HALF_FREQS
            for t in range(TILES):
                for s in range(2):
                    done = ts(sin_cos4[:, s, t, :], freqs[:, :], pos_f[:, t:t + 1], None, ALU.mult)
            link(done)
            for s in range(2):
                done = ts(turns[:, s * half:(s + 1) * half], sin_cos[:, s * half:(s + 1) * half], 1.0 / TWO_PI, 0.25 * s, ALU.mult, ALU.add)
            link(done)
            link(ts(turns, turns, ROUND_MAGIC, None, ALU.add))
            link(ts(turns, turns, ROUND_MAGIC, None, ALU.subtract))
            for part in (TWO_PI_HI, TWO_PI_MID, TWO_PI_LO):
                link(stt(sin_cos[:, :], turns, -part, sin_cos[:, :], ALU.mult, ALU.add))
            link(ts(sin_cos[:, half:], sin_cos[:, half:], float(np.pi / 2), None, ALU.add))
            ts(turns, sin_cos[:, :], SIN_LIMIT, -SIN_LIMIT, ALU.min, ALU.max).then_inc(turns_ready, 1)
            dve.wait_ge(rope_ready, 1)

            def rope(source, dest, heads, dim, t):
                first, n = (0, HEAD_DIM // 2) if dim == HEAD_DIM else (HEAD_DIM // 2, IDX_DIM // 2)
                sin, cos = (sin_cos4[:, s, t, first:first + n].unsqueeze(1).broadcast_to([P, 2 * heads, n]) for s in range(2))
                src = source.rearrange("p (h f) -> p h f", f=n)
                a, b = (r[:, 0:2 * heads * n].rearrange("p (h f) -> p h f", f=n) for r in (rope_a, rope_b))
                tt(a, src, cos, ALU.mult)
                link(tt(b, src, sin, ALU.mult))
                a4, b4 = (r[:, 0:2 * heads * n].rearrange("p (h s f) -> p h s f", s=2, f=n) for r in (rope_a, rope_b))
                d4 = dest.rearrange("p (h s f) -> p h s f", s=2, f=n)
                tt(d4[:, :, 0, :], a4[:, :, 0, :], b4[:, :, 1, :], ALU.subtract)
                return tt(d4[:, :, 1, :], a4[:, :, 1, :], b4[:, :, 0, :], ALU.add)

            IQ, IK = IDX_HEADS * IDX_DIM, IDX_DIM
            for t in range(TILES):
                job = ("proj_idx", t)
                wait_job(dve, job)
                link(rope(bank(job)[:, 0:IQ + IK], idx_nat[:, t, 0:IQ + IK], IDX_HEADS + 1, IDX_DIM, t))
                copy(idx_nat[:, t, IQ + IK:].rearrange("p (a b) -> p a b", a=3),
                     idx_nat[:, t, IQ:IQ + IK].unsqueeze(1).broadcast_to([P, 3, IK])).then_inc(idx_nat_ready, 1)
                ts(iw[:, t * IDX_HEADS:(t + 1) * IDX_HEADS], bank(job)[:, IQ + IK:IDX_COLS], IDX_HEADS ** -0.5, None, ALU.mult)
                link(tt(dt_x[:, t * SSD_HEADS:(t + 1) * SSD_HEADS], bank(job)[:, IDX_COLS:IDX_COLS + SSD_HEADS], heads_in[:, 0:SSD_HEADS], ALU.add))
                dve.sem_inc(free(job), 1)
            link(ts(dt_w[:, :], dt_x[:, :], -1.0, None, ALU.mult))
            tt(dt_e[:, :], dt_x[:, :], dt_w[:, :], ALU.min).then_inc(dt_arg_ready, 1)
            dve.wait_ge(dt_exp_ready, 1)
            link(ts(dt_w[:, :], dt_e[:, :], 2.0, None, ALU.add))
            link(nc.vector.reciprocal(dt_p[:, :], dt_w[:, :]))
            link(tt(dt_w[:, :], dt_e[:, :], dt_p[:, :], ALU.mult))
            link(tt(dt_w2[:, :], dt_w[:, :], dt_w[:, :], ALU.mult))
            link(ts(dt_p[:, :], dt_w2[:, :], 1.0 / 15.0, None, ALU.mult))
            for k in range(6, 0, -1):
                link(stt(dt_p[:, :], dt_p[:, :], 1.0 / (2 * k + 1), dt_w2[:, :], ALU.add, ALU.mult))
            link(stt(dt_p[:, :], dt_p[:, :], 1.0, dt_w[:, :], ALU.add, ALU.mult))
            link(ts(dt_x[:, :], dt_x[:, :], 0.0, None, ALU.max))
            link(stt(dt[:, :], dt_p[:, :], 2.0, dt_x[:, :], ALU.mult, ALU.add))
            link(ts(neg_a[:, :], neg_a[:, :], -1.0, None, ALU.mult))
            tt(dta[:, :].rearrange("p (t h) -> p t h", t=TILES), dt[:, :].rearrange("p (t h) -> p t h", t=TILES),
               neg_a[:, :].unsqueeze(1).broadcast_to([P, TILES, SSD_HEADS]), ALU.mult).then_inc(dta_ready, 1)

            def rope_qk(s, t):
                job = (("proj_q", "proj_k")[s], t)
                wait_job(dve, job)
                rope(bank(job)[:, :], qk_nat[t][:, s, :], HEADS, HEAD_DIM, t).then_inc(qk_nat_ready[s], 1)
                dve.wait_ge(qk_nat_ready[s], t + 1)
                dve.sem_inc(free(job), 1)

            def score_tile(t):
                nk = (t + 1) * P
                dve.wait_ge(rel_ready, t + 1)
                penalty = causal[:, SEQ - nk:]
                for h in range(IDX_HEADS):
                    before = penalty if h == 0 else score[:, 0:nk]
                    ins = stt(score[:, 0:nk], rel[:, h, 0:nk], iw[:, t * IDX_HEADS + h:t * IDX_HEADS + h + 1], before, ALU.mult, ALU.add)
                    if h < IDX_HEADS - 1:
                        link(ins)
                ins.then_inc(rel_used, 1)
                dve.wait_ge(rel_used, t + 1)
                for n in range(TOPK_KEYS // 8):
                    work = score if n == 0 else score_rest
                    link(nc.vector.max(top8[:, :], work[:, 0:nk]))
                    link(nc.vector.match_replace(score_rest[:, 0:nk], top8[:, :], work[:, 0:nk], TAKEN))
                link(ts(score[:, 0:nk], score_rest[:, 0:nk], TAKEN_BELOW, NOT_SELECTED, ALU.is_ge, ALU.mult))
                link(tt(select_bias[:, t, 0:nk], score[:, 0:nk], penalty, ALU.min))

            for t in range(TILES):
                rope_qk(0, t)
            rope_qk(1, 0)
            score_tile(0)
            rope_qk(1, 1)
            dve.sem_inc(scratch_roped, 1)
            link(nc.vector.memset(xbc_raw[:, :, 0:CONV_WIDTH - 1], 0.0))
            score_tile(1)
            job = ("consts",)
            wait_job(dve, job)
            copy(keys_t[:, :, :], bank_view(job, 2, P))
            copy(conv_t[:, :], bank(job)[:, 2 * P:2 * P + (CONV_WIDTH + 1) * CT]).then_inc(consts_t_ready, 1)
            dve.wait_ge(consts_t_ready, 1)
            dve.sem_inc(free(job), 1)
            for c in range(CT):
                if c % 2 == 0:
                    dve.wait_ge(raw_ready, c // 2 + 1)
                tap = lambda k: conv_t[:, k * CT + c:k * CT + c + 1]
                link(ts(xbc[:, c, :], xbc_raw[:, c, 0:SEQ], tap(0), tap(CONV_WIDTH), ALU.mult, ALU.add))
                for k in range(1, CONV_WIDTH):
                    ins = stt(xbc[:, c, :], xbc_raw[:, c, k:k + SEQ], tap(k), xbc[:, c, :], ALU.mult, ALU.add)
                    if k < CONV_WIDTH - 1:
                        link(ins)
                ins.then_inc(conv_ready, 1)

            def decay_argument(t):
                mine = slice(t * SSD_HEADS, (t + 1) * SSD_HEADS)
                job = ("cum_col", t)
                wait_job(dve, job)
                link(copy(cum[:, mine], bank(job)[:, 0:SSD_HEADS]))
                dve.sem_inc(free(job), 1)
                if t:
                    wait_job(dve, ("y_diag", t - 1))
                for half in range(2):
                    job = ("cum_row", t, half)
                    wait_job(dve, job)
                    if t == 0:
                        link(tt(to_end[:, 4 * half:4 * half + 4], bank(job)[:, P - 1:4 * P:P], cum[:, 4 * half:4 * half + 4], ALU.subtract))
                    for n in range(4):
                        h = 4 * half + n
                        ins = ts(decay[:, h, :], bank(job)[:, n * P:(n + 1) * P], cum[:, t * SSD_HEADS + h:t * SSD_HEADS + h + 1],
                                 0.0, ALU.subtract, ALU.min)
                    ins.then_inc(free(job), 1)
                    dve.wait_ge(free(job), use(job))
                dve.sem_inc(decay_arg_ready, 1)

            def take_logits(t):
                nk = (t + 1) * P
                if t:
                    wait_job(dve, ("T_p", t - 1, 2 * t - 1))
                for n in range(4):
                    job = ("logits", t, n)
                    wait_job(dve, job)
                    h = pairs_of(n)[0]
                    stt(logits[:, h:h + 3:2, 0:nk], bank_view(job, 2, nk), HEAD_DIM ** -0.5,
                        select_bias[:, t, 0:nk].unsqueeze(1).broadcast_to([P, 2, nk]), ALU.mult, ALU.add).then_inc(free(job), 1)
                    dve.wait_ge(free(job), use(job))
                link(nc.vector.tensor_reduce(row_max[:, :], logits[:, :, 0:nk], AX.X, ALU.max))
                ts(row_max[:, :], row_max[:, :], -1.0, None, ALU.mult).then_inc(logits_ready, 1)

            def source_side(t):
                job = ("cb", t)
                wait_job(dve, job)
                tt(cb_masked[:, :, :], bank_view(job, GROUPS, P), upper[:, :].unsqueeze(1).broadcast_to([P, GROUPS, P]),
                   ALU.mult).then_inc(free(job), 1)
                dve.wait_ge(free(job), use(job))
                job = ("T_xs", t)
                wait_job(dve, job)
                mine = slice(t * SSD_HEADS, (t + 1) * SSD_HEADS)
                copy(xs_nat, bank_view(job, SSD_HEADS, 64))
                link(tt(xdt, bank_view(job, SSD_HEADS, 64), dt[:, mine].unsqueeze(2).broadcast_to([P, SSD_HEADS, 64]), ALU.mult))
                dve.sem_inc(free(job), 1)
                dve.wait_ge(decay_ready, t + 1)
                if t == 0:
                    link(tt(xdt_end, xdt, to_end[:, :].unsqueeze(2).broadcast_to([P, SSD_HEADS, 64]), ALU.mult))
                dve.sem_inc(xdt_ready, 1)
                for g in range(GROUPS):
                    heads = slice(g * GROUP_HEADS, (g + 1) * GROUP_HEADS)
                    ins = tt(decay[:, heads, :], decay[:, heads, :], cb_masked[:, g, :].unsqueeze(1).broadcast_to([P, GROUP_HEADS, P]), ALU.mult)
                ins.then_inc(decay_masked, 1)

            def take_probs(t):
                for n in range(1, 2 * (t + 1), 2):
                    job = ("T_p", t, n)
                    wait_job(dve, job)
                    copy(probs_t[t][:, n // 2, 4:8, :], bank_view(job, 4, P)).then_inc(free(job), 1)
                    dve.wait_ge(free(job), use(job))
                    dve.sem_inc(probs_t_vec, 1)

            def take_attention(t):
                dve.wait_ge(probs_ready, t + 1)
                link(nc.vector.reciprocal(row_inv[:, :], row_sum[:, t * HEADS:(t + 1) * HEADS]))
                job = ("pv", t)
                wait_job(dve, job)
                if t:
                    wait_job(dve, ("T_attn", t - 1))
                tt(attn, bank_view(job, HEADS, HEAD_DIM), row_inv[:, :].unsqueeze(2).broadcast_to([P, HEADS, HEAD_DIM]),
                   ALU.mult).then_inc(free(job), 1)
                dve.wait_ge(free(job), use(job))
                dve.sem_inc(attn_ready, 1)

            def take_ssd(t):
                if t:
                    wait_job(dve, ("T_y", t - 1))
                dve.wait_ge(z_ready, t + 1)
                wide = lambda a: a.unsqueeze(2).broadcast_to([P, SSD_HEADS, 64])
                link(tt(y_ssd, xs_nat, wide(heads_in[:, 2 * SSD_HEADS:]), ALU.mult))
                if t:
                    job = ("y_off",)
                    wait_job(dve, job)
                    link(tt(xdt_end, bank_view(job, SSD_HEADS, 64), wide(exp_cum[:, :]), ALU.mult))
                    dve.sem_inc(free(job), 1)
                    link(tt(y_ssd, y_ssd, xdt_end, ALU.add))
                job = ("y_diag", t)
                wait_job(dve, job)
                link(tt(y_ssd, bank_view(job, SSD_HEADS, 64), y_ssd, ALU.add))
                dve.sem_inc(free(job), 1)
                flat = y_ssd.rearrange("p a b -> p (a b)")
                link(tt(flat, flat, z_silu[:, t, :], ALU.mult))
                for g in range(GROUPS):
                    part = flat[:, g * 256:(g + 1) * 256]
                    ins = stt(xdt.rearrange("p a b -> p (a b)")[:, g * 256:(g + 1) * 256], part, 1.0, part, ALU.mult, ALU.mult,
                              accum_out=squares[:, g:g + 1])
                link(ins)
                ts(rms[:, :], squares[:, :], 1.0 / 256, LN_EPS, ALU.mult, ALU.add).then_inc(rms_arg_ready, 1)
                dve.wait_ge(rms_ready, t + 1)
                link(nc.vector.reciprocal(rms[:, :], rms[:, :]))
                for g in range(GROUPS):
                    part = slice(g * 256, (g + 1) * 256)
                    ins = stt(flat[:, part], flat[:, part], rms[:, g:g + 1], norm_w[:, part], ALU.mult, ALU.mult)
                ins.then_inc(y_ready, 1)

            def layer_norm(t, n, done, add_half):
                for half in range(2):
                    part = slice(half * 512, (half + 1) * 512)
                    add_half(half, part)
                    ins = nc.vector.bn_stats(stats[:, 6 * half:6 * half + 6], x_sb[:, t, part])
                link(ins)
                link(nc.vector.bn_aggr(moments[:, :], stats[:, :]))
                ts(rstd[:, :], moments[:, 1:2], LN_EPS, None, ALU.add).then_inc(var_ready, 1)
                halves = [slice(half * 512, (half + 1) * 512) for half in range(2)]
                for part in halves:
                    ins = stt(x_sb[:, t, part], x_sb[:, t, part], moments[:, 0:1], ln_gb[:, 0, part], ALU.subtract, ALU.mult)
                link(ins)
                dve.wait_ge(std_ready, n + 1)
                link(nc.vector.reciprocal(rstd[:, :], rstd[:, :]))
                for part in halves:
                    stt(x_sb[:, t, part], x_sb[:, t, part], rstd[:, :], ln_gb[:, 1, part], ALU.mult, ALU.add).then_inc(done, 1)

            def mixer_norm(t):
                def add_half(half, part):
                    job = ("out", t, half)
                    wait_job(dve, job)
                    stt(x_sb[:, t, part], x_sb[:, t, part], ALPHA, bank(job)[:, :], ALU.mult, ALU.add).then_inc(free(job), 1)
                    dve.wait_ge(free(job), use(job))

                layer_norm(t, t, h_ready, add_half)

            decay_argument(0)
            take_logits(0)
            dve.wait_ge(ln1_in, 3 * 16)
            source_side(0)
            take_probs(0)
            take_logits(1)
            take_ssd(0)
            take_attention(0)
            take_probs(1)
            decay_argument(1)
            source_side(1)
            dve.wait_ge(x_in, 16)
            mixer_norm(0)
            take_ssd(1)
            take_attention(1)

            def route(u, parity):
                link_to_search(copy(side_scores.rearrange("p a b -> p (a b)"), big[:, bass.ds(u * 2 * N_KEYS, 2 * N_KEYS)]))
                for s in range(2):
                    ins = nc.vector.max(top_v[:, s, 0:8], side_scores[:, s, :])
                link_to_search(ins)
                for s in range(2):
                    nc.vector.max_index(top_i[:, s, 0:8], top_v[:, s, 0:8], side_scores[:, s, :])
                for s in range(2):
                    ins = nc.vector.match_replace(side_rest[:, s, :], top_v[:, s, 0:8], side_scores[:, s, :], TAKEN)
                link_to_search(ins)
                for s in range(2):
                    ins = nc.vector.max(top_v[:, s, 8:16], side_rest[:, s, :])
                link_to_search(ins)
                for s in range(2):
                    nc.vector.max_index(top_i[:, s, 8:16], top_v[:, s, 8:16], side_rest[:, s, :])
                link(tt(cand, top_v[:, 0, :].unsqueeze(2).broadcast_to([P, 16, 16]),
                        top_v[:, 1, :].unsqueeze(1).broadcast_to([P, 16, 16]), ALU.add))
                flat = cand.rearrange("p a b -> p (a b)")
                copy(top_if[:, :, :], top_i[:, :, :])
                link_to_search(nc.vector.max(best[:, 0:8], flat))
                nc.vector.max_index(best_pos[:, 0:8], best[:, 0:8], flat)
                link_to_search(nc.vector.match_replace(cand_rest, best[:, 0:8], flat, TAKEN))
                link(nc.vector.max(best[:, 8:16], cand_rest))
                ts(neg_best[:, :], best[:, 0:1], -1.0, None, ALU.mult).then_inc(best_ready, 1)
                link(nc.vector.max_index(best_pos[:, 8:16], best[:, 8:16], cand_rest))
                nc.vector.tensor_single_scalar(pos_ij[:, 0, :], best_pos[:, :], 4, ALU.logical_shift_right)
                link(nc.vector.tensor_single_scalar(pos_ij[:, 1, :], best_pos[:, :], 15, ALU.bitwise_and))
                link(copy(pos_ijf[:, :, :], pos_ij[:, :, :]))
                oh = one_hot.rearrange("p s k c -> p (s k) c")
                link(tt(oh, pos_ijf[:, :, :].rearrange("p s k -> p (s k)").unsqueeze(2).broadcast_to([P, 32, 16]),
                        iota16[:, :].unsqueeze(1).broadcast_to([P, 32, 16]), ALU.is_equal))
                link(tt(one_hot, one_hot, top_if[:, :, :].unsqueeze(2).broadcast_to([P, 2, 16, 16]), ALU.mult))
                link(nc.vector.tensor_reduce(picked[:, :, :].rearrange("p s k -> p (s k)"), oh, AX.X, ALU.add))
                stt(expert[:, parity, :], picked[:, 0, :], float(N_KEYS), picked[:, 1, :], ALU.mult, ALU.add).then_inc(experts_ready, 1)

            def finish_gate(u, parity):
                dve.wait_ge(gate_exp_ready, u + 1)
                link(nc.vector.reciprocal(gate_sum[:, :], gate_sum[:, :]))
                ts(gate[:, parity, :], gate_e[:, :], gate_sum[:, :], None, ALU.mult).then_inc(gate_ready, 1)

            def take_sum(u, tile, parity):
                dve.wait_ge(slot_used, (u + 1) * SLOTS)
                for half in range(2):
                    where = mix[:, bass.ds(tile * D_MODEL + half * 512, 512)]
                    ins = tt(where, banks[2 * parity + half][:, :], where, ALU.add)
                ins.then_inc(sum_taken, 1)

            def add_experts(t):
                link(stt(x_sb[:, t, :], x_sb[:, t, :], ALPHA, ffn[:, t, :], ALU.mult, ALU.add))

            def dot_slots(u, tile, parity, group):
                for j in group:
                    slot = slots_of(u)[j]
                    dve.wait_ge(rows_in[slot], 16 * fills(u, j))
                    rows = arena[:, slot * SLOT:slot * SLOT + D_MODEL]
                    ins = stt(rows, x_rows[:, bass.ds(tile * D_MODEL, D_MODEL)], 1.0, rows,
                              ALU.mult, ALU.mult, accum_out=dots[:, parity, j:j + 1])
                ins.then_inc(dots_ready, 1)

            def dot_unit(u, tile, parity, former_tile, last=False):
                if not last:
                    route(u + 1, 1 - parity)
                for g, group in enumerate(slot_groups(last)):
                    dot_slots(u, tile, parity, group)
                    if g == 0:
                        take_sum(u - 1, former_tile, 1 - parity)
                        if not last:
                            finish_gate(u + 1, 1 - parity)

            x_rows = x_sb[:, :, :].rearrange("p a b -> p (a b)")
            dve.wait_ge(scores_ready, 1)
            route(0, 0)
            finish_gate(0, 0)
            mixer_norm(1)
            dve.wait_ge(h_ready, 2 * TILES)
            dve.sem_inc(ln1_done, 1)
            nc.vector.memset(ffn[:, 0, :], 0.0).then_inc(sum_taken, 1)
            dve.wait_ge(sum_taken, 1)
            groups = slot_groups(False)
            dot_slots(0, 0, 0, groups[0])
            dve.wait_ge(scores_ready, 2)
            route(1, 1)
            dot_slots(0, 0, 0, groups[1])
            finish_gate(1, 1)
            dot_slots(0, 0, 0, groups[2])
            dot_slots(0, 0, 0, groups[3])
            dve.wait_ge(scores_ready, score_order.index((0, 1)) + 2)
            for u in range(1, EARLY_UNITS):
                before = count[0]
                dot_unit(u, 0, u % 2, 0)
                per_unit = count[0] - before
            dve.wait_ge(scores_ready, len(score_order) + 1)
            link(nc.vector.memset(ffn[:, 1, :], 0.0))
            with dve.Fori(0, LOOP_TURNS) as i:
                for n in (EARLY_UNITS, EARLY_UNITS + 1):
                    u = 2 * i + n
                    count[1] = i * 2 * per_unit
                    dot_unit(u, u // PEER_HEADS, n % 2, (u - 1) // PEER_HEADS)
            count[1] = (LOOP_TURNS - 1) * 2 * per_unit
            dve.wait_ge(ln2_in, 32)
            add_experts(0)
            layer_norm(0, TILES, result_ready, lambda half, part: None)
            dot_unit(UNITS - 1, TILES - 1, 1, TILES - 1, last=True)
            dve.wait_ge(sum_taken, UNITS)
            add_experts(TILES - 1)

            def add_last_sum(half, part):
                dve.wait_ge(*((slot_used, UNITS * SLOTS) if half else (half_summed, 1)))
                link(tt(x_sb[:, TILES - 1, part], banks[2 + half][:, :], x_sb[:, TILES - 1, part], ALU.add))

            layer_norm(TILES - 1, 2 * TILES - 1, result_ready, add_last_sum)


def kernel(**inputs):
    import concourse.bacc as bacc
    from concourse.bass_utils import run_bass_kernel_spmd

    row = lambda name: np.ascontiguousarray(np.asarray(inputs[name])[0])
    freqs = lambda d: (np.float32(ROPE_THETA) ** (-np.arange(0, d, 2, dtype=np.float32) / np.float32(d))).astype(np.float32)
    x, w_in = row("x"), row("w_in")
    arrays = {"x": x, "x_columns": np.ascontiguousarray(x.T), "positions": row("positions")}
    arrays["inv_freq"] = np.concatenate([freqs(HEAD_DIM), freqs(IDX_DIM)])
    arrays["w_idx"] = np.concatenate([w_in[:, I0:Z0], w_in[:, DT0:]], axis=1)
    for name in ("w_in", "conv_w", "conv_b", "dt_bias", "a_log", "d_skip", "ssm_norm_w", "w_out",
                 "ln1_g", "ln1_b", "peer_wq", "peer_k1", "peer_k2"):
        arrays[name] = row(name)
    arrays["expert_uv"] = np.concatenate([row("peer_u"), row("peer_v")], axis=1)
    arrays["ln2_g"], arrays["ln2_b"] = row("ln2_g"), row("ln2_b")

    nc = bacc.Bacc("TRN2", target_bir_lowering=False, num_devices=1)
    args = [nc.dram_tensor(f"in_{n}", a.shape, mybir.dt.from_np(a.dtype), kind="ExternalInput").ap() for n, a in arrays.items()]
    out = nc.dram_tensor("out", (SEQ, D_MODEL), mybir.dt.float32, kind="ExternalOutput").ap()
    build_layer(nc, *args, out)
    got = run_bass_kernel_spmd(nc, [{f"in_{n}": a for n, a in arrays.items()}], core_ids=[0])
    return got.results[0]["out"].reshape(1, SEQ, D_MODEL)
```
